# Optimizing a Trainium2 kernel written in Bass

```python
import math
import jax
import jax.numpy as jnp
from jax import lax
import numpy as np

D_MODEL = 1024
BATCH = 1
SEQ = 128
DEPTH = 2
DEC_BATCH = 1
DEC_SEQ = 512
PAST_LEN = 128

GRID_W = 64
D_A = D_MODEL
FOURIER_GROUPS = 4
FOURIER_GROUP_DIM = D_A // FOURIER_GROUPS
D_B = D_MODEL
CONV_K = 3
FC_IN = 2 * D_A + 4 * D_B
SSD_EXPAND = 2
SSD_D_INNER = SSD_EXPAND * D_MODEL
SSD_HEAD_DIM = 64
SSD_HEADS = SSD_D_INNER // SSD_HEAD_DIM
SSD_GROUPS = 8
SSD_D_STATE = 128
SSD_CONV_DIM = SSD_D_INNER + 2 * SSD_GROUPS * SSD_D_STATE
SSD_IN = SSD_D_INNER + SSD_CONV_DIM + 2 * SSD_HEADS
CHUNK = 128
EPS = 1e-6

kernel_name = "hybrid_fourier_shortconv_ssd_diffusion_step"

def rmsnorm(x, g):
    xf = x.astype(jnp.float32)
    y = xf * lax.rsqrt(jnp.mean(xf * xf, axis=-1, keepdims=True) + EPS)
    return (y * g.astype(jnp.float32)).astype(x.dtype)

def dwconv3(u, w, rows, row_len):
    bsz, L, C = u.shape
    ug = u.reshape(bsz, rows, row_len, C)
    up = jnp.pad(ug, ((0, 0), (0, 0), (1, 1), (0, 0)))
    y = up[:, :, :-2] * w[0] + up[:, :, 1:-1] * w[1] + up[:, :, 2:] * w[2]
    return y.reshape(bsz, L, C)

def fc_mixer(h, w_in, conv_w, w_out, rows, row_len):
    bsz, L, _ = h.shape
    proj = h @ w_in
    u_a, z_a, b_b, c_b, v_b, z_b = jnp.split(proj, 6, axis=-1)
    ua = u_a.astype(jnp.float32).reshape(bsz, L, FOURIER_GROUPS, FOURIER_GROUP_DIM)
    y_a = jnp.fft.fftn(ua, axes=(1, 3), norm="ortho").real.reshape(bsz, L, D_A).astype(h.dtype)
    y_a = y_a * jax.nn.silu(z_a)
    y_b = b_b * dwconv3(c_b * v_b, conv_w, rows, row_len)
    y_b = y_b * jax.nn.silu(z_b)
    return jnp.concatenate([y_a, y_b], axis=-1) @ w_out

def ssd_scan(x, dt, a, b_in, c_in, h0):
    bsz, L, H, P = x.shape
    G, N = b_in.shape[2], b_in.shape[3]
    R = H // G
    nc = L // CHUNK
    xd = (x * dt[..., None]).reshape(bsz, nc, CHUNK, G, R, P)
    la_cum = jnp.cumsum((dt * a).reshape(bsz, nc, CHUNK, G, R), axis=2)
    bc = b_in.reshape(bsz, nc, CHUNK, G, N)
    cc = c_in.reshape(bsz, nc, CHUNK, G, N)
    causal = jnp.tril(jnp.ones((CHUNK, CHUNK), dtype=bool))[None, None, :, :, None, None]
    seg = la_cum[:, :, :, None] - la_cum[:, :, None, :]
    decay = jnp.exp(jnp.where(causal, seg, -jnp.inf))
    cb = jnp.einsum('bclgn,bcsgn->bclsg', cc, bc)
    y_diag = jnp.einsum('bclsgr,bcsgrp->bclgrp', decay * cb[..., None], xd)
    decay_to_end = jnp.exp(la_cum[:, :, -1:] - la_cum)
    st = jnp.einsum('bclgn,bclgr,bclgrp->bcgrpn', bc, decay_to_end, xd)
    chunk_decay = jnp.exp(la_cum[:, :, -1])

    def step(hc, inp):
        st_c, dec_c = inp
        return hc * dec_c[..., None, None] + st_c, hc

    h_final, h_in = lax.scan(step, h0.reshape(bsz, G, R, P, N),
                             (jnp.swapaxes(st, 0, 1), jnp.swapaxes(chunk_decay, 0, 1)))
    h_in = jnp.swapaxes(h_in, 0, 1)
    y_off = jnp.einsum('bclgn,bcgrpn,bclgr->bclgrp', cc, h_in, jnp.exp(la_cum))
    y = (y_diag + y_off).reshape(bsz, L, H, P)
    return y, h_final.reshape(bsz, H, P, N)

def ssd_mixer(h, w_in, conv_w, conv_b, dt_bias, a_log, d_skip, norm_g, w_out, h0_f, h0_b):
    bsz, L, _ = h.shape
    proj = h @ w_in
    z = proj[..., :SSD_D_INNER]
    xbc = proj[..., SSD_D_INNER:SSD_D_INNER + SSD_CONV_DIM]
    dt_raw = proj[..., SSD_D_INNER + SSD_CONV_DIM:]
    xbc = jax.nn.silu(dwconv3(xbc, conv_w, 1, L) + conv_b).astype(jnp.float32)
    xs = xbc[..., :SSD_D_INNER].reshape(bsz, L, SSD_HEADS, SSD_HEAD_DIM)
    bs = xbc[..., SSD_D_INNER:SSD_D_INNER + SSD_GROUPS * SSD_D_STATE].reshape(bsz, L, SSD_GROUPS, SSD_D_STATE)
    cs = xbc[..., SSD_D_INNER + SSD_GROUPS * SSD_D_STATE:].reshape(bsz, L, SSD_GROUPS, SSD_D_STATE)
    dt = jax.nn.softplus(dt_raw.astype(jnp.float32).reshape(bsz, L, 2, SSD_HEADS)
                         + dt_bias.astype(jnp.float32))
    a = -jnp.exp(a_log.astype(jnp.float32))
    y_f, hf = ssd_scan(xs, dt[:, :, 0], a[0], bs, cs, h0_f.astype(jnp.float32))
    flip = lambda t: jnp.flip(t, axis=1)
    y_b, hb = ssd_scan(flip(xs), flip(dt[:, :, 1]), a[1], flip(bs), flip(cs), h0_b.astype(jnp.float32))
    y = y_f + flip(y_b) + d_skip.astype(jnp.float32)[:, None] * xs
    y = y.reshape(bsz, L, SSD_D_INNER) * jax.nn.silu(z.astype(jnp.float32))
    yg = y.reshape(bsz, L, SSD_GROUPS, SSD_D_INNER // SSD_GROUPS)
    yg = yg * lax.rsqrt(jnp.mean(yg * yg, axis=-1, keepdims=True) + EPS)
    y = yg.reshape(bsz, L, SSD_D_INNER) * norm_g.astype(jnp.float32)
    return y.astype(h.dtype) @ w_out, hf.astype(h.dtype), hb.astype(h.dtype)

def trunk(x, cond, rows, row_len, h0, w_mod, b_mod, norm_g, fc_w_in, fc_conv_w, fc_w_out,
          ssd_w_in, ssd_conv_w, ssd_conv_b, ssd_dt_bias, ssd_a_log, ssd_d, ssd_norm_g,
          ssd_w_out, final_norm_g):
    cond_act = jax.nn.silu(cond)
    states = []
    for layer in range(DEPTH):
        shift, scale, gate = jnp.split(cond_act @ w_mod[layer] + b_mod[layer], 3, axis=-1)
        hm = rmsnorm(x, norm_g[layer]) * (1 + scale[:, None]) + shift[:, None]
        i = layer // 2
        if layer % 2 == 0:
            out = fc_mixer(hm, fc_w_in[i], fc_conv_w[i], fc_w_out[i], rows, row_len)
        else:
            out, hf, hb = ssd_mixer(hm, ssd_w_in[i], ssd_conv_w[i], ssd_conv_b[i], ssd_dt_bias[i],
                                    ssd_a_log[i], ssd_d[i], ssd_norm_g[i], ssd_w_out[i],
                                    h0[:, i, 0], h0[:, i, 1])
            states.append(jnp.stack([hf, hb], axis=1))
        x = x + gate[:, None] * out
    return rmsnorm(x, final_norm_g), jnp.stack(states, axis=1)

def setup_inputs(seed: int = 0) -> dict:
    key = jax.random.key(seed)
    ks = jax.random.split(key, 24)
    nrm = lambda k, shape, s: jax.random.normal(k, shape, jnp.float32) * s
    ne = (DEPTH + 1) // 2
    no = DEPTH // 2
    dt0 = jnp.exp(jax.random.uniform(ks[14], (no, 2, SSD_HEADS), jnp.float32,
                                     minval=math.log(1e-3), maxval=math.log(1e-1)))
    return {
        "x_prompt": nrm(ks[0], (BATCH, SEQ, D_MODEL), 1.0),
        "x_sample": nrm(ks[1], (DEC_BATCH, DEC_SEQ, D_MODEL), 1.0),
        "state_ssm": nrm(ks[2], (DEC_BATCH, no, 2, SSD_HEADS, SSD_HEAD_DIM, SSD_D_STATE), 0.3),
        "c": nrm(ks[3], (DEC_BATCH, D_MODEL), 1.0),
        "c_ctx": nrm(ks[4], (D_MODEL,), 1.0),
        "w_mod": nrm(ks[5], (DEPTH, D_MODEL, 3 * D_MODEL), D_MODEL ** -0.5),
        "b_mod": nrm(ks[6], (DEPTH, 3 * D_MODEL), 0.02),
        "norm_g": 1.0 + nrm(ks[7], (DEPTH, D_MODEL), 0.02),
        "fc_w_in": nrm(ks[8], (ne, D_MODEL, FC_IN), D_MODEL ** -0.5),
        "fc_conv_w": nrm(ks[9], (ne, CONV_K, D_B), CONV_K ** -0.5),
        "fc_w_out": nrm(ks[10], (ne, D_A + D_B, D_MODEL), (D_A + D_B) ** -0.5),
        "ssd_w_in": nrm(ks[11], (no, D_MODEL, SSD_IN), D_MODEL ** -0.5),
        "ssd_conv_w": nrm(ks[12], (no, CONV_K, SSD_CONV_DIM), CONV_K ** -0.5),
        "ssd_conv_b": nrm(ks[13], (no, SSD_CONV_DIM), 0.02),
        "ssd_dt_bias": dt0 + jnp.log(-jnp.expm1(-dt0)),
        "ssd_a_log": jnp.log(jax.random.uniform(ks[15], (no, 2, SSD_HEADS), jnp.float32, minval=1.0, maxval=16.0)),
        "ssd_d": 1.0 + nrm(ks[16], (no, SSD_HEADS), 0.1),
        "ssd_norm_g": 1.0 + nrm(ks[17], (no, SSD_D_INNER), 0.02),
        "ssd_w_out": nrm(ks[18], (no, SSD_D_INNER, D_MODEL), SSD_D_INNER ** -0.5),
        "final_norm_g": 1.0 + nrm(ks[19], (D_MODEL,), 0.02),
    }

def reference(x_prompt, x_sample, state_ssm, c, c_ctx, w_mod, b_mod, norm_g, fc_w_in, fc_conv_w,
              fc_w_out, ssd_w_in, ssd_conv_w, ssd_conv_b, ssd_dt_bias, ssd_a_log, ssd_d,
              ssd_norm_g, ssd_w_out, final_norm_g):
    params = (w_mod, b_mod, norm_g, fc_w_in, fc_conv_w, fc_w_out, ssd_w_in, ssd_conv_w,
              ssd_conv_b, ssd_dt_bias, ssd_a_log, ssd_d, ssd_norm_g, ssd_w_out, final_norm_g)
    h0_ctx = jnp.zeros((x_prompt.shape[0],) + state_ssm.shape[1:], x_prompt.dtype)
    y_prompt, new_state_ssm = trunk(x_prompt, c_ctx[None, :], 1, x_prompt.shape[1], h0_ctx, *params)
    rows = x_sample.shape[1] // GRID_W
    y_sample, _ = trunk(x_sample, c, rows, GRID_W, state_ssm, *params)
    return (y_prompt, y_sample, new_state_ssm)


_drawn_inputs = setup_inputs


def setup_inputs(seed=0):
    import zlib

    import numpy as np

    out = dict(_drawn_inputs(seed))
    spreads = {}
    factors = {'ssd_d': 4.353, 'ssd_norm_g': 6.856, 'final_norm_g': 2.801}
    for name, (base, spread) in spreads.items():
        noise = np.random.default_rng([zlib.crc32(name.encode()), seed]).standard_normal(out[name].shape)
        drawn = base * np.exp(spread * noise) if base else spread * noise
        out[name] = jnp.asarray(drawn.astype(out[name].dtype))
    for name, factor in factors.items():
        out[name] = (out[name] * factor).astype(out[name].dtype)
    return out
```

```python
from contextlib import ExitStack

import concourse.bass as bass
from concourse import mybir

F32 = mybir.dt.float32
F32R = mybir.dt.float32r
ALU = mybir.AluOpType
ACT = mybir.ActivationFunctionType

P = 128
D = 1024
KT = D // P
LAT, CTX = 512, 128
TOK = LAT + CTX
NT = TOK // P
SEGS = ((0, LAT), (LAT, TOK))
FC_IN = 6 * D
UNIT = 1024
RING = 4
EPS = 1e-6
N_IN0 = 48
N_OUT = 16
OUT0 = N_IN0
IN1 = OUT0 + N_OUT
G = 8
UPG = 6
OUT1 = IN1 + G * UPG
UNITS = OUT1 + N_OUT
HEADS = 32
DI = 2048
SSD_IN = 6208


class Chain:

    def __init__(self, eng, sem, base=0):
        self.eng, self.sem, self.base, self.n = eng, sem, base, 0

    def tick(self, ins):
        self.n += 1
        ins.then_inc(self.sem, 1)

    def sync(self):
        self.eng.wait_ge(self.sem, self.base + self.n)


def fc_unit_src(fc_w_in, col):
    return fc_w_in[0].rearrange("(k p) n -> p k n", p=P)[:, :, bass.ds(col, P)]


def build_step(nc, A, outs, stage=2):
    y_prompt, y_sample, new_state = outs
    mod_scr = nc.dram_tensor("mod_scr", (4, 2, D), F32, kind="Internal").ap()
    x1_scr = nc.dram_tensor("x1_scr", (P, NT * D), F32, kind="Internal").ap()

    l_scr = nc.dram_tensor("l_scr", (64, TOK), F32, kind="Internal").ap()
    y_scr = nc.dram_tensor("y_scr", (P, 16, TOK), F32, kind="Internal").ap()

    ssd_src = A["ssd_w_in"][0].rearrange("(k p) n -> p k n", p=P)
    fc_src = A["fc_w_in"][0].rearrange("(k p) n -> p k n", p=P)
    wm_src = [A["w_mod"][l].rearrange("(p t) n -> p t n", t=KT) for l in range(2)]
    wout_src = [A[n][0].rearrange("(k p) n -> p k n", p=P) for n in ("fc_w_out", "ssd_w_out")]

    ctx = ExitStack()
    with ctx:
        def sb(name, shape, dt=F32):
            return ctx.enter_context(nc.sbuf_tensor(name, shape, dt))

        def sem(name):
            return ctx.enter_context(nc.semaphore(name))

        PS = ctx.enter_context(nc.psum_tensor("PS", [P, 8, 512], F32))
        PSf = PS[:, :, :].rearrange("p b n -> p (b n)")
        raw_w = sb("raw_w", [P, RING, UNIT])
        w_hi = sb("w_hi", [P, RING, UNIT], F32R)
        w_lo = sb("w_lo", [P, RING, UNIT], F32R)
        h_hi = sb("h_hi", [P, KT, TOK], F32R)
        h_lo = sb("h_lo", [P, KT, TOK], F32R)
        y_hi = sb("y_hi", [P, 2, TOK], F32R)
        y_lo = sb("y_lo", [P, 2, TOK], F32R)
        cst = sb("cst", [P, 3 * P])
        ident, upper, lower = cst[:, 0:P], cst[:, P:2 * P], cst[:, 2 * P:3 * P]
        ones = sb("ones", [P, P])
        cond = sb("cond", [P, 2, KT])
        par1 = sb("par1", [P, P])
        par2 = sb("par2", [P, 72])
        ss_mod = sb("ss_mod", [P, 2, 2, KT])
        ssq = sb("ssq", [P, 16])
        rstd = sb("rstd", [P, 16])
        half_neg = sb("half_neg", [P, 1])
        eps_col = sb("eps_col", [P, 1])
        NBIG = 26700 - 200
        big = sb("big", [P, NBIG])

        def carve(off, *dims):
            n = 1
            for d in dims:
                n *= d
            assert off + n <= NBIG, (off, dims)
            v = big[:, off:off + n]
            if len(dims) == 2:
                return v.rearrange("p (a b) -> p a b", a=dims[0])
            if len(dims) == 3:
                return v.rearrange("p (a b c) -> p a b c", a=dims[0], b=dims[1])
            if len(dims) == 4:
                return v.rearrange("p (a b c d) -> p a b c d", a=dims[0], b=dims[1], c=dims[2])
            return v

        x = carve(0, NT, D)
        yT = carve(5120, 16, TOK)
        mod_w = carve(15360, 2, D)
        acc = carve(17408, 2, D)
        gate = carve(19456, 2, D)
        wm_ring = carve(5120, 4, 2, 1024)
        xn = carve(5120 + 8192, 2, D)
        xT0 = carve(15360, KT, TOK)
        mod_sb = carve(21504, 2 * D)
        praw = carve(21504 + 2048, 2, P)
        praw3 = carve(23808, P)
        dft_g = carve(21504, 2, 512)
        dft_l = carve(22528, 10, P)
        sz_a = carve(23808, 2, TOK)
        ut = carve(5120 + 8 * TOK, 2, TOK)
        ub = carve(5120 + 8 * TOK + 1280, 2, 512)
        ab = carve(5120 + 8 * TOK + 2304, 5, 512)
        d02_sb = carve(0, 512)
        e01 = carve(512, 2, 256)
        cv_c = carve(0, 2, TOK)
        cv = carve(1280, 2, TOK)
        cc = carve(2560, 2, TOK)
        sz_b = carve(3840, 2, TOK)
        mod_row = carve(21504, 2 * D)[0:1]
        bias_row = carve(23808, D)[0:1]
        xn1 = carve(5120, 2, D)
        xT1 = carve(5120 + 2048, KT, TOK)
        gtmp = carve(25100, 2, 512)

        fin_g = carve(17408, D)
        sq_junk = carve(15360, 2, D)
        dtw_raw = carve(24000, KT, 64)

        at = [0]

        def take(*dims):
            n = 1
            for d in dims:
                n *= d
            v = carve(at[0], *dims)
            at[0] += n
            return v

        cvx = take(3, TOK)
        cvC = take(2, TOK)
        th = take(TOK)
        zth = take(2, 256)
        xb = take(NT, 384)
        sz = take(NT, 256)
        lfb = take(2, 8, P)
        cbm = take(2, NT, P)
        ea = take(2, 4, P)
        gm = take(2, 2, 4, P)
        xdt = take(2, 512)
        xws = take(4, 512)
        hs = take(4, 512)
        hd = take(512)
        h0r = take(4, P)
        nst = take(512)
        yo = take(512)
        uu = take(2, 256)
        aa = take(2, 256)
        yn = take(2, 256)
        ysb = take(2, 2, P)
        GTW = 206
        GT = take(G, GTW)
        CPG = take(G, 16)
        gt = take(2, GTW)
        cp = take(2, 16)
        ssy = take(2)
        ry = take(2)
        tX, tNX, tNA, tU, tW, tLW, tC, tDT, tDA, tL = (carve(12400 + 320 * k, NT, 64) for k in range(10))
        tT = carve(12400 + 3200, NT, 64)
        lrow = carve(12400 + 3520, TOK)
        b_in, a_in, b_pm, a_pm = (carve(12400 + 4160 + 64 * k, 64) for k in range(4))
        d_in = carve(12400 + 4416, HEADS)

        landed = [sem(f"landed{i}") for i in range(RING)]
        hi_ready, lo_ready, unit_used = sem("hi_ready"), sem("lo_ready"), sem("unit_used")
        act_freed, dve_freed = sem("act_freed"), sem("dve_freed")
        cond_landed, x_landed, par_landed = sem("cond_landed"), sem("x_landed"), sem("par_landed")
        wm_landed = [sem(f"wm_landed{i}") for i in range(4)]
        wm_used, mod_mm, mod_copied, mod_T, mod_ready = sem("wm_used"), sem("mod_mm"), sem("mod_copied"), sem("mod_T"), sem("mod_ready")
        cond_ready, ones_ready, par_T, par_ready = sem("cond_ready"), sem("ones_ready"), sem("par_T"), sem("par_ready")
        sq_done, ms_done, rstd_done, xn_done = sem("sq_done"), sem("ms_done"), sem("rstd_done"), sem("xn_done")
        xt_ready, xt_done, v_done, hh_done, h_ready = sem("xt_ready"), sem("xt_done"), sem("v_done"), sem("hh_done"), sem("h_ready")
        fdone, ub_ready, gd_ready, q_ready, ab_act, ab_dve = sem("fdone"), sem("ub_ready"), sem("gd_ready"), sem("q_ready"), sem("ab_act"), sem("ab_dve")
        ld_ready, ya_done, dft_landed = sem("ld_ready"), sem("ya_done"), sem("dft_landed")
        conv_step, yb_done = sem("conv_step"), sem("yb_done")
        modw_landed, modw_used, acc_step, red_ready, row_copied, row_stored, bias_landed = (
            sem("modw_landed"), sem("modw_used"), sem("acc_step"), sem("red_ready"), sem("row_copied"), sem("row_stored"), sem("bias_landed"))
        x_back, gate_landed = sem("x_back"), sem("gate_landed")
        yh_done, yl_done, y_even_used = sem("yh_done"), sem("yl_done"), sem("y_even_used")
        out_ready, out_evac, x_updated = sem("out_ready"), sem("out_evac"), sem("x_updated")
        p3_landed, stored = sem("p3_landed"), sem("stored")
        mod_step = sem("mod_step")
        exponent_ready = sem("exponent_ready")
        (dtw_landed, tot_copied, bc_landed, dtw_hi, dtw_lo, dtp_ready, cum_ready, lt_ready, tab_dve, tab_act, tables_ready) = (sem(n) for n in (
            "dtw_landed", "tot_copied", "bc_landed", "dtw_hi", "dtw_lo", "dtp_ready", "cum_ready", "lt_ready", "tab_dve", "tab_act", "tables_ready"))
        (proj_free, z_ready, zth_done, cen_done, tap_step, th_done, conv_done, grp_done) = (sem(n) for n in (
            "proj_free", "z_ready", "zth_done", "cen_done", "tap_step", "th_done", "conv_done", "grp_done"))
        (tr_ready, tok_done, h0_landed, h_T, hs0_done, cb_ready, cbm_done, xw_done, st_ready, st_done, hd_done) = (sem(n) for n in (
            "tr_ready", "tok_done", "h0_landed", "h_T", "hs0_done", "cb_ready", "cbm_done", "xw_done", "st_ready", "st_done", "hd_done"))
        (sc_ready, sc_done, small_stored, m_done, exp_done, g_done, y_ready, t_done, pool_step, u_done, a_step, gz_done) = (sem(n) for n in (
            "sc_ready", "sc_done", "small_stored", "m_done", "exp_done", "g_done", "y_ready", "t_done", "pool_step", "u_done", "a_step", "gz_done"))
        (sqy_done, msy_done, ry_done, yn_done, ytr_ready, yt_done, fg_landed, fin_done) = (sem(n) for n in (
            "sqy_done", "msy_done", "ry_done", "yn_done", "ytr_ready", "yt_done", "fg_landed", "fin_done"))
        y_stored = [sem(f"y_stored{i}") for i in range(2)]
        lfb_landed = [sem(f"lfb_landed{i}") for i in range(2)]

        LAST_UNIT = IN1 if stage == 0 else UNITS
        block = ctx.enter_context(nc.Block())

        def split_hi(act, u, slot):
            act.wait_ge(landed[slot], 16 * (u // RING + 1) if isinstance(u, int) else u[1])
            un = u if isinstance(u, int) else u[0]
            if not isinstance(u, int) or u >= RING:
                act.wait_ge(unit_used, un - (RING - 1))
            act.activation(w_hi[:, slot, :], raw_w[:, slot, :], ACT.Copy).then_inc(hi_ready, 1)

        def split_lo(dve, u, slot):
            un = u if isinstance(u, int) else u[0]
            dve.wait_ge(hi_ready, un + 1)
            dve.tensor_tensor(w_lo[:, slot, :], raw_w[:, slot, :], w_hi[:, slot, :].bitcast(F32),
                              ALU.subtract).then_inc(lo_ready, 1)

        def unit(base, it, per, k):
            assert (base + k) % 1 == 0 and per % RING == 0
            if isinstance(it, int):
                return base + per * it + k
            return (per * it + (base + k), 4 * per * it + 16 * ((base + k) // RING + 1))

        def channel_tile(pe, slot, pair, h_base=None):
            for kt in range(KT):
                if h_base is not None:
                    pe.wait_ge(h_ready, h_base + kt + 1)
                ws = slice(kt * P, (kt + 1) * P)
                for n, (w, h) in enumerate(((w_hi, h_hi), (w_hi, h_lo), (w_lo, h_hi))):
                    for s, (a, b) in enumerate(SEGS):
                        mm = pe.matmul(PS[:, 2 * pair + s, 0:b - a], w[:, slot, ws], h[:, kt, a:b],
                                       start=(kt == 0 and n == 0), stop=(kt == KT - 1 and n == 2))
            mm.then_inc(unit_used, 1)

        def norm_act(act, layer, xnb, xTb):
            for t in range(NT + 1):
                if t < NT:
                    n = NT * layer + t
                    if layer == 0:
                        act.wait_ge(x_landed, 32)
                    else:
                        act.wait_ge(x_updated, NT * 2 * (layer - 1) + NT + t + 1)
                    if t >= 2:
                        act.wait_ge(xt_ready, n - 1)
                    act.activation(xnb[:, t % 2, :], x[:, t, :], ACT.Square,
                                   accum_out=ssq[:, n:n + 1]).then_inc(sq_done, 1)
                if t >= 1:
                    m = NT * layer + t - 1
                    act.wait_ge(xt_ready, m + 1)
                    b = 4 + 2 * ((t - 1) % 2)
                    act.activation(xTb[:, :, (t - 1) * P:t * P],
                                   PS[:, b:b + 2, :].rearrange("p b (k n) -> p (b k) n", n=P),
                                   ACT.Copy).then_inc(xt_done, 1)

        def norm_pool(pool, layer):
            for t in range(NT):
                n = NT * layer + t
                pool.wait_ge(sq_done, n + 1)
                pool.tensor_scalar(rstd[:, n:n + 1], ssq[:, n:n + 1], 1.0 / D, EPS, ALU.mult, ALU.add).then_inc(ms_done, 1)
                pool.wait_ge(ms_done, n + 1)
                pool.tensor_tensor(rstd[:, n:n + 1], rstd[:, n:n + 1], half_neg[:, :], ALU.pow).then_inc(rstd_done, 1)

        def norm_dve(dve, layer, xnb):
            for t in range(NT):
                norm_dve_tile(dve, layer, xnb, t)

        def norm_dve_tile(dve, layer, xnb, t):
                n = NT * layer + t
                dve.wait_ge(rstd_done, n + 1)
                if t >= 2:
                    dve.wait_ge(xt_ready, n - 1)
                dve.tensor_scalar(xnb[:, t % 2, :], x[:, t, :], rstd[:, n:n + 1], None, ALU.mult).then_inc(xn_done, 1)

        def norm_pe(pe, layer, xnb):
            for t in range(NT):
                n = NT * layer + t
                pe.wait_ge(xn_done, n + 1)
                if t >= 2:
                    pe.wait_ge(xt_done, n - 1)
                if t == 1 and layer == 1:
                    pe.wait_ge(out_evac, 8)
                if t == 1 and layer == 0:
                    pe.wait_ge(par_ready, 2)
                b = 4 + 2 * (t % 2)
                for k in range(KT):
                    mm = pe.transpose(PS[:, b + k // 4, (k % 4) * P:(k % 4 + 1) * P], xnb[:, t % 2, k * P:(k + 1) * P], ident)
                mm.then_inc(xt_ready, 1)

        def h_dve(dve, layer, xTb):
            dve.wait_ge(xt_done, NT * (layer + 1))
            dve.wait_ge(mod_ready, 2 * (layer + 1))
            for k in range(KT + 1):
                if k < KT:
                    for c, (a, b) in enumerate(SEGS):
                        dve.tensor_scalar(xTb[:, k, a:b], xTb[:, k, a:b], ss_mod[:, 1, c, k:k + 1], ss_mod[:, 0, c, k:k + 1],
                                          ALU.mult, ALU.add).then_inc(v_done, 1)
                if k >= 1:
                    dve.wait_ge(hh_done, KT * layer + k)
                    dve.tensor_tensor(h_lo[:, k - 1, :], xTb[:, k - 1, :], h_hi[:, k - 1, :].bitcast(F32),
                                      ALU.subtract).then_inc(h_ready, 1)

        def h_act(act, layer, xTb):
            for k in range(KT):
                act.wait_ge(v_done, 2 * (KT * layer + k + 1))
                act.activation(h_hi[:, k, :], xTb[:, k, :], ACT.Copy).then_inc(hh_done, 1)

        def y_ready_wait(eng, layer, kt):
            if layer == 0:
                if kt < 8:
                    eng.wait_ge(ya_done, kt + 1)
                else:
                    eng.wait_ge(yb_done, kt - 7)
            else:
                eng.wait_ge(y_back[kt // 4], 16)

        def out_ring_wait(eng, layer, q):
            if q >= 2 or layer == 1:
                r = q - 2
                u0 = (OUT0, OUT1)[layer]
                if r < 0:
                    return
                if r % 2 == 0:
                    eng.wait_ge(y_even_used, 16 * layer + r // 2 + 1)
                else:
                    eng.wait_ge(unit_used, u0 + r // 2 + 1)

        def out_act(act, layer):
            u0 = (OUT0, OUT1)[layer]
            for q in range(32):
                if q < 16:
                    y_ready_wait(act, layer, q)
                out_ring_wait(act, layer, q)
                act.activation(y_hi[:, q % 2, :], yT[:, q % 16, :], ACT.Copy).then_inc(yh_done, 1)
                if q % 2 == 0 and q:
                    out_next_unit(act, split_hi, u0 + q // 2 - 1)
            out_next_unit(act, split_hi, u0 + 15)

        def out_next_unit(eng, split, u):
            if u + RING < LAST_UNIT:
                split(eng, u + RING, u % RING)

        def residual(dve, layer, hh, t):
            u0 = (OUT0, OUT1)[layer]
            if hh == 0 and t == 0:
                dve.wait_ge(x_back, 32 * (layer + 1))
                dve.wait_ge(gate_landed, 32 * (layer + 1))
            if t < NT - 1:
                dve.wait_ge(out_ready, 8 * layer + 4 * hh + t + 1)
            else:
                dve.wait_ge(unit_used, u0 + 8 * (hh + 1))
            n = 10 * layer + 5 * hh + t
            if n >= 2:
                dve.wait_ge(x_updated, n - 1)
            dve.tensor_tensor(gtmp[:, t % 2, :], PS[:, (5 * hh + t) % 8, :], gate[:, int(t == NT - 1), 512 * hh:512 * hh + 512],
                              ALU.mult).then_inc(out_evac, 1)
            dve.wait_ge(out_evac, 10 * layer + 5 * hh + t + 1)
            xs = x[:, t, 512 * hh:512 * hh + 512]
            dve.tensor_tensor(xs, xs, gtmp[:, t % 2, :], ALU.add).then_inc(x_updated, 1)

        def out_dve(dve, layer):
            u0 = (OUT0, OUT1)[layer]
            for q in range(32):
                dve.wait_ge(yh_done, 32 * layer + q + 1)
                dve.tensor_tensor(y_lo[:, q % 2, :], yT[:, q % 16, :], y_hi[:, q % 2, :].bitcast(F32),
                                  ALU.subtract).then_inc(yl_done, 1)
                if q % 2 == 0 and q:
                    out_next_unit(dve, split_lo, u0 + q // 2 - 1)
                if q == 16:
                    residual(dve, layer, 0, 0)
                    residual(dve, layer, 0, 1)
                if 17 <= q < 20:
                    residual(dve, layer, 0, q - 15)
            out_next_unit(dve, split_lo, u0 + 15)
            for t in range(NT + 2):
                if t < NT:
                    residual(dve, layer, 1, t)
                if t >= 2 and layer == 0 and stage:
                    norm_dve_tile(dve, 1, xn1, t - 2)

        def out_pe(pe, layer):
            u0 = (OUT0, OUT1)[layer]
            for q in range(32):
                hh, kt = q // 16, q % 16
                u = u0 + q // 2
                if kt % 2 == 0:
                    pe.wait_ge(lo_ready, u + 1)
                pe.wait_ge(yl_done, 32 * layer + q + 1)
                for t in range(NT):
                    if hh == 1 and kt == 0 and t >= 3:
                        pe.wait_ge(out_evac, 10 * layer + t - 2)
                    for n, (yy, w) in enumerate(((y_hi, w_hi), (y_hi, w_lo), (y_lo, w_hi))):
                        mm = pe.matmul(PS[:, (5 * hh + t) % 8, :], yy[:, q % 2, t * P:(t + 1) * P],
                                       w[:, u % RING, (kt % 2) * 512:(kt % 2) * 512 + 512],
                                       start=(kt == 0 and n == 0), stop=(kt == 15 and n == 2))
                    if kt == 15 and t < NT - 1:
                        mm.then_inc(out_ready, 1)
                mm.then_inc(unit_used if kt % 2 else y_even_used, 1)

        y_back = [sem(f"y_back{i}") for i in range(4)]

        def start_pe(pe):
            pe.wait_ge(par_landed, 16 * PAR_DMAS)
            pe.transpose(PS[:, 6, 0:P], praw[:, 0, :], ident)
            pe.transpose(PS[:, 6, P:P + 72], praw[0:72, 1, :], ident[0:72, 0:72]).then_inc(par_T, 1)
            pe.wait_ge(cond_ready, 1)
            for s in range(8):
                q, half = s // 2, s % 2
                pe.wait_ge(wm_landed[s % 4], 16 * (s // 4 + 1))
                for t in range(2):
                    for b in range(2):
                        mm = pe.matmul(PS[0:2, 2 * half + b, :], cond[:, :, 2 * q + t], wm_ring[:, s % 4, t, 512 * b:512 * b + 512],
                                       start=(q == 0 and t == 0), stop=(q == 3 and t == 1))
                mm.then_inc(wm_used, 1)

        def start_pe_mod_T(pe):
            pe.wait_ge(mod_copied, 2)
            pe.wait_ge(xt_done, NT)
            for j in range(16):
                mm = pe.transpose(PS[:, 4, 2 * j:2 * j + 2], mod_sb[0:2, j * P:(j + 1) * P], ident[0:2, 0:2])
            mm.then_inc(mod_T, 1)

        def fourier_pe(pe, i, first):
            for k in range(4):
                pe.wait_ge(lo_ready, 4 * i + k + 1)
                if not (first and k < 2):
                    pe.wait_ge(act_freed, 4 * i + k - 1)
                channel_tile(pe, k, k % 2, 0 if first and k == 0 else None)
            pe.wait_ge(ub_ready, 2 * i + 2)
            if first:
                pe.wait_ge(dft_landed, 32)
            else:
                pe.wait_ge(ya_done, 2 * i)
            for b, src in enumerate((2, 3, 0, 1, None)):
                if b == 4:
                    pe.wait_ge(q_ready, i + 1)
                for kt in range(2):
                    lhs = ut[:, kt, LAT:TOK] if src is None else ub[:, kt, src * P:(src + 1) * P]
                    mm = pe.matmul(PS[:, 4 + b % 4, :], lhs, dft_g[:, kt, :], start=(kt == 0), stop=(kt == 1))
                mm.then_inc(gd_ready, 1)
            pe.wait_ge(ab_act, 3 * i + 3)
            pe.wait_ge(ab_dve, i + 1)
            for kt in range(2):
                for r in range(5):
                    o = PS[:, (5, 7)[kt], r * P:(r + 1) * P] if r < 4 else PS[:, (6, 4)[kt], 0:P]
                    cs, sn = (r, 4 + r) if r < 4 else (8, 9)
                    pe.matmul(o, ab[:, r, kt * P:(kt + 1) * P], dft_l[:, cs, :], start=True, stop=False)
                    mm = pe.matmul(o, ab[:, r, 256 + kt * P:256 + (kt + 1) * P], dft_l[:, sn, :], start=False, stop=True)
                mm.then_inc(ld_ready, 1)

        def fourier_act(act, i, first):
            for k in range(4):
                act.wait_ge(unit_used, 4 * i + k + 1)
                src = PSf[:, 1024 * (k % 2):1024 * (k % 2) + TOK]
                if k < 2:
                    if not first:
                        act.wait_ge(gd_ready, 5 * i)
                    act.activation(ut[:, k, :], src, ACT.Copy).then_inc(act_freed, 1)
                else:
                    if not first:
                        act.wait_ge(ya_done, 2 * i)
                    act.activation(sz_a[:, k - 2, :], src, ACT.Silu).then_inc(act_freed, 1)
                split_hi(act, unit(RING, i, 4, k), k)
            act.wait_ge(gd_ready, 5 * i + 1)
            if not first:
                act.wait_ge(ab_dve, i)
            act.activation(d02_sb, PS[:, 4, :], ACT.Copy).then_inc(q_ready, 1)
            if not first:
                act.wait_ge(ld_ready, 2 * i)
            for b, r in ((2, 0), (3, 2), (4, 4)):
                act.wait_ge(gd_ready, 5 * i + b + 1)
                act.activation(ab[:, r, :], PS[:, 4 + b % 4, :], ACT.Copy).then_inc(ab_act, 1)

        def fourier_dve(dve, i, first):
            ch = Chain(dve, fdone, 4 * i)
            for k in range(4):
                if k < 2:
                    dve.wait_ge(act_freed, 4 * i + k + 1)
                    if not first:
                        dve.wait_ge(gd_ready, 5 * i)
                        if k == 0:
                            dve.wait_ge(ub_ready, 2 * i)
                    lo2, hi2 = ut[:, k, 0:256], ut[:, k, 256:512]
                    ch.tick(dve.tensor_tensor(e01[:, k, :], lo2, hi2, ALU.add))
                    ch.tick(dve.tensor_tensor(ub[:, k, 256:512], lo2, hi2, ALU.subtract))
                    ch.sync()
                    dve.tensor_tensor(ub[:, k, 128:256], e01[:, k, 0:P], e01[:, k, P:256], ALU.subtract)
                    dve.tensor_tensor(ub[:, k, 0:P], e01[:, k, 0:P], e01[:, k, P:256], ALU.add).then_inc(ub_ready, 1)
                split_lo(dve, unit(RING, i, 4, k), k)
                if k == 2:
                    mod_slot_dve(dve, 0, i, i, first)
            dve.wait_ge(q_ready, i + 1)
            dve.wait_ge(gd_ready, 5 * i + 2)
            if not first:
                dve.wait_ge(ld_ready, 2 * i)
            C, S = slice(0, 256), slice(256, 512)
            dve.tensor_tensor(ab[:, 1, C], d02_sb[:, C], PS[:, 5, S], ALU.subtract)
            dve.tensor_tensor(ab[:, 1, S], d02_sb[:, S], PS[:, 5, C], ALU.add)
            dve.tensor_tensor(ab[:, 3, C], d02_sb[:, C], PS[:, 5, S], ALU.add)
            dve.tensor_tensor(ab[:, 3, S], d02_sb[:, S], PS[:, 5, C], ALU.subtract).then_inc(ab_dve, 1)
            for kt in range(2):
                dve.wait_ge(ld_ready, 2 * i + kt + 1)
                dve.wait_ge(act_freed, 4 * i + 4)
                yt = yT[:, bass.ds(2 * i + kt, 1), :]
                dve.tensor_tensor(yt[:, 0, 0:LAT].rearrange("p (m r) -> p r m", r=4),
                                  PS[:, (5, 7)[kt], :].rearrange("p (r m) -> p r m", r=4),
                                  sz_a[:, kt, 0:LAT].rearrange("p (m r) -> p r m", r=4), ALU.mult)
                dve.tensor_tensor(yt[:, 0, LAT:TOK], PS[:, (6, 4)[kt], 0:P], sz_a[:, kt, LAT:TOK], ALU.mult).then_inc(ya_done, 1)

        def mod_slot_dve(dve, chunk, tp, n, first):
            ch = Chain(dve, acc_step, 4 * n)
            if first:
                dve.memset(acc[:, :, :], 0.0).then_inc(mod_step, 1)
                dve.wait_ge(mod_step, 2)
            else:
                ch.sync()
            dve.wait_ge(modw_landed, 16 * n + 16)
            for t in range(2):
                if t:
                    ch.sync()
                for c in range(2):
                    ch.tick(dve.scalar_tensor_tensor(out=acc[:, c, :], in0=mod_w[:, t, :],
                                                     scalar=cond[:, c, bass.ds(2 * tp + t, 1)], in1=acc[:, c, :],
                                                     op0=ALU.mult, op1=ALU.add))

        def mod_reduce_pe(pe, i, first):
            pe.wait_ge(acc_step, 16 * i + 16)
            pe.wait_ge(bias_landed, 16 * i + 16)
            if first:
                pe.wait_ge(ya_done, 8)
            else:
                pe.wait_ge(row_copied, i)
            for c in range(2):
                for b in range(2):
                    o = PS[0:1, 4 + 2 * c + b, :]
                    pe.matmul(o, ones[:, 0:1], acc[:, c, 512 * b:512 * b + 512], start=True, stop=False)
                    mm = pe.matmul(o, ones[0:1, 0:1], bias_row[:, 512 * b:512 * b + 512], start=False, stop=True)
            mm.then_inc(red_ready, 1)

        CONV_DVE = 10
        C0 = 16

        def conv_pe(pe, i, first, last):
            for p in range(8):
                pe.wait_ge(lo_ready, C0 + 8 * i + p + 1)
                if p < 4:
                    pe.wait_ge(act_freed, C0 + 4 * i - 1 + p)
                else:
                    pe.wait_ge(dve_freed, 4 * i + p - 3)
                channel_tile(pe, p % 4, p % 2)
                if p == 0:
                    mod_reduce_pe(pe, i, first)

        def conv_act(act, i, first, last):
            for p in range(8):
                act.wait_ge(unit_used, C0 + 8 * i + p + 1)
                src = PSf[:, 1024 * (p % 2):1024 * (p % 2) + TOK]
                j = p % 2
                if p < 2:
                    if first:
                        act.wait_ge(ya_done, 8)
                    else:
                        act.wait_ge(dve_freed, 4 * i - 3 + j)
                    act.activation(cv_c[:, j, :], src, ACT.Copy).then_inc(act_freed, 1)
                if p == 2:
                    act.wait_ge(red_ready, i + 1)
                    if not first:
                        act.wait_ge(row_stored, 16 * i)
                    act.activation(mod_row, PSf[0:1, 2048:4096], ACT.Copy).then_inc(row_copied, 1)
                if p >= 6:
                    if not first:
                        act.wait_ge(yb_done, 2 * i)
                    act.activation(sz_b[:, j, :], src, ACT.Silu).then_inc(act_freed, 1)
                split_hi(act, unit(C0 + RING, i, 8, p), p % 4)

        def conv_dve(dve, i, first, last):
            ch = Chain(dve, conv_step, CONV_DVE * i)
            for p in range(8):
                j = p % 2
                src = PSf[:, 1024 * (p % 2):1024 * (p % 2) + TOK]

                def tap(k):
                    return par2[:, bass.ds(2 * i + (16 + 8 * k + j), 1)]
                rows = [b[:, j, :].rearrange("p (r n) -> p r n", n=64) for b in (cv, cc)]
                if p in (2, 3):
                    dve.wait_ge(unit_used, C0 + 8 * i + p + 1)
                    dve.wait_ge(act_freed, C0 + 4 * i + j + 1)
                    dve.tensor_tensor(cv[:, j, :], src, cv_c[:, j, :], ALU.mult).then_inc(dve_freed, 1)
                    dve.wait_ge(dve_freed, 4 * i + j + 1)
                    ch.tick(dve.tensor_scalar(cc[:, j, :], cv[:, j, :], tap(1), None, ALU.mult))
                    ch.sync()
                    ch.tick(dve.scalar_tensor_tensor(out=rows[1][:, :, 1:64], in0=rows[0][:, :, 0:63], scalar=tap(0),
                                                     in1=rows[1][:, :, 1:64], op0=ALU.mult, op1=ALU.add))
                    ch.sync()
                    ch.tick(dve.scalar_tensor_tensor(out=rows[1][:, :, 0:63], in0=rows[0][:, :, 1:64], scalar=tap(2),
                                                     in1=rows[1][:, :, 0:63], op0=ALU.mult, op1=ALU.add))
                    ch.sync()
                    a, b = LAT + 63, LAT + 64
                    ch.tick(dve.scalar_tensor_tensor(out=cc[:, j, b:b + 1], in0=cv[:, j, a:a + 1], scalar=tap(0),
                                                     in1=cc[:, j, b:b + 1], op0=ALU.mult, op1=ALU.add))
                    ch.tick(dve.scalar_tensor_tensor(out=cc[:, j, a:a + 1], in0=cv[:, j, b:b + 1], scalar=tap(2),
                                                     in1=cc[:, j, a:a + 1], op0=ALU.mult, op1=ALU.add))
                if p in (4, 5):
                    if p == 4:
                        ch.sync()
                    dve.wait_ge(unit_used, C0 + 8 * i + p + 1)
                    dve.tensor_tensor(cc[:, j, :], src, cc[:, j, :], ALU.mult).then_inc(dve_freed, 1)
                if p in (6, 7):
                    dve.wait_ge(dve_freed, 4 * i + 4)
                    dve.wait_ge(act_freed, C0 + 4 * i + 3 + j)
                    dve.tensor_tensor(yT[:, bass.ds(8 + 2 * i + j, 1), :][:, 0, :], cc[:, j, :], sz_b[:, j, :],
                                      ALU.mult).then_inc(yb_done, 1)
                split_lo(dve, unit(C0 + RING, i, 8, p), p % 4)
                if not last and p % 2 == 1:
                    if p == 1:
                        dve.wait_ge(red_ready, i + 1)
                        dve.memset(acc[:, :, :], 0.0).then_inc(mod_step, 1)
                        dve.wait_ge(mod_step, i + 3)
                    conv_mod_slot(dve, i, p // 2)
            assert ch.n == CONV_DVE

        def conv_mod_slot(dve, i, tp):
            ch = Chain(dve, acc_step, 16 * i + 16 + 4 * tp)
            if tp:
                ch.sync()
            dve.wait_ge(modw_landed, 64 * i + 64 + 16 * tp + 16)
            for t in range(2):
                if t:
                    ch.sync()
                for c in range(2):
                    ch.tick(dve.scalar_tensor_tensor(out=acc[:, c, :], in0=mod_w[:, t, :], scalar=cond[:, c, 2 * tp + t:2 * tp + t + 1],
                                                     in1=acc[:, c, :], op0=ALU.mult, op1=ALU.add))


        def ssd_unit_src(g, k):
            if k < 4:
                col = (DI + 256 * g, DI + 256 * g + P, 2 * DI + P * g, 2 * DI + D + P * g)[k]
                return ssd_src[:, :, bass.ds(col, P)]
            return ssd_src[:, 4 * (k - 4):4 * (k - 4) + 4].rearrange("p k (g n) -> p k g n", n=64)[:, :, bass.ds(4 * g, 4)]

        def ssd_load(sp, g, k, slot):
            dst = raw_w[:, slot, :].rearrange("p (k n) -> p k n", n=P)
            if k >= 4:
                dst = raw_w[:, slot, :].rearrange("p (k g n) -> p k g n", k=4, n=64)
            sp.dma_start(dst, ssd_unit_src(g, k)).then_inc(landed[slot], 16)

        def state_view(t, d, g):
            return t[0, 0, d].rearrange("(g j q) p n -> (q p) g j n", j=2, q=2)[:, bass.ds(g, 1), :, :]

        def lfb_load(sp, g, c, slot):
            src = l_scr.rearrange("(g r) t -> g r t", r=8)[bass.ds(g, 1), :, c * P:(c + 1) * P]
            sp.dma_start(lfb[:, slot, :, :], src.partition_broadcast(P)).then_inc(lfb_landed[slot], 16)

        def table(tab, off, n):
            return tab[:, 0:200].rearrange("p (c k) -> p c k", c=NT)[:, :, off:off + n]

        def all_tables(off, n):
            return GT[:, :, 0:200].rearrange("p g (c k) -> p c g k", c=NT)[:, :, :, off:off + n]
        EL, DTO, WDT, DEC, DLT, NLB = 0, 8, 16, 24, 32, 36

        def perm(v):
            return v.rearrange("p (d g h) -> p g d h", d=2, g=G)

        def by_group(v):
            return v.rearrange("p c (g r) -> p c g r", g=G)

        def table_sp(sp):
            sp.dma_start(dtw_raw, ssd_src[:, :, SSD_IN - 64:SSD_IN]).then_inc(dtw_landed, 16)

        def table_sp2(sp):
            sp.dma_start(b_in, A["ssd_dt_bias"][0].rearrange("d h -> (d h)").partition_broadcast(P)).then_inc(bc_landed, 16)
            sp.dma_start(a_in, A["ssd_a_log"][0].rearrange("d h -> (d h)").partition_broadcast(P)).then_inc(bc_landed, 16)
            sp.dma_start(d_in, A["ssd_d"][0].partition_broadcast(P)).then_inc(bc_landed, 16)
            for d in range(2):
                sp.dma_start(h0r[:, 2 * d:2 * d + 2, :], state_view(A["state_ssm"], d, 0)[:, 0]).then_inc(h0_landed, 16)
            sp.wait_ge(yt_done, 1)
            sp.dma_start(l_scr, lrow[0:64, :]).then_inc(small_stored, 16)
            sp.wait_ge(small_stored, 16)
            for c in range(2):
                lfb_load(sp, 0, c, c)

        wd = [y[:, :, :].rearrange("p a b -> p (a b)")[:, 0:512].rearrange("p (k g r) -> p k g r", k=KT, g=G) for y in (y_hi, y_lo)]

        def dt_weights_act(act):
            act.wait_ge(unit_used, IN1)
            act.wait_ge(dtw_landed, 16)
            src = dtw_raw.rearrange("p k (d g h) -> p k d g h", d=2, g=G)
            for d in range(2):
                act.activation(wd[0][:, :, :, 4 * d:4 * d + 4], src[:, :, d], ACT.Copy).then_inc(dtw_hi, 1)

        def table_act(act):
            act.wait_ge(y_stored[0], 16)
            act.wait_ge(y_stored[1], 16)
            act.wait_ge(bc_landed, 48)
            act.wait_ge(h_ready, 2 * KT)
            act.activation(a_pm.rearrange("p (g d h) -> p g d h", g=G, d=2)[:, :, 0, :], perm(a_in)[:, :, 0, :], ACT.Exp)
            act.activation(a_pm.rearrange("p (g d h) -> p g d h", g=G, d=2)[:, :, 1, :], perm(a_in)[:, :, 1, :], ACT.Exp).then_inc(tab_act, 1)
            act.wait_ge(tab_dve, 4)
            act.activation(tU, tNA, ACT.Exp).then_inc(tab_act, 1)
            act.wait_ge(tab_dve, 6)
            act.activation(tLW, tW, ACT.Ln).then_inc(tab_act, 1)
            act.wait_ge(cum_ready, 1)
            act.activation(tL, PS[:, 1, 0:320].rearrange("p (c r) -> p c r", c=NT), ACT.Copy).then_inc(tab_act, 1)
            act.wait_ge(tab_dve, 14)
            act.activation(tX, tT, ACT.Exp).then_inc(tab_act, 1)
            act.wait_ge(lt_ready, 1)
            act.activation(lrow[0:64, :], PSf[0:64, 2048:2048 + TOK], ACT.Copy).then_inc(yt_done, 1)
            act.activation(all_tables(EL, 8), by_group(tL), ACT.Exp)
            act.wait_ge(tot_copied, 1)
            act.activation(all_tables(DEC, 8), by_group(tNX), ACT.Exp).then_inc(tab_act, 1)

        def table_pe(pe):
            pe.wait_ge(dtw_lo, 2)
            pe.wait_ge(h_ready, 2 * KT)
            for t in range(NT):
                for k in range(KT):
                    for n, (h, w) in enumerate(((h_hi, 0), (h_hi, 1), (h_lo, 0))):
                        mm = pe.matmul(PS[:, 0, 64 * t:64 * t + 64], h[:, k, t * P:(t + 1) * P],
                                       wd[w][:, k].rearrange("p g r -> p (g r)"),
                                       start=(k == 0 and n == 0), stop=(k == KT - 1 and n == 2))
            mm.then_inc(dtp_ready, 1)
            pe.wait_ge(tab_dve, 13)
            o = PS[:, 1, 0:320].rearrange("p (c g d h) -> p c g d h", c=NT, g=G, d=2)
            da = tDA.rearrange("p c (g d h) -> p c g d h", g=G, d=2)
            pe.matmul(o[:, :, :, 0], upper, da[:, :, :, 0], start=True, stop=True)
            pe.matmul(o[:, :, :, 1], lower, da[:, :, :, 1], start=True, stop=True)
            pe.matmul(PS[:, 2, 0:320], ones[:, :], tDA.rearrange("p c r -> p (c r)"), start=True, stop=True).then_inc(cum_ready, 1)
            pe.wait_ge(tab_act, 4)
            for t in range(NT):
                mm = pe.transpose(PSf[0:64, 2048 + t * P:2048 + (t + 1) * P], tL[:, t, :], ident)
            mm.then_inc(lt_ready, 1)

        def table_dve(dve):
            dve.wait_ge(unit_used, IN1)
            for d in range(2):
                dve.wait_ge(dtw_hi, d + 1)
                dve.tensor_tensor(wd[1][:, :, :, 4 * d:4 * d + 4], dtw_raw.rearrange("p k (d g h) -> p k d g h", d=2, g=G)[:, :, d],
                                  wd[0][:, :, :, 4 * d:4 * d + 4].bitcast(F32), ALU.subtract).then_inc(dtw_lo, 1)

        def table_dve2(dve):
            dve.wait_ge(y_stored[0], 16)
            dve.wait_ge(y_stored[1], 16)
            dve.wait_ge(bc_landed, 48)
            p1 = par1[:, :].rearrange("p (k t) -> p k t", k=4)
            CPv = CPG.rearrange("p g (i k) -> p i k g", i=4)
            for i in range(4):
                src = p1[:, :, i:16:2] if i < 2 else p1[:, :, 16 + 8 * (i - 2):24 + 8 * (i - 2)]
                dve.tensor_copy(CPv[:, i], src)
            dve.tensor_copy(GT[:, :, 200:204], d_in.rearrange("p (g h) -> p g h", g=G))
            dve.tensor_scalar(GT[:, :, 204:206], par2[:, 40:56].rearrange("p (g j) -> p g j", g=G), 0.5, None, ALU.mult)
            ch = Chain(dve, tab_dve)
            for d in range(2):
                last = dve.tensor_copy(b_pm.rearrange("p (g d h) -> p g d h", g=G, d=2)[:, :, d, :], perm(b_in)[:, :, d, :])
            ch.tick(last)
            ch.sync()
            dve.wait_ge(dtp_ready, 1)
            ch.tick(dve.tensor_tensor(tX, PS[:, 0, 0:320].rearrange("p (c r) -> p c r", c=NT),
                                      b_pm.unsqueeze(1).to_broadcast([P, NT, 64]), ALU.add))
            ch.sync()
            ch.tick(dve.tensor_scalar(tNX, tX, -1.0, None, ALU.mult))
            ch.sync()
            ch.tick(dve.tensor_tensor(tNA, tX, tNX, ALU.min))
            ch.tick(dve.tensor_scalar(tC, tX, 0.0, None, ALU.max))
            dve.wait_ge(tab_act, 2)
            ch.tick(dve.tensor_scalar(tW, tU, 1.0, None, ALU.add))
            ch.sync()
            ch.tick(dve.tensor_scalar(tNA, tW, -1.0, None, ALU.add))
            ch.sync()
            ch.tick(dve.tensor_tensor(tNA, tU, tNA, ALU.subtract))
            ch.tick(dve.reciprocal(tT, tW))
            ch.sync()
            ch.tick(dve.tensor_tensor(tNA, tNA, tT, ALU.mult))
            dve.wait_ge(tab_act, 3)
            ch.sync()
            ch.tick(dve.tensor_tensor(tNA, tNA, tLW, ALU.add))
            ch.sync()
            ch.tick(dve.tensor_tensor(tDT, tNA, tC, ALU.add))
            ch.sync()
            ch.tick(dve.scalar_tensor_tensor(out=tDA, in0=tDT, scalar=-1.0, in1=a_pm.unsqueeze(1).to_broadcast([P, NT, 64]),
                                             op0=ALU.mult, op1=ALU.mult))
            dve.wait_ge(tab_act, 4)
            ch.sync()
            ch.tick(dve.tensor_tensor(tT, PS[:, 2, 0:320].rearrange("p (c r) -> p c r", c=NT), tL, ALU.subtract))
            dve.tensor_copy(tNX, PS[:, 2, 0:320].rearrange("p (c r) -> p c r", c=NT)).then_inc(tot_copied, 1)
            dve.tensor_copy(all_tables(DTO, 8), by_group(tDT))
            lv = tL.rearrange("p c (g d h) -> p c g d h", g=G, d=2)
            for c in range(NT):
                dve.tensor_tensor(all_tables(DLT, 4)[:, c], lv[:, c, :, 1], lv[:, c, :, 0], ALU.subtract)
            for c in range(NT):
                dve.tensor_scalar(all_tables(NLB, 4)[:, c], lv[:, c, :, 1], -1.0, None, ALU.mult)
            dve.wait_ge(tab_act, 5)
            dve.tensor_tensor(all_tables(WDT, 8), by_group(tDT), by_group(tX), ALU.mult).then_inc(tables_ready, 1)

        def groups_copy(pool, g_ssd, g_proj, ps, pp):
            last = None
            if g_ssd is not None:
                last = pool.tensor_copy(gt[:, ps, :].unsqueeze(1), GT[:, bass.ds(g_ssd, 1), :])
            if g_proj is not None:
                last = pool.tensor_copy(cp[:, pp, :].unsqueeze(1), CPG[:, bass.ds(g_proj, 1), :])
            return last

        BODY = """
        P00 T0 P01 tok0 T1 P02 tok1 T2 M0 lfb0 P03 tok2 T3 xdt0 P04 tok3 T4 exp0 M1 lfb1 P05 tok4 H0 xw0 exp1 P06 CB0 hev0 hd0 xw1
        P07 cbm0 CB1 cen0 G0 cbm1 tap0 hi0 xw2 lo0 ld0
        P10 tanh0 P11 S0 fin0 xw3 P12 hup0 hd1 xdt1 P13 S1 G1 P14 hup1 hd2 M2 lfb2 P15 S2 exp2 P16 hup2 SC0 P17 scev0 nst0
        cen1 tap1 hi1 lo1 ld1 Y0
        P20 tanh1 yt0 u0 fin1 P21 xdt2 G2x P22 ya0 sq0 rs0 P23 Y1 M3 lfb3 P24 yn0 yt1 u1 G2 exp3 P25 ya1 sq1 rs1 P26 yn1 P27
        cen2 tap2 hi2 lo2 ld2 YT0
        P30 ytev0 yst0 tanh2 P31 fin2 P32 Y2 xdt3 P33 yt2 u2 G3 P34 YT1 ytev1 yst1 M4 lfb4 P35 ya2 sq2 rs2 exp4 P36 Y3 yn2 P37
        yt3 u3 cen3 tap3 hi3 lo3 ld3
        Z00 YT2 ytev2 yst2 xdt4 G4 tanh3 fin3 Z01 ya3 sq3 rs3 ztanh0 sz0 Z10 Y4 yn3 Z11 u4 ztanh1 sz1 YT3 ytev3 yst3
        Z20 ya4 sq4 rs4 Z21 ztanh2 sz2 Z30 yn4 Z31 ztanh3 sz3 YT4 ytev4 yst4 Z40 Z41 ztanh4 sz4 hi4 lo4 ld4 hi5 lo5 ld5 grp0
        """.split()
        BODY = [(e.rstrip("0123456789"), e[len(e.rstrip("0123456789")):]) for e in BODY if e != "G2x"]
        PROJ = ("P", "Z", "cen", "tap", "tanh", "fin", "ztanh", "sz", "hi", "lo", "ld")

        class Body:

            def __init__(self, i, par, ssd=True, proj=True):
                self.i, self.par, self.ssd, self.proj = i, par, ssd, proj
                self.g = 2 * i + par
                self.n = self.g + 1
                self.np = (par + 1) % 2
                self.static = isinstance(i, int)

            def steps(self):
                for ev, num in BODY:
                    if (ev in PROJ and self.proj) or (ev not in PROJ and self.ssd):
                        yield ev, [int(d) for d in num]

            def unit(self, k):
                return 12 * self.i + (IN1 + 6 * (self.par + 1) + k), (6 * (self.par + 1) + k) % RING

            def split_unit(self, k):
                c = IN1 + 6 * (self.par + 1) + k + 4
                if self.static:
                    return c + 12 * self.i
                return (12 * self.i + c, 48 * self.i + 16 * (c // RING + 1))

            def count2(self, c):
                m = 5 * self.par + c
                return 5 * self.i + m // 2, m % 2

        def ssd_pe(pe, B):
            g, n = B.g, B.n
            b0 = 5 * g
            for ev, a in B.steps():
                k = a[0]
                if ev == "P":
                    u, slot = B.unit(k)
                    pair, kt = (B.np + k) % 2, a[1]
                    if kt == 0:
                        pe.wait_ge(lo_ready, u + 1)
                        if not (B.static and 9 * n + k < 2):
                            pe.wait_ge(proj_free, 9 * n + k - 1)
                        elif k == 1:
                            pe.wait_ge(tot_copied, 1)
                    ws = slice(kt * P, (kt + 1) * P)
                    for j, (w, h) in enumerate(((w_hi, h_hi), (w_hi, h_lo), (w_lo, h_hi))):
                        for s, (lo, hi) in enumerate(SEGS):
                            mm = pe.matmul(PS[:, 2 * pair + s, 0:hi - lo], w[:, slot, ws], h[:, kt, lo:hi],
                                           start=(kt == 0 and j == 0), stop=(kt == KT - 1 and j == 2))
                    if kt == KT - 1:
                        mm.then_inc(unit_used, 1)
                elif ev == "Z":
                    t, half = a
                    u, slot = B.unit(4)
                    pair = (B.np + 4 + t) % 2
                    if t == 0 and half == 0:
                        pe.wait_ge(lo_ready, u + 2)
                    if half == 0:
                        pe.wait_ge(proj_free, 9 * n + 3 + t)
                    for kt in range(4 * half, 4 * half + 4):
                        for j, (h, w) in enumerate(((h_hi, w_hi), (h_hi, w_lo), (h_lo, w_hi))):
                            mm = pe.matmul(PS[:, 2 * pair, 0:256], h[:, kt, t * P:(t + 1) * P],
                                           w[:, slot + kt // 4, 256 * (kt % 4):256 * (kt % 4) + 256],
                                           start=(kt == 0 and j == 0), stop=(kt == KT - 1 and j == 2))
                    if half == 1:
                        mm.then_inc(*((z_ready, 1) if t < NT - 1 else (unit_used, 2)))
                elif ev == "T":
                    if k == 0:
                        pe.wait_ge(conv_done, 4 * g + 4)
                        pe.wait_ge(yt_done, b0 + 1)
                    if k >= 2:
                        pe.wait_ge(tok_done, b0 + k - 1)
                    for j in range(3):
                        mm = pe.transpose(PS[:, 4 + k % 2, j * P:(j + 1) * P], cvx[:, j, k * P:(k + 1) * P], ident)
                    mm.then_inc(tr_ready, 1)
                elif ev == "H":
                    pe.wait_ge(h0_landed, 32 * g + 32)
                    for j in range(4):
                        mm = pe.transpose(PS[:, 6, j * P:(j + 1) * P], h0r[:, j, :], ident)
                    mm.then_inc(h_T, 1)
                elif ev == "CB":
                    if k == 1:
                        pe.wait_ge(tok_done, b0 + 4)
                    for c in range(4) if k == 0 else (4,):
                        o = PS[:, 7, c * P:(c + 1) * P] if k == 0 else PS[:, 5, 0:P]
                        mm = pe.matmul(o, cvx[:, 2, c * P:(c + 1) * P], cvC[:, B.par, c * P:(c + 1) * P], start=True, stop=True)
                    mm.then_inc(cb_ready, 1)
                elif ev == "S":
                    pe.wait_ge(xw_done, 4 * g + k + 1)
                    if k == 0:
                        pe.wait_ge(cbm_done, 2 * g + 2)
                    else:
                        pe.wait_ge(st_done, 3 * g + k)
                    pe.matmul(PS[:, 5, 0:256], xb[:, k, 256:384], xws[:, k, 0:256], start=True, stop=True)
                    pe.matmul(PS[:, 5, 256:512], xb[:, 3 - k, 256:384], xws[:, k, 256:512], start=True, stop=True).then_inc(st_ready, 1)
                elif ev == "SC":
                    pe.wait_ge(xw_done, 4 * g + 4)
                    pe.wait_ge(tok_done, b0 + 5)
                    for j in range(4):
                        mm = pe.matmul(PS[:, 4, j * P:(j + 1) * P], xws[:, 3, j * P:(j + 1) * P], xb[:, 4, 256:384], start=True, stop=True)
                    mm.then_inc(sc_ready, 1)
                elif ev == "Y":
                    r = (B.par + k) % 2
                    bo, bd = (6, 7) if k % 2 == 0 else (4, 5)
                    if k == 0:
                        pe.wait_ge(st_done, 3 * g + 3)
                        pe.wait_ge(hs0_done, g + 1)
                    elif k == 1:
                        pe.wait_ge(sc_done, g + 1)
                    else:
                        pe.wait_ge(yt_done, b0 + k)
                    if k < 4:
                        cc_ = cvC[:, B.par, k * P:(k + 1) * P]
                        pe.matmul(PS[:, bo, 0:256], cc_, hs[:, k, 0:256], start=True, stop=True)
                        pe.matmul(PS[:, bo, 256:512], cc_, hs[:, 3 - k, 256:512], start=True, stop=True)
                    pe.wait_ge(g_done, b0 + k + 1)
                    for h in range(4):
                        o = PS[:, bd, 64 * h:64 * h + 64]
                        pe.matmul(o, gm[:, r, 0, h, :], xdt[:, r, 64 * h:64 * h + 64], start=True, stop=False)
                        mm = pe.matmul(o, gm[:, r, 1, h, :], xdt[:, r, 256 + 64 * h:256 + 64 * h + 64], start=False, stop=True)
                    mm.then_inc(y_ready, 1)
                elif ev == "YT":
                    r = (B.par + k) % 2
                    pe.wait_ge(yn_done, b0 + k + 1)
                    for j in range(2):
                        mm = pe.transpose(PS[:, (6, 4)[k % 2], j * P:(j + 1) * P], yn[:, r, j * P:(j + 1) * P], ident)
                    mm.then_inc(ytr_ready, 1)

        def ssd_act(act, B):
            g, n = B.g, B.n
            b0 = 5 * g
            act.wait_ge(grp_done, n if not (B.static and n == 0) else 1)
            for ev, a in B.steps():
                k = a[0]
                pair = (B.np + k) % 2
                src = PSf[:, 1024 * pair:1024 * pair + TOK]
                cpn = cp[:, B.np, :]
                cv_ = cvx[:, k, :] if k < 3 else cvC[:, B.np, :]
                if ev == "cen":
                    u, _ = B.unit(k)
                    act.wait_ge(unit_used, u + 1)
                    if not (B.static and n == 0):
                        act.wait_ge(*((cb_ready, 2 * n) if k == 2 else (tr_ready, 5 * n)))
                    act.activation(cv_, src, ACT.Identity, bias=cpn[:, 4 * k + 3:4 * k + 4], scale=cpn[:, 4 * k + 1:4 * k + 2]).then_inc(cen_done, 1)
                elif ev == "tanh":
                    act.wait_ge(proj_free, 9 * n + k + 1)
                    if not (B.static and 4 * n + k == 0):
                        act.wait_ge(conv_done, 4 * n + k)
                    act.activation(th, cv_, ACT.Tanh).then_inc(th_done, 1)
                elif ev == "ztanh":
                    if k < NT - 1:
                        act.wait_ge(z_ready, 4 * n + k + 1)
                    else:
                        act.wait_ge(unit_used, B.unit(4)[0] + 2)
                    if k >= 2:
                        act.wait_ge(proj_free, 9 * n + 4 + k - 1)
                    zs = PS[:, 2 * ((B.np + 4 + k) % 2), 0:256]
                    act.activation(zth[:, k % 2, :], zs, ACT.Tanh, scale=0.5).then_inc(zth_done, 1)
                elif ev == "hi":
                    split_hi(act, B.split_unit(k), B.unit(k)[1])
                elif ev == "tok":
                    act.wait_ge(tr_ready, b0 + k + 1)
                    act.activation(xb[:, k, :], PS[:, 4 + k % 2, 0:384], ACT.Copy).then_inc(tok_done, 1)
                elif ev == "hev":
                    act.wait_ge(h_T, g + 1)
                    act.activation(hs[:, 0, :], PS[:, 6, :], ACT.Copy).then_inc(hs0_done, 1)
                elif ev == "exp":
                    act.wait_ge(m_done, b0 + k + 1)
                    r = (B.par + k) % 2
                    for h in range(4):
                        e = act.activation(ea[:, r, h, :], ea[:, r, h, :], ACT.Exp, bias=table(gt[:, B.par, :], NLB, 4)[:, k, h:h + 1])
                    e.then_inc(exp_done, 1)
                elif ev == "scev":
                    act.wait_ge(sc_ready, g + 1)
                    act.wait_ge(small_stored, 32 * g + 16)
                    act.activation(nst, PS[:, 4, :], ACT.Copy).then_inc(sc_done, 1)
                elif ev == "sq":
                    r = (B.par + k) % 2
                    act.wait_ge(gz_done, b0 + k + 1)
                    act.activation(yn[:, r, :], aa[:, r, :], ACT.Square, scale=1.0 / 32, accum_out=ssy[:, r:r + 1]).then_inc(sqy_done, 1)
                elif ev == "yn":
                    r = (B.par + k) % 2
                    act.wait_ge(ry_done, b0 + k + 1)
                    act.activation(yn[:, r, :], aa[:, r, :], ACT.Copy, scale=ry[:, r:r + 1]).then_inc(yn_done, 1)
                elif ev == "ytev":
                    cnt, r = B.count2(k)
                    act.wait_ge(ytr_ready, b0 + k + 1)
                    act.wait_ge(y_stored[r], 16 * cnt + 16)
                    for j in range(2):
                        e = act.activation(ysb[:, r, j, :], PS[:, (6, 4)[k % 2], j * P:(j + 1) * P], ACT.Copy,
                                           scale=gt[:, B.par, 204 + j:205 + j])
                    e.then_inc(yt_done, 1)

        def ssd_dve(dve, B):
            g, n = B.g, B.n
            b0 = 5 * g
            dve.wait_ge(grp_done, n if not (B.static and n == 0) else 1)
            tab = gt[:, B.par, :]

            def heads(off, nh, c):
                return table(tab, off, nh)[:, c, :].unsqueeze(2).to_broadcast([P, nh, 64])
            for ev, a in B.steps():
                k = a[0]
                pair = (B.np + k) % 2
                r = (B.par + k) % 2
                if ev == "tap":
                    cpn = cp[:, B.np, :]
                    cv_ = cvx[:, k, :] if k < 3 else cvC[:, B.np, :]
                    src = PSf[:, 1024 * pair:1024 * pair + TOK]
                    dve.wait_ge(cen_done, 4 * n + k + 1)
                    for side, (lo, hi) in ((0, SEGS[0]), (0, SEGS[1]), (2, SEGS[0]), (2, SEGS[1])):
                        o = cv_[:, lo + 1:hi] if side == 0 else cv_[:, lo:hi - 1]
                        i_ = src[:, lo:hi - 1] if side == 0 else src[:, lo + 1:hi]
                        if side == 2 and lo == 0:
                            dve.wait_ge(tap_step, 12 * n + 3 * k + 2)
                        ins = dve.scalar_tensor_tensor(out=o, in0=i_, scalar=cpn[:, 4 * k + side:4 * k + side + 1], in1=o,
                                                       op0=ALU.mult, op1=ALU.add)
                        ins.then_inc(proj_free if side == 2 and lo else tap_step, 1)
                elif ev == "fin":
                    cv_ = cvx[:, k, :] if k < 3 else cvC[:, B.np, :]
                    dve.wait_ge(th_done, 4 * n + k + 1)
                    dve.scalar_tensor_tensor(out=cv_, in0=th, scalar=1.0, in1=cv_, op0=ALU.add, op1=ALU.mult).then_inc(conv_done, 1)
                elif ev == "sz":
                    zs = PS[:, 2 * ((B.np + 4 + k) % 2), 0:256]
                    dve.wait_ge(zth_done, 5 * n + k + 1)
                    if not (B.static and n == 0):
                        dve.wait_ge(gz_done, 5 * n - 5 + k + 1)
                    dve.scalar_tensor_tensor(out=sz[:, k, :], in0=zth[:, k % 2, :], scalar=1.0, in1=zs,
                                             op0=ALU.add, op1=ALU.mult).then_inc(proj_free, 1)
                elif ev == "lo":
                    split_lo(dve, B.split_unit(k), B.unit(k)[1])
                elif ev == "M":
                    cnt, slot = B.count2(k)
                    dve.wait_ge(lfb_landed[slot], 16 * cnt + 16)
                    if k >= 2:
                        dve.wait_ge(g_done, b0 + k - 1)
                    for h in range(4):
                        e = dve.scalar_tensor_tensor(out=ea[:, r, h, :], in0=lfb[:, slot, h, :], scalar=table(tab, DLT, 4)[:, k, h:h + 1],
                                                     in1=lfb[:, slot, 4 + h, :], op0=ALU.add, op1=ALU.min)
                    e.then_inc(m_done, 1)
                elif ev == "cbm":
                    dve.wait_ge(cb_ready, 2 * g + k + 1)
                    m, src = (4, PS[:, 7, :].rearrange("p (c l) -> p c l", c=4)) if k == 0 else (1, PS[:, 5, 0:P].unsqueeze(1))
                    for j, mask in enumerate((upper, lower)):
                        e = dve.tensor_tensor(cbm[:, j, 4 * k:4 * k + m, :], src, mask.unsqueeze(1).to_broadcast([P, m, P]), ALU.mult)
                    e.then_inc(cbm_done, 1)
                elif ev == "xdt":
                    dve.wait_ge(tok_done, b0 + k + 1)
                    if k >= 2:
                        dve.wait_ge(y_ready, b0 + k - 1)
                    dve.tensor_tensor(xdt[:, r, :].rearrange("p (d h q) -> p d h q", d=2, h=4),
                                      xb[:, k, 0:256].rearrange("p (h q) -> p h q", h=4).unsqueeze(1).to_broadcast([P, 2, 4, 64]),
                                      table(tab, DTO, 8)[:, k, :].rearrange("p (d h) -> p d h", d=2).unsqueeze(3).to_broadcast([P, 2, 4, 64]),
                                      ALU.mult)
                elif ev == "G":
                    dve.wait_ge(exp_done, b0 + k + 1)
                    dve.wait_ge(cbm_done, 2 * g + (1 if k < 4 else 2))
                    if k >= 2:
                        dve.wait_ge(y_ready, b0 + k - 1)
                    for j in range(2):
                        e = dve.tensor_tensor(gm[:, r, j, :, :], ea[:, r, :, :], cbm[:, j, k, :].unsqueeze(1).to_broadcast([P, 4, P]), ALU.mult)
                    e.then_inc(g_done, 1)
                elif ev == "hup":
                    dve.wait_ge(st_ready, 3 * g + k + 1)
                    dve.wait_ge(hd_done, 3 * g + k + 1)
                    dve.tensor_tensor(hs[:, k + 1, :], PS[:, 5, :], hd, ALU.add).then_inc(st_done, 1)
                elif ev == "yt":
                    dve.wait_ge(y_ready, b0 + k + 1)
                    if k >= 1:
                        dve.wait_ge(u_done, b0 + k)
                    dve.tensor_tensor(yo.rearrange("p (h q) -> p h q", h=8), PS[:, (6, 4)[k % 2], :].rearrange("p (h q) -> p h q", h=8),
                                      heads(EL, 8, k), ALU.mult).then_inc(t_done, 1)
                elif ev == "ya":
                    dve.wait_ge(u_done, b0 + k + 1)
                    dve.wait_ge(y_ready, b0 + k + 1)
                    if k >= 2:
                        dve.wait_ge(yn_done, b0 + k - 1)
                    dve.tensor_tensor(aa[:, r, :], PS[:, (7, 5)[k % 2], 0:256], uu[:, r, :], ALU.add).then_inc(a_step, 1)
                    dve.wait_ge(a_step, b0 + k + 1)
                    dve.tensor_tensor(aa[:, r, :], aa[:, r, :], sz[:, k, :], ALU.mult).then_inc(gz_done, 1)

        def ssd_pool(pool, B):
            g, n = B.g, B.n
            b0 = 5 * g
            tab = gt[:, B.par, :]
            ch = Chain(pool, pool_step, 8 * g)

            def xh(c):
                return xb[:, c, 0:256].rearrange("p (h q) -> p h q", h=4)

            def heads(col):
                return col.unsqueeze(2).to_broadcast([P, 4, 64])

            def hv(v):
                return v.rearrange("p (h q) -> p h q", h=4)
            if B.ssd:
                pool.wait_ge(grp_done, n)
            for ev, a in B.steps():
                k = a[0]
                r = (B.par + k) % 2
                if ev == "xw":
                    pool.wait_ge(tok_done, b0 + (4 if k == 0 else 5))
                    for d in range(2):
                        c = (k, 3 - k)[d] if k < 3 else 4
                        e = pool.tensor_tensor(hv(xws[:, k, 256 * d:256 * d + 256]), xh(c), heads(table(tab, WDT + 4 * d, 4)[:, c, :]), ALU.mult)
                    e.then_inc(xw_done, 1)
                elif ev == "hd":
                    pool.wait_ge(*((hs0_done, g + 1) if k == 0 else (st_done, 3 * g + k)))
                    for d in range(2):
                        c = (k, 3 - k)[d]
                        e = pool.tensor_tensor(hv(hd[:, 256 * d:256 * d + 256]), hv(hs[:, k, 256 * d:256 * d + 256]),
                                               heads(table(tab, DEC + 4 * d, 4)[:, c, :]), ALU.mult)
                    e.then_inc(hd_done, 1)
                elif ev == "u":
                    if k < 4:
                        pool.wait_ge(t_done, 4 * g + k + 1)
                    else:
                        pool.wait_ge(gz_done, b0 + 3)
                    xd = pool.tensor_tensor(hv(uu[:, r, :]), xh(k), heads(gt[:, B.par, 200:204]), ALU.mult)
                    if k == 4:
                        xd.then_inc(u_done, 1)
                    else:
                        ch.tick(xd)
                        ch.tick(pool.tensor_tensor(yo[:, 0:256], yo[:, 0:256], yo[:, 256:512], ALU.add))
                        ch.sync()
                        pool.tensor_tensor(uu[:, r, :], uu[:, r, :], yo[:, 0:256], ALU.add).then_inc(u_done, 1)
                elif ev == "rs":
                    pool.wait_ge(sqy_done, b0 + k + 1)
                    pool.tensor_tensor(ry[:, r:r + 1], ssy[:, r:r + 1], eps_col[:, :], ALU.add).then_inc(msy_done, 1)
                    pool.wait_ge(msy_done, b0 + k + 1)
                    pool.tensor_tensor(ry[:, r:r + 1], ry[:, r:r + 1], half_neg[:, :], ALU.pow).then_inc(ry_done, 1)
                elif ev == "grp":
                    more = (not B.static) or g + 2 < G
                    if not B.static or g + 1 < G:
                        pool.wait_ge(yt_done, b0 + 1)
                        pool.wait_ge(conv_done, 4 * g + 4)
                        groups_copy(pool, g + 1, g + 2 if more else None, 1 - B.par, B.par).then_inc(grp_done, 1)

        def ssd_sp(sp, B):
            g, n = B.g, B.n
            b0 = 5 * g
            for ev, a in B.steps():
                k = a[0]
                if ev == "ld":
                    u, slot = B.unit(k)
                    sp.wait_ge(lo_ready, u + 3)
                    if B.static and n + 1 >= G:
                        out_load(sp, 1, k)
                    else:
                        ssd_load(sp, 2 * B.i + (B.par + 2), k, (slot + 6) % RING)
                elif ev == "lfb":
                    if B.static and g == G - 1 and k >= 3:
                        continue
                    sp.wait_ge(m_done, b0 + k + 1)
                    gg, c = (g, k + 2) if k < 3 else (g + 1, k - 3)
                    lfb_load(sp, gg, c, B.count2(k)[1])
                elif ev == "nst":
                    sp.wait_ge(sc_done, g + 1)
                    for d in range(2):
                        sp.dma_start(state_view(new_state, d, g)[:, 0], nst.rearrange("p (j n) -> p j n", j=4)[:, 2 * d:2 * d + 2, :]).then_inc(small_stored, 16)
                    if not (B.static and g + 1 == G):
                        sp.wait_ge(h_T, g + 1)
                        for d in range(2):
                            sp.dma_start(h0r[:, 2 * d:2 * d + 2, :], state_view(A["state_ssm"], d, g + 1)[:, 0]).then_inc(h0_landed, 16)
                elif ev == "yst":
                    _, r = B.count2(k)
                    sp.wait_ge(yt_done, b0 + k + 2)
                    sp.dma_start(y_scr[:, bass.ds(2 * g, 2), k * P:(k + 1) * P], ysb[:, r, :, :]).then_inc(y_stored[r], 16)

        def all_groups(eng, part):
            part(eng, Body(-1, 1, ssd=False))
            with eng.Fori(0, 3) as i:
                part(eng, Body(i, 0))
                part(eng, Body(i, 1))
            part(eng, Body(3, 0))
            part(eng, Body(3, 1, proj=False))

        PAR_DMAS = 7

        def fc_col(u):
            if u < 16:
                i, k = u // 4, u % 4
                return (0, 0, D, D)[k] + P * (2 * i + k % 2)
            i, p = (u - 16) // 8, (u - 16) % 8
            return (3 * D, 4 * D, 2 * D, 5 * D)[p // 2] + P * (2 * i + p % 2)

        def out_load(sp, layer, v):
            u = (OUT0, OUT1)[layer] + v
            sp.dma_start(raw_w[:, u % 4, :].rearrange("p (k n) -> p k n", k=2),
                         wout_src[layer][:, 2 * (v % 8):2 * (v % 8) + 2, 512 * (v // 8):512 * (v // 8) + 512]).then_inc(landed[u % 4], 16)

        @block.sync
        def _(sp):
            sp.dma_start(cond[:, 0, :], A["c"].rearrange("a (p t) -> (a p) t", t=KT)).then_inc(cond_landed, 16)
            sp.dma_start(cond[:, 1, :], A["c_ctx"].rearrange("(p t) -> p t", t=KT)).then_inc(cond_landed, 16)
            sp.dma_start(cst[:, :], A["consts"]).then_inc(par_landed, 16)
            sp.dma_start(praw[0:96, 0, :], A["ssd_conv_w"].rearrange("a k (t n) -> (a k t) n", n=P)).then_inc(par_landed, 16)
            sp.dma_start(praw[96:128, 0, :], A["ssd_conv_b"].rearrange("a (t n) -> (a t) n", n=P)).then_inc(par_landed, 16)
            sp.dma_start(praw[0:16, 1, :], A["norm_g"].rearrange("a (t n) -> (a t) n", n=P)).then_inc(par_landed, 16)
            sp.dma_start(praw[16:40, 1, :], A["fc_conv_w"].rearrange("a k (t n) -> (a k t) n", n=P)).then_inc(par_landed, 16)
            sp.dma_start(praw[40:56, 1, :], A["ssd_norm_g"].rearrange("a (t n) -> (a t) n", n=P)).then_inc(par_landed, 16)
            sp.dma_start(praw[56:72, 1, :], A["b_mod"].rearrange("a (t n) -> (a t) n", n=P)[0:16, :]).then_inc(par_landed, 16)
            xs = A["x_sample"][0].rearrange("(t p) d -> p t d", p=P)
            for s in range(8):
                if s >= 4:
                    sp.wait_ge(wm_used, s - 3)
                q, half = s // 2, s % 2
                sp.dma_start(wm_ring[:, s % 4], wm_src[0][:, 2 * q:2 * q + 2, 1024 * half:1024 * half + 1024]).then_inc(wm_landed[s % 4], 16)
                if s == 3:
                    sp.dma_start(x[:, 0:4, :], xs).then_inc(x_landed, 16)
                    sp.dma_start(x[:, 4, :], A["x_prompt"][0]).then_inc(x_landed, 16)
                    for u in range(4):
                        sp.dma_start(raw_w[:, u, :], fc_src[:, :, fc_col(u):fc_col(u) + P]).then_inc(landed[u], 16)
            sp.wait_ge(mod_ready, 2)
            sp.dma_start(dft_g, A["dft_group"]).then_inc(dft_landed, 16)
            sp.dma_start(dft_l, A["dft_token"]).then_inc(dft_landed, 16)
            def mod_load(n, src, wait=True):
                if wait:
                    sp.wait_ge(acc_step, 4 * n)
                sp.dma_start(mod_w, src).then_inc(modw_landed, 16)
            sp.wait_ge(h_ready, KT)
            mod_load(0, wm_src[0][:, 0:2, 2048:3072], wait=False)
            for i in (0, 1, 2):
                for k in range(4):
                    sp.wait_ge(lo_ready, 4 * i + k + 1)
                    sp.dma_start(raw_w[:, k, :], fc_src[:, :, fc_col(4 * i + 4 + k):fc_col(4 * i + 4 + k) + P]).then_inc(landed[k], 16)
                mod_load(i + 1, wm_src[0][:, 2 * i + 2:2 * i + 4, 2048:3072])
            for k in range(4):
                sp.wait_ge(lo_ready, 12 + k + 1)
                sp.dma_start(raw_w[:, k, :], fc_src[:, :, fc_col(16 + k):fc_col(16 + k) + P]).then_inc(landed[k], 16)
            b_flat = A["b_mod"].rearrange("a n -> (a n)").rearrange("(o n) -> o n", o=1)
            for i in range(4):
                for p in range(8):
                    u = C0 + 8 * i + p + 4
                    sp.wait_ge(lo_ready, u - 3)
                    if u < OUT0:
                        src = fc_src[:, :, fc_col(u):fc_col(u) + P]
                        sp.dma_start(raw_w[:, u % 4, :], src).then_inc(landed[u % 4], 16)
                    else:
                        out_load(sp, 0, u - OUT0)
                    if p == 0:
                        if i == 0:
                            sp.wait_ge(ya_done, 8)
                        else:
                            sp.wait_ge(red_ready, i)
                        sp.dma_start(bias_row, b_flat[:, 2048 + 1024 * i:3072 + 1024 * i]).then_inc(bias_landed, 16)
                        if i < 3:
                            mod_load(4 * i + 4, wm_src[1][:, 0:2, 1024 * i:1024 * i + 1024])
                    if p in (1, 3, 5) and i < 3:
                        tp = p // 2 + 1
                        mod_load(4 * i + 4 + tp, wm_src[1][:, 2 * tp:2 * tp + 2, 1024 * i:1024 * i + 1024])
                    if p == 4:
                        sp.wait_ge(row_copied, i + 1)
                        sp.dma_start(mod_scr[i].rearrange("c n -> (c n)").rearrange("(o n) -> o n", o=1), mod_row).then_inc(row_stored, 16)
            sp.wait_ge(row_stored, 64)
            for c in range(2):
                sp.dma_start(gate[:, c, :], mod_scr[0, c].partition_broadcast(P)).then_inc(gate_landed, 16)
            sp.dma_start(praw3[0:32, :], mod_scr[1:3].rearrange("k c (j n) -> (k c j) n", n=P)).then_inc(p3_landed, 16)
            sp.wait_ge(yb_done, 8)
            sp.dma_start(x[:, 0:4, :], xs).then_inc(x_back, 16)
            sp.dma_start(x[:, 4, :], A["x_prompt"][0]).then_inc(x_back, 16)
            for v in range(4, N_OUT):
                sp.wait_ge(lo_ready, OUT0 + v - 3)
                out_load(sp, 0, v)
            if stage:
                table_sp(sp)
                for k in range(4):
                    sp.wait_ge(lo_ready, IN1 + k - 3)
                    ssd_load(sp, 0, k, k)
                sp.wait_ge(x_updated, 10)
                sp.dma_start(x1_scr[:, 0:4 * D], x[:, 0:4, :].rearrange("p t d -> p (t d)")).then_inc(y_stored[0], 16)
                sp.dma_start(x1_scr[:, 4 * D:5 * D], x[:, 4, :]).then_inc(y_stored[1], 16)
                for k in range(4, 6):
                    sp.wait_ge(lo_ready, IN1 + k - 3)
                    ssd_load(sp, 0, k, k % RING)
                sp.wait_ge(h_ready, 2 * KT)
                sp.wait_ge(y_stored[0], 16)
                table_sp2(sp)
                all_groups(sp, ssd_sp)
                sp.wait_ge(yt_done, 1 + 5 * G)
                sp.wait_ge(y_stored[0], 16 + 16 * 20)
                sp.wait_ge(y_stored[1], 16 + 16 * 20)
                sp.wait_ge(small_stored, 16 + 32 * G)
                for j in range(4):
                    sp.dma_start(yT[:, 4 * j:4 * j + 4, :], y_scr[:, 4 * j:4 * j + 4, :]).then_inc(y_back[j], 16)
                sp.dma_start(x[:, 0:4, :], x1_scr[:, 0:4 * D].rearrange("p (t d) -> p t d", d=D)).then_inc(x_back, 16)
                sp.dma_start(x[:, 4, :], x1_scr[:, 4 * D:5 * D]).then_inc(x_back, 16)
                for c in range(2):
                    sp.dma_start(gate[:, c, :], mod_scr[3, c].partition_broadcast(P)).then_inc(gate_landed, 16)
                sp.dma_start(fin_g, A["final_norm_g"].partition_broadcast(P)).then_inc(fg_landed, 16)
                for v in range(6, N_OUT):
                    sp.wait_ge(lo_ready, OUT1 + v - 3)
                    out_load(sp, 1, v)
                for t in range(NT):
                    sp.wait_ge(fin_done, t + 1)
                    dst = y_sample[0].rearrange("(t p) d -> p t d", p=P)[:, t, :] if t < 4 else y_prompt[0]
                    sp.dma_start(dst, x[:, t, :]).then_inc(stored, 16)
                sp.wait_ge(stored, 16 * NT)
            if stage == 0:
                sp.wait_ge(x_updated, 10)
                sp.dma_start(y_sample[0].rearrange("(t p) d -> p t d", p=P), x[:, 0:4, :]).then_inc(stored, 16)
                sp.dma_start(y_prompt[0], x[:, 4, :]).then_inc(stored, 16)
                sp.dma_start(new_state.rearrange("a b c h p n -> (a b c h p n)").rearrange("(p f) -> p f", p=P), yT[:, 0:8, :].rearrange("p a b -> p (a b)")[:, 0:4096]).then_inc(stored, 16)
                sp.wait_ge(stored, 48)

        @block.tensor
        def _(pe):
            start_pe(pe)
            norm_pe(pe, 0, xn)
            start_pe_mod_T(pe)
            fourier_pe(pe, 0, True)
            with pe.Fori(1, 4) as i:
                fourier_pe(pe, i, False)
            conv_pe(pe, 0, True, False)
            with pe.Fori(1, 4) as i:
                conv_pe(pe, i, False, False)
            pe.wait_ge(act_freed, 32)
            pe.wait_ge(dve_freed, 16)
            pe.wait_ge(row_copied, 4)
            out_pe(pe, 0)
            if stage:
                pe.wait_ge(p3_landed, 16)
                pe.wait_ge(out_evac, 4)
                pe.transpose(PS[:, 3, 0:32], praw3[0:32, :], ident[0:32, 0:32]).then_inc(mod_T, 1)
                norm_pe(pe, 1, xn1)
                table_pe(pe)
                all_groups(pe, ssd_pe)
                pe.wait_ge(proj_free, 9 * G)
                pe.wait_ge(yt_done, 1 + 5 * G)
                out_pe(pe, 1)

        @block.scalar
        def _(act):
            act.wait_ge(cond_landed, 32)
            act.activation(cond[:, :, :], cond[:, :, :], ACT.Silu).then_inc(cond_ready, 1)
            norm_act(act, 0, xn, xT0)
            for u in range(4):
                split_hi(act, u, u)
            act.wait_ge(wm_used, 8)
            act.activation(mod_sb[0:2, 0:1024], PSf[0:2, 0:1024], ACT.Copy).then_inc(mod_copied, 1)
            h_act(act, 0, xT0)
            fourier_act(act, 0, True)
            with act.Fori(1, 4) as i:
                fourier_act(act, i, False)
            conv_act(act, 0, True, False)
            with act.Fori(1, 4) as i:
                conv_act(act, i, False, False)
            out_act(act, 0)
            if stage:
                norm_act(act, 1, xn1, xT1)
                dt_weights_act(act)
                h_act(act, 1, xT1)
                table_act(act)
                all_groups(act, ssd_act)
                out_act(act, 1)
                for t in range(NT):
                    act.wait_ge(x_updated, 15 + t + 1)
                    if t >= 2:
                        act.wait_ge(sq_done, 10 + t - 1)
                    act.activation(sq_junk[:, t % 2, :], x[:, t, :], ACT.Square, accum_out=ssq[:, 10 + t:11 + t]).then_inc(sq_done, 1)

        @block.vector
        def _(dve):
            dve.memset(ones[:, :], 1.0).then_inc(ones_ready, 1)
            dve.wait_ge(par_T, 1)
            dve.tensor_scalar(par1[:, :], PS[:, 6, 0:P], 0.5, None, ALU.mult).then_inc(par_ready, 1)
            dve.tensor_copy(par2[:, :], PS[:, 6, P:P + 72]).then_inc(par_ready, 1)
            norm_dve(dve, 0, xn)
            for u in range(4):
                split_lo(dve, u, u)
            dve.wait_ge(wm_used, 8)
            dve.tensor_copy(mod_sb[0:2, 1024:2048], PSf[0:2, 1024:2048]).then_inc(mod_copied, 1)
            dve.wait_ge(mod_T, 1)
            dve.wait_ge(par_ready, 2)
            for k in range(2):
                dve.tensor_tensor(ss_mod[:, k].rearrange("p c j -> p j c"), PS[:, 4, 16 * k:16 * k + 16].rearrange("p (j c) -> p j c", c=2),
                                  par2[:, 56 + 8 * k:64 + 8 * k].unsqueeze(2).to_broadcast([P, KT, 2]), ALU.add).then_inc(mod_ready, 1)
            dve.wait_ge(mod_ready, 2)
            dve.scalar_tensor_tensor(out=ss_mod[:, 1], in0=ss_mod[:, 1], scalar=1.0,
                                     in1=par2[:, 0:8].unsqueeze(1).to_broadcast([P, 2, KT]), op0=ALU.add, op1=ALU.mult).then_inc(mod_step, 1)
            dve.wait_ge(mod_step, 1)
            h_dve(dve, 0, xT0)
            fourier_dve(dve, 0, True)
            with dve.Fori(1, 4) as i:
                fourier_dve(dve, i, False)
            conv_dve(dve, 0, True, False)
            with dve.Fori(1, 3) as i:
                conv_dve(dve, i, False, False)
            conv_dve(dve, 3, False, True)
            out_dve(dve, 0)
            if stage:
                dve.wait_ge(mod_T, 2)
                dve.tensor_copy(ss_mod[:, 0], PS[:, 3, 0:16].rearrange("p (c j) -> p c j", c=2)).then_inc(mod_ready, 1)
                dve.scalar_tensor_tensor(out=ss_mod[:, 1], in0=PS[:, 3, 16:32].rearrange("p (c j) -> p c j", c=2), scalar=1.0,
                                         in1=par2[:, 8:16].unsqueeze(1).to_broadcast([P, 2, KT]), op0=ALU.add, op1=ALU.mult).then_inc(mod_ready, 1)
                table_dve(dve)
                h_dve(dve, 1, xT1)
                table_dve2(dve)
                all_groups(dve, ssd_dve)
                out_dve(dve, 1)
                dve.wait_ge(fg_landed, 16)
                for t in range(NT):
                    dve.wait_ge(rstd_done, 10 + t + 1)
                    dve.scalar_tensor_tensor(out=x[:, t, :], in0=x[:, t, :], scalar=rstd[:, 10 + t:11 + t], in1=fin_g,
                                             op0=ALU.mult, op1=ALU.mult).then_inc(fin_done, 1)

        @block.gpsimd
        def _(pool):
            pool.memset(half_neg[:, :], -0.5).then_inc(exponent_ready, 1)
            pool.memset(eps_col[:, :], EPS).then_inc(exponent_ready, 1)
            pool.wait_ge(exponent_ready, 2)
            norm_pool(pool, 0)
            if stage:
                norm_pool(pool, 1)
                pool.wait_ge(tables_ready, 1)
                pool.wait_ge(tab_act, 6)
                groups_copy(pool, 0, None, 0, 0)
                groups_copy(pool, None, 0, 0, 0)
                groups_copy(pool, None, 1, 0, 1).then_inc(grp_done, 1)
                all_groups(pool, ssd_pool)
                norm_pool(pool, 2)


def constants():
    import numpy as np
    r = np.arange(P)
    tri = [np.eye(P), r[:, None] <= r[None, :], r[:, None] >= r[None, :]]
    consts = np.concatenate([np.asarray(t, np.float64) for t in tri], 1)
    k = np.arange(256)
    th = 2 * np.pi * ((k[:, None] * k[None, :]) % 256) / 256
    grp = np.concatenate([np.cos(th), np.sin(th)], 1) / 16
    grp = grp.reshape(2, P, 512).transpose(1, 0, 2)
    tok = []
    for f in (np.cos, lambda t: -np.sin(t)):
        for q in range(4):
            th = 2 * np.pi * ((r[:, None] * (4 * r[None, :] + q)) % LAT) / LAT
            tok.append(f(th) / np.sqrt(LAT))
    th = 2 * np.pi * ((r[:, None] * r[None, :]) % CTX) / CTX
    tok += [np.cos(th) / np.sqrt(CTX), -np.sin(th) / np.sqrt(CTX)]
    tok = np.stack(tok, 1)
    return {"consts": consts.astype(np.float32), "dft_group": grp.astype(np.float32), "dft_token": tok.astype(np.float32)}


_INS = ["x_prompt", "x_sample", "state_ssm", "c", "c_ctx", "w_mod", "b_mod", "norm_g", "fc_w_in", "fc_conv_w", "fc_w_out",
        "ssd_w_in", "ssd_conv_w", "ssd_conv_b", "ssd_dt_bias", "ssd_a_log", "ssd_d", "ssd_norm_g", "ssd_w_out", "final_norm_g"]
_OUTS = [(1, CTX, D), (1, LAT, D), (1, 1, 2, HEADS, 64, P)]
STAGE = 2


def kernel(**inputs):
    import numpy as _np
    import concourse.bacc as _bacc
    from concourse.bass_utils import run_bass_kernel_spmd as _run

    nc = _bacc.Bacc("TRN2", target_bir_lowering=False, num_devices=1)
    arrays, args = {}, {}
    given = {name: _np.ascontiguousarray(inputs[name]) for name in _INS}
    given.update(constants())
    for name, a in given.items():
        arrays[f"in_{name}_dram"] = a
        args[name] = nc.dram_tensor(f"in_{name}_dram", a.shape, mybir.dt.from_np(a.dtype), kind="ExternalInput").ap()
    outs = [nc.dram_tensor(f"out_{i}_dram", shape, F32, kind="ExternalOutput").ap() for i, shape in enumerate(_OUTS)]
    build_step(nc, args, outs, STAGE)
    r = _run(nc, [arrays], core_ids=[0])
    return tuple(r.results[0][f"out_{i}_dram"] for i in range(len(_OUTS)))
```

```python
from contextlib import ExitStack

import concourse.bass as bass
from concourse import mybir

F32 = mybir.dt.float32
F32R = mybir.dt.float32r
ALU = mybir.AluOpType
ACT = mybir.ActivationFunctionType

P = 128
D = 1024
KT = D // P
LAT, CTX = 512, 128
TOK = LAT + CTX
NT = TOK // P
SEGS = ((0, LAT), (LAT, TOK))
HALF = TOK // 2
FC_IN = 6 * D
UNIT = 1024
RING = 4
EPS = 1e-6
N_IN0 = 48
N_OUT = 16
OUT0 = N_IN0
IN1 = OUT0 + N_OUT
G = 8
UPG = 6
OUT1 = IN1 + G * UPG
UNITS = OUT1 + N_OUT
HEADS = 32
DI = 2048
SSD_IN = 6208


class Chain:

    def __init__(self, eng, sem, base=0):
        self.eng, self.sem, self.base, self.n = eng, sem, base, 0

    def tick(self, ins):
        self.n += 1
        ins.then_inc(self.sem, 1)

    def sync(self):
        self.eng.wait_ge(self.sem, self.base + self.n)


def fc_unit_src(fc_w_in, col):
    return fc_w_in[0].rearrange("(k p) n -> p k n", p=P)[:, :, bass.ds(col, P)]


def build_step(nc, A, outs, stage=2):
    y_prompt, y_sample, new_state = outs
    mod_scr = nc.dram_tensor("mod_scr", (4, 2, D), F32, kind="Internal").ap()
    x1_scr = nc.dram_tensor("x1_scr", (P, NT * D), F32, kind="Internal").ap()

    l_scr = nc.dram_tensor("l_scr", (64, TOK), F32, kind="Internal").ap()
    y_scr = nc.dram_tensor("y_scr", (P, 16, TOK), F32, kind="Internal").ap()

    ssd_src = A["ssd_w_in"][0].rearrange("(k p) n -> p k n", p=P)
    fc_src = A["fc_w_in"][0].rearrange("(k p) n -> p k n", p=P)
    wm_src = [A["w_mod"][l].rearrange("(p t) n -> p t n", t=KT) for l in range(2)]
    wout_src = [A[n][0].rearrange("(k p) n -> p k n", p=P) for n in ("fc_w_out", "ssd_w_out")]

    ctx = ExitStack()
    with ctx:
        def sb(name, shape, dt=F32):
            return ctx.enter_context(nc.sbuf_tensor(name, shape, dt))

        def sem(name):
            return ctx.enter_context(nc.semaphore(name))

        PS = ctx.enter_context(nc.psum_tensor("PS", [P, 8, 512], F32))
        PSf = PS[:, :, :].rearrange("p b n -> p (b n)")
        raw_w = sb("raw_w", [P, RING, UNIT])
        w_hi = sb("w_hi", [P, RING, UNIT], F32R)
        w_lo = sb("w_lo", [P, RING, UNIT], F32R)
        h_hi = sb("h_hi", [P, KT, TOK], F32R)
        h_lo = sb("h_lo", [P, KT, TOK], F32R)
        y_hi = sb("y_hi", [P, 2, TOK], F32R)
        y_lo = sb("y_lo", [P, 2, TOK], F32R)
        cst = sb("cst", [P, 3 * P])
        ident, upper, lower = cst[:, 0:P], cst[:, P:2 * P], cst[:, 2 * P:3 * P]
        ones = sb("ones", [P, P])
        cond = sb("cond", [P, 2, KT])
        par1 = sb("par1", [P, P])
        par2 = sb("par2", [P, 72])
        ss_mod = sb("ss_mod", [P, 2, 2, KT])
        ssq = sb("ssq", [P, 16])
        rstd = sb("rstd", [P, 16])
        half_neg = sb("half_neg", [P, 1])
        eps_col = sb("eps_col", [P, 1])
        NBIG = 26700 - 200
        big = sb("big", [P, NBIG])

        def carve(off, *dims):
            n = 1
            for d in dims:
                n *= d
            assert off + n <= NBIG, (off, dims)
            v = big[:, off:off + n]
            if len(dims) == 2:
                return v.rearrange("p (a b) -> p a b", a=dims[0])
            if len(dims) == 3:
                return v.rearrange("p (a b c) -> p a b c", a=dims[0], b=dims[1])
            if len(dims) == 4:
                return v.rearrange("p (a b c d) -> p a b c d", a=dims[0], b=dims[1], c=dims[2])
            return v

        x = carve(0, NT, D)
        yT = carve(5120, 16, TOK)
        mod_w = carve(15360, 2, D)
        acc = carve(17408, 2, D)
        gate = carve(19456, 2, D)
        wm_ring = carve(5120, 4, 2, 1024)
        xn = carve(5120 + 8192, 2, D)
        xT0 = carve(15360, KT, TOK)
        mod_sb = carve(21504, 2 * D)
        praw = carve(21504 + 2048, 2, P)
        praw3 = carve(23808, P)
        dft_g = carve(21504, 2, 512)
        dft_l = carve(22528, 10, P)
        sz_a = carve(23808, 2, TOK)
        ut = carve(5120 + 8 * TOK, 2, TOK)
        ub = carve(5120 + 8 * TOK + 1280, 2, 512)
        ab = carve(5120 + 8 * TOK + 2304, 5, 512)
        d02_sb = carve(0, 512)
        e01 = carve(512, 2, 256)
        cv_c = carve(0, 2, TOK)
        cv = carve(1280, 2, TOK)
        cc = carve(2560, 2, TOK)
        sz_b = carve(3840, 2, TOK)
        mod_row = carve(21504, 2 * D)[0:1]
        bias_rows = carve(20480, D)
        xn1 = carve(5120, 2, D)
        xT1 = carve(5120 + 2048, KT, TOK)
        gtmp = carve(25100, 2, 512)

        fin_g = carve(17408, D)
        sq_junk = carve(15360, 2, D)
        dtw_raw = carve(24000, KT, 64)

        at = [0]

        def take(*dims):
            n = 1
            for d in dims:
                n *= d
            v = carve(at[0], *dims)
            at[0] += n
            return v

        cvx = take(3, TOK)
        cvC = take(2, TOK)
        th = take(TOK)
        zth = take(2, 256)
        xb = take(NT, 384)
        sz = take(NT, 256)
        lfb = take(2, 8, P)
        cbm = take(2, NT, P)
        ea = take(2, 4, P)
        gm = take(2, 2, 4, P)
        xdt = take(2, 512)
        xws = take(4, 512)
        hs = take(4, 512)
        hd = take(512)
        h0r = take(4, P)
        nst = take(512)
        yo = take(512)
        uu = take(2, 256)
        aa = take(2, 256)
        yn = take(2, 256)
        ysb = take(2, 2, P)
        GTW = 206
        GT = take(G, GTW)
        CPG = take(G, 16)
        gt = take(2, GTW)
        cp = take(2, 16)
        ssy = take(2)
        ry = take(2)
        tX, tNX, tNA, tU, tW, tLW, tC, tDT, tDA, tL = (carve(12400 + 320 * k, NT, 64) for k in range(10))
        tT = carve(12400 + 3200, NT, 64)
        lrow = carve(12400 + 3520, TOK)
        b_in, a_in, b_pm, a_pm = (carve(12400 + 4160 + 64 * k, 64) for k in range(4))
        d_in = carve(12400 + 4416, HEADS)

        landed = [sem(f"landed{i}") for i in range(RING)]
        hi_ready, lo_ready, unit_used = sem("hi_ready"), sem("lo_ready"), sem("unit_used")
        act_freed, dve_freed = sem("act_freed"), sem("dve_freed")
        cond_landed, x_landed, par_landed = sem("cond_landed"), sem("x_landed"), sem("par_landed")
        wm_landed = [sem(f"wm_landed{i}") for i in range(4)]
        wm_used, mod_mm, mod_copied, mod_T, mod_ready = sem("wm_used"), sem("mod_mm"), sem("mod_copied"), sem("mod_T"), sem("mod_ready")
        cond_ready, ones_ready, par_T, par_ready = sem("cond_ready"), sem("ones_ready"), sem("par_T"), sem("par_ready")
        sq_done, ms_done, rstd_done, xn_done = sem("sq_done"), sem("ms_done"), sem("rstd_done"), sem("xn_done")
        xt_ready, xt_done, v_done, hh_done, h_ready = sem("xt_ready"), sem("xt_done"), sem("v_done"), sem("hh_done"), sem("h_ready")
        fdone, ub_ready, gd_ready, q_ready, ab_act, ab_dve = sem("fdone"), sem("ub_ready"), sem("gd_ready"), sem("q_ready"), sem("ab_act"), sem("ab_dve")
        ld_ready, ya_done, dft_landed = sem("ld_ready"), sem("ya_done"), sem("dft_landed")
        conv_step, yb_done = sem("conv_step"), sem("yb_done")
        modw_landed, modw_used, acc_step, red_ready, row_copied, row_stored, bias_landed = (
            sem("modw_landed"), sem("modw_used"), sem("acc_step"), sem("red_ready"), sem("row_copied"), sem("row_stored"), sem("bias_landed"))
        bias_zeroed = sem("bias_zeroed")
        x_back, gate_landed = sem("x_back"), sem("gate_landed")
        yh_done, yl_done, y_even_used = sem("yh_done"), sem("yl_done"), sem("y_even_used")
        out_ready, out_evac, x_updated = sem("out_ready"), sem("out_evac"), sem("x_updated")
        p3_landed, stored = sem("p3_landed"), sem("stored")
        mod_step = sem("mod_step")
        exponent_ready = sem("exponent_ready")
        cpg_ready, cp0_ready, dt_rows = sem("cpg_ready"), sem("cp0_ready"), sem("dt_rows")
        (dtw_landed, tot_copied, bc_landed, dtw_hi, dtw_lo, dtp_ready, cum_ready, lt_ready, tab_dve, tab_act, tables_ready) = (sem(n) for n in (
            "dtw_landed", "tot_copied", "bc_landed", "dtw_hi", "dtw_lo", "dtp_ready", "cum_ready", "lt_ready", "tab_dve", "tab_act", "tables_ready"))
        (proj_free, z_ready, zth_done, cen_done, tap_step, th_done, conv_done, grp_done) = (sem(n) for n in (
            "proj_free", "z_ready", "zth_done", "cen_done", "tap_step", "th_done", "conv_done", "grp_done"))
        (tr_ready, tok_done, h0_landed, h_T, hs0_done, cb_ready, cbm_done, xw_done, st_ready, st_done, hd_done) = (sem(n) for n in (
            "tr_ready", "tok_done", "h0_landed", "h_T", "hs0_done", "cb_ready", "cbm_done", "xw_done", "st_ready", "st_done", "hd_done"))
        (sc_ready, sc_done, small_stored, m_done, exp_done, g_done, y_ready, t_done, pool_step, u_done, a_step, gz_done) = (sem(n) for n in (
            "sc_ready", "sc_done", "small_stored", "m_done", "exp_done", "g_done", "y_ready", "t_done", "pool_step", "u_done", "a_step", "gz_done"))
        (sqy_done, msy_done, ry_done, yn_done, ytr_ready, yt_done, fg_landed, fin_done) = (sem(n) for n in (
            "sqy_done", "msy_done", "ry_done", "yn_done", "ytr_ready", "yt_done", "fg_landed", "fin_done"))
        y_stored = [sem(f"y_stored{i}") for i in range(2)]
        lfb_landed = [sem(f"lfb_landed{i}") for i in range(2)]

        LAST_UNIT = IN1 if stage == 0 else UNITS
        block = ctx.enter_context(nc.Block())

        def split_hi(act, u, slot):
            act.wait_ge(landed[slot], 16 * (u // RING + 1) if isinstance(u, int) else u[1])
            un = u if isinstance(u, int) else u[0]
            if not isinstance(u, int) or u >= RING:
                act.wait_ge(unit_used, un - (RING - 1))
            act.activation(w_hi[:, slot, :], raw_w[:, slot, :], ACT.Copy).then_inc(hi_ready, 1)

        def split_lo(dve, u, slot):
            un = u if isinstance(u, int) else u[0]
            dve.wait_ge(hi_ready, un + 1)
            dve.tensor_tensor(w_lo[:, slot, :], raw_w[:, slot, :], w_hi[:, slot, :].bitcast(F32),
                              ALU.subtract).then_inc(lo_ready, 1)

        def unit(base, it, per, k):
            assert (base + k) % 1 == 0 and per % RING == 0
            if isinstance(it, int):
                return base + per * it + k
            return (per * it + (base + k), 4 * per * it + 16 * ((base + k) // RING + 1))

        def pair_view(pair):
            return PS[:, 2 * pair:2 * pair + 2, 0:HALF]

        def halves(v):
            return v.rearrange("p (s n) -> p s n", s=2)

        def channel_tile(pe, slot, pair, h_base=None):
            for kt in range(KT):
                if h_base is not None:
                    pe.wait_ge(h_ready, h_base + kt + 1)
                ws = slice(kt * P, (kt + 1) * P)
                for n, (w, h) in enumerate(((w_hi, h_hi), (w_hi, h_lo), (w_lo, h_hi))):
                    for s in range(2):
                        mm = pe.matmul(PS[:, 2 * pair + s, 0:HALF], w[:, slot, ws], h[:, kt, s * HALF:(s + 1) * HALF],
                                       start=(kt == 0 and n == 0), stop=(kt == KT - 1 and n == 2))
            mm.then_inc(unit_used, 1)

        def norm_act(act, layer, xnb, xTb):
            for t in range(NT + 1):
                if t < NT:
                    n = NT * layer + t
                    if layer == 0:
                        act.wait_ge(x_landed, 32)
                    else:
                        act.wait_ge(x_updated, NT * 2 * (layer - 1) + NT + t + 1)
                    if t >= 2:
                        act.wait_ge(xt_ready, n - 1)
                    act.activation(xnb[:, t % 2, :], x[:, t, :], ACT.Square,
                                   accum_out=ssq[:, n:n + 1]).then_inc(sq_done, 1)
                if t >= 1:
                    m = NT * layer + t - 1
                    act.wait_ge(xt_ready, m + 1)
                    b = 4 + 2 * ((t - 1) % 2)
                    act.activation(xTb[:, :, (t - 1) * P:t * P],
                                   PS[:, b:b + 2, :].rearrange("p b (k n) -> p (b k) n", n=P),
                                   ACT.Copy).then_inc(xt_done, 1)

        def norm_pool(pool, layer):
            for t in range(NT):
                n = NT * layer + t
                pool.wait_ge(sq_done, n + 1)
                pool.tensor_scalar(rstd[:, n:n + 1], ssq[:, n:n + 1], 1.0 / D, EPS, ALU.mult, ALU.add).then_inc(ms_done, 1)
                pool.wait_ge(ms_done, n + 1)
                pool.tensor_tensor(rstd[:, n:n + 1], rstd[:, n:n + 1], half_neg[:, :], ALU.pow).then_inc(rstd_done, 1)

        def norm_dve(dve, layer, xnb):
            for t in range(NT):
                norm_dve_tile(dve, layer, xnb, t)

        def norm_dve_tile(dve, layer, xnb, t):
                n = NT * layer + t
                dve.wait_ge(rstd_done, n + 1)
                if t >= 2:
                    dve.wait_ge(xt_ready, n - 1)
                dve.tensor_scalar(xnb[:, t % 2, :], x[:, t, :], rstd[:, n:n + 1], None, ALU.mult).then_inc(xn_done, 1)

        def norm_pe(pe, layer, xnb):
            for t in range(NT):
                n = NT * layer + t
                pe.wait_ge(xn_done, n + 1)
                if t >= 2:
                    pe.wait_ge(xt_done, n - 1)
                if t == 1 and layer == 1:
                    pe.wait_ge(out_evac, 8)
                if t == 1 and layer == 0:
                    pe.wait_ge(par_ready, 2)
                b = 4 + 2 * (t % 2)
                for k in range(KT):
                    mm = pe.transpose(PS[:, b + k // 4, (k % 4) * P:(k % 4 + 1) * P], xnb[:, t % 2, k * P:(k + 1) * P], ident)
                mm.then_inc(xt_ready, 1)

        def h_dve(dve, layer, xTb):
            dve.wait_ge(xt_done, NT * (layer + 1))
            dve.wait_ge(mod_ready, 2 * (layer + 1))
            for k in range(KT + 1):
                if k < KT:
                    for c, (a, b) in enumerate(SEGS):
                        dve.tensor_scalar(xTb[:, k, a:b], xTb[:, k, a:b], ss_mod[:, 1, c, k:k + 1], ss_mod[:, 0, c, k:k + 1],
                                          ALU.mult, ALU.add).then_inc(v_done, 1)
                if k >= 1:
                    dve.wait_ge(hh_done, KT * layer + k)
                    dve.tensor_tensor(h_lo[:, k - 1, :], xTb[:, k - 1, :], h_hi[:, k - 1, :].bitcast(F32),
                                      ALU.subtract).then_inc(h_ready, 1)

        def h_act(act, layer, xTb):
            for k in range(KT):
                act.wait_ge(v_done, 2 * (KT * layer + k + 1))
                act.activation(h_hi[:, k, :], xTb[:, k, :], ACT.Copy).then_inc(hh_done, 1)

        RING_STEPS = (list(range(32)), list(range(8, 16)) + list(range(24, 32)))

        def y_ready_wait(eng, layer, kt):
            if layer == 0:
                if kt < 8:
                    eng.wait_ge(ya_done, kt + 1)
                else:
                    eng.wait_ge(yb_done, kt - 7)
            else:
                eng.wait_ge(y_back[4 if kt < 12 else 5 if kt < 14 else 6], 16)

        def out_ring_wait(eng, layer, q):
            r = RING_STEPS[layer].index(q)
            if r < 2:
                return
            last = RING_STEPS[layer][r - 2]
            if last % 2 == 0:
                eng.wait_ge(y_even_used, 16 * layer + last // 2 + 1)
            else:
                eng.wait_ge(unit_used, (OUT0, OUT1)[layer] + last // 2 + 1)

        def out_units(eng, split, layer, q):
            u0 = (OUT0, OUT1)[layer]
            if layer == 1 and q < 10:
                for v in (2 * (q - 8), 2 * (q - 8) + 1):
                    out_next_unit(eng, split, u0 + v)
            elif q % 2 == 0 and q:
                out_next_unit(eng, split, u0 + q // 2 - 1)

        def out_act(act, layer):
            for q in range(8 * layer, 32):
                if q in RING_STEPS[layer]:
                    if q < 16:
                        y_ready_wait(act, layer, q)
                    out_ring_wait(act, layer, q)
                    act.activation(y_hi[:, q % 2, :], yT[:, q % 16, :], ACT.Copy).then_inc(yh_done, 1)
                out_units(act, split_hi, layer, q)
            out_next_unit(act, split_hi, (OUT0, OUT1)[layer] + 15)

        def out_next_unit(eng, split, u):
            if u + RING < LAST_UNIT:
                split(eng, u + RING, u % RING)

        def residual(dve, layer, hh, t):
            u0 = (OUT0, OUT1)[layer]
            if hh == 0 and t == 0:
                dve.wait_ge(x_back, 32 * (layer + 1))
                dve.wait_ge(gate_landed, 32 * (layer + 1))
            if t < NT - 1:
                dve.wait_ge(out_ready, 8 * layer + 4 * hh + t + 1)
            else:
                dve.wait_ge(unit_used, u0 + 8 * (hh + 1))
            n = 10 * layer + 5 * hh + t
            if n >= 2:
                dve.wait_ge(x_updated, n - 1)
            dve.tensor_tensor(gtmp[:, t % 2, :], PS[:, (5 * hh + t) % 8, :], gate[:, int(t == NT - 1), 512 * hh:512 * hh + 512],
                              ALU.mult).then_inc(out_evac, 1)
            dve.wait_ge(out_evac, 10 * layer + 5 * hh + t + 1)
            xs = x[:, t, 512 * hh:512 * hh + 512]
            dve.tensor_tensor(xs, xs, gtmp[:, t % 2, :], ALU.add).then_inc(x_updated, 1)

        def out_dve(dve, layer):
            u0 = (OUT0, OUT1)[layer]
            for q in range(8 * layer, 32):
                if q in RING_STEPS[layer]:
                    dve.wait_ge(yh_done, 32 * layer + RING_STEPS[layer].index(q) + 1)
                    dve.tensor_tensor(y_lo[:, q % 2, :], yT[:, q % 16, :], y_hi[:, q % 2, :].bitcast(F32),
                                      ALU.subtract).then_inc(yl_done, 1)
                out_units(dve, split_lo, layer, q)
                if q == 16:
                    residual(dve, layer, 0, 0)
                    residual(dve, layer, 0, 1)
                if 17 <= q < 20:
                    residual(dve, layer, 0, q - 15)
            out_next_unit(dve, split_lo, u0 + 15)
            for t in range(NT + 2):
                if t < NT:
                    residual(dve, layer, 1, t)
                if t >= 2 and layer == 0 and stage:
                    norm_dve_tile(dve, 1, xn1, t - 2)

        def out_tile(pe, layer, q, t):
            hh, kt, u = q // 16, q % 16, (OUT0, OUT1)[layer] + q // 2
            ys = [v[:, kt] for v in (h_hi, h_lo)] if layer == 1 and kt < 8 else [v[:, q % 2] for v in (y_hi, y_lo)]
            for n, (y, w) in enumerate(((ys[0], w_hi), (ys[0], w_lo), (ys[1], w_hi))):
                mm = pe.matmul(PS[:, (5 * hh + t) % 8, :], y[:, t * P:(t + 1) * P],
                               w[:, u % RING, (kt % 2) * 512:(kt % 2) * 512 + 512],
                               start=(kt == 0 and n == 0), stop=(kt == 15 and n == 2))
            return mm

        def out_pe(pe, layer):
            u0 = (OUT0, OUT1)[layer]
            for q in range(32):
                hh, kt = q // 16, q % 16
                if layer == 1 and q < 8:
                    out_tile(pe, 1, q, 4).then_inc(unit_used if kt % 2 else y_even_used, 1)
                    continue
                if kt % 2 == 0:
                    pe.wait_ge(lo_ready, u0 + q // 2 + 1)
                if q in RING_STEPS[layer]:
                    pe.wait_ge(yl_done, 32 * layer + RING_STEPS[layer].index(q) + 1)
                for t in range(NT):
                    if hh == 1 and kt == 0 and t >= 3:
                        pe.wait_ge(out_evac, 10 * layer + t - 2)
                    mm = out_tile(pe, layer, q, t)
                    if kt == 15 and t < NT - 1:
                        mm.then_inc(out_ready, 1)
                mm.then_inc(unit_used if kt % 2 else y_even_used, 1)

        def early_sp(sp, j):
            if j == 0:
                sp.wait_ge(unit_used, OUT1)
                for r in range(2):
                    sp.wait_ge(y_stored[r], 16 + 16 * 10)
            sp.dma_start(h_lo[:, 2 * j:2 * j + 2, :].bitcast(F32), y_scr[:, 2 * j:2 * j + 2, :]).then_inc(y_back[j], 16)

        def early_act(act, k):
            act.wait_ge(y_back[k // 2], 16)
            act.activation(h_hi[:, k, :], h_lo[:, k, :].bitcast(F32), ACT.Copy).then_inc(eh_done, 1)

        def early_dve(dve, k):
            dve.wait_ge(eh_done, k + 1)
            dve.tensor_tensor(h_lo[:, k, :], h_lo[:, k, :].bitcast(F32), h_hi[:, k, :].bitcast(F32), ALU.subtract).then_inc(el_done, 1)

        def early_pe(pe, k):
            if k == 0:
                pe.wait_ge(proj_free, 9 * G)
            if k % 2 == 0:
                pe.wait_ge(lo_ready, OUT1 + k // 2 + 1)
            pe.wait_ge(el_done, k + 1)
            for t in range(4):
                out_tile(pe, 1, k, t)

        y_back = [sem(f"y_back{i}") for i in range(7)]
        eh_done, el_done = sem("eh_done"), sem("el_done")

        def start_pe(pe):
            pe.wait_ge(par_landed, 16 * PAR_DMAS)
            pe.transpose(PS[:, 6, 0:P], praw[:, 0, :], ident)
            pe.transpose(PS[:, 6, P:P + 72], praw[0:72, 1, :], ident[0:72, 0:72]).then_inc(par_T, 1)
            pe.wait_ge(cond_ready, 1)
            for s in range(8):
                q, half = s // 2, s % 2
                pe.wait_ge(wm_landed[s % 4], 16 * (s // 4 + 1))
                for t in range(2):
                    for b in range(2):
                        mm = pe.matmul(PS[0:2, 2 * half + b, :], cond[:, :, 2 * q + t], wm_ring[:, s % 4, t, 512 * b:512 * b + 512],
                                       start=(q == 0 and t == 0), stop=(q == 3 and t == 1))
                mm.then_inc(wm_used, 1)

        def start_pe_mod_T(pe):
            pe.wait_ge(mod_copied, 2)
            pe.wait_ge(xt_done, NT)
            for j in range(16):
                mm = pe.transpose(PS[:, 4, 2 * j:2 * j + 2], mod_sb[0:2, j * P:(j + 1) * P], ident[0:2, 0:2])
            mm.then_inc(mod_T, 1)

        def fourier_pe(pe, i, first):
            for k in range(4):
                pe.wait_ge(lo_ready, 4 * i + k + 1)
                if not (first and k < 2):
                    pe.wait_ge(act_freed, 4 * i + k - 1)
                channel_tile(pe, k, k % 2, 0 if first and k == 0 else None)
            pe.wait_ge(ub_ready, 2 * i + 2)
            if first:
                pe.wait_ge(dft_landed, 32)
            else:
                pe.wait_ge(ya_done, 2 * i)
            for b, src in enumerate((2, 3, 0, 1, None)):
                if b == 4:
                    pe.wait_ge(q_ready, i + 1)
                for kt in range(2):
                    lhs = ut[:, kt, LAT:TOK] if src is None else ub[:, kt, src * P:(src + 1) * P]
                    mm = pe.matmul(PS[:, 4 + b % 4, :], lhs, dft_g[:, kt, :], start=(kt == 0), stop=(kt == 1))
                mm.then_inc(gd_ready, 1)
            pe.wait_ge(ab_act, 3 * i + 3)
            pe.wait_ge(ab_dve, i + 1)
            for kt in range(2):
                for r in range(5):
                    o = PS[:, (5, 7)[kt], r * P:(r + 1) * P] if r < 4 else PS[:, (6, 4)[kt], 0:P]
                    cs, sn = (r, 4 + r) if r < 4 else (8, 9)
                    pe.matmul(o, ab[:, r, kt * P:(kt + 1) * P], dft_l[:, cs, :], start=True, stop=False)
                    mm = pe.matmul(o, ab[:, r, 256 + kt * P:256 + (kt + 1) * P], dft_l[:, sn, :], start=False, stop=True)
                mm.then_inc(ld_ready, 1)

        def fourier_act(act, i, first):
            for k in range(4):
                act.wait_ge(unit_used, 4 * i + k + 1)
                src = pair_view(k % 2)
                if k < 2:
                    if not first:
                        act.wait_ge(gd_ready, 5 * i)
                    act.activation(halves(ut[:, k, :]), src, ACT.Copy).then_inc(act_freed, 1)
                else:
                    if not first:
                        act.wait_ge(ya_done, 2 * i)
                    act.activation(halves(sz_a[:, k - 2, :]), src, ACT.Silu).then_inc(act_freed, 1)
                split_hi(act, unit(RING, i, 4, k), k)
            act.wait_ge(gd_ready, 5 * i + 1)
            if not first:
                act.wait_ge(ab_dve, i)
            act.activation(d02_sb, PS[:, 4, :], ACT.Copy).then_inc(q_ready, 1)
            if not first:
                act.wait_ge(ld_ready, 2 * i)
            for b, r in ((2, 0), (3, 2), (4, 4)):
                act.wait_ge(gd_ready, 5 * i + b + 1)
                act.activation(ab[:, r, :], PS[:, 4 + b % 4, :], ACT.Copy).then_inc(ab_act, 1)

        def fourier_dve(dve, i, first):
            ch = Chain(dve, fdone, 4 * i)
            for k in range(4):
                if k < 2:
                    dve.wait_ge(act_freed, 4 * i + k + 1)
                    if not first:
                        dve.wait_ge(gd_ready, 5 * i)
                        if k == 0:
                            dve.wait_ge(ub_ready, 2 * i)
                    lo2, hi2 = ut[:, k, 0:256], ut[:, k, 256:512]
                    ch.tick(dve.tensor_tensor(e01[:, k, :], lo2, hi2, ALU.add))
                    ch.tick(dve.tensor_tensor(ub[:, k, 256:512], lo2, hi2, ALU.subtract))
                    ch.sync()
                    dve.tensor_tensor(ub[:, k, 128:256], e01[:, k, 0:P], e01[:, k, P:256], ALU.subtract)
                    dve.tensor_tensor(ub[:, k, 0:P], e01[:, k, 0:P], e01[:, k, P:256], ALU.add).then_inc(ub_ready, 1)
                split_lo(dve, unit(RING, i, 4, k), k)
                if k == 2:
                    if first:
                        dve.wait_ge(bias_landed, 16)
                    mod_slot_dve(dve, i, i, first)
            dve.wait_ge(q_ready, i + 1)
            dve.wait_ge(gd_ready, 5 * i + 2)
            if not first:
                dve.wait_ge(ld_ready, 2 * i)
            C, S = slice(0, 256), slice(256, 512)
            dve.tensor_tensor(ab[:, 1, C], d02_sb[:, C], PS[:, 5, S], ALU.subtract)
            dve.tensor_tensor(ab[:, 1, S], d02_sb[:, S], PS[:, 5, C], ALU.add)
            dve.tensor_tensor(ab[:, 3, C], d02_sb[:, C], PS[:, 5, S], ALU.add)
            dve.tensor_tensor(ab[:, 3, S], d02_sb[:, S], PS[:, 5, C], ALU.subtract).then_inc(ab_dve, 1)
            for kt in range(2):
                dve.wait_ge(ld_ready, 2 * i + kt + 1)
                dve.wait_ge(act_freed, 4 * i + 4)
                yt = yT[:, bass.ds(2 * i + kt, 1), :]
                dve.tensor_tensor(yt[:, 0, 0:LAT].rearrange("p (m r) -> p r m", r=4),
                                  PS[:, (5, 7)[kt], :].rearrange("p (r m) -> p r m", r=4),
                                  sz_a[:, kt, 0:LAT].rearrange("p (m r) -> p r m", r=4), ALU.mult)
                dve.tensor_tensor(yt[:, 0, LAT:TOK], PS[:, (6, 4)[kt], 0:P], sz_a[:, kt, LAT:TOK], ALU.mult).then_inc(ya_done, 1)

        def mod_slot_dve(dve, n, tp, start):
            ch = Chain(dve, acc_step, 4 * n)
            if not start:
                ch.sync()
            dve.wait_ge(modw_landed, 16 * n + 16)
            for t in range(2):
                if t:
                    ch.sync()
                for c in range(2):
                    ch.tick(dve.scalar_tensor_tensor(out=acc[:, c, :], in0=mod_w[:, t, :],
                                                     scalar=cond[:, c, (bass.ds(2 * tp + t, 1) if not isinstance(tp, int) else slice(2 * tp + t, 2 * tp + t + 1))],
                                                     in1=bias_rows if start and t == 0 else acc[:, c, :],
                                                     op0=ALU.mult, op1=ALU.add))

        def mod_reduce_pe(pe, i, first):
            pe.wait_ge(acc_step, 16 * i + 16)
            if first:
                pe.wait_ge(ya_done, 8)
            else:
                pe.wait_ge(row_copied, i)
            for c in range(2):
                for b in range(2):
                    mm = pe.matmul(PS[0:1, 4 + 2 * c + b, :], ones[:, 0:1], acc[:, c, 512 * b:512 * b + 512], start=True, stop=True)
            mm.then_inc(red_ready, 1)

        def mod_pool(pool):
            pool.memset(bias_rows, 0.0).then_inc(bias_zeroed, 1)
            pool.wait_ge(bias_zeroed, 1)
            b_flat = A["b_mod"].rearrange("a n -> (a n)").rearrange("(o n) -> o n", o=1)

            def bias_load(chunk):
                pool.dma_start(bias_rows[0:1, :], b_flat[:, 2048 + 1024 * chunk:3072 + 1024 * chunk]).then_inc(bias_landed, 16)

            def row_store(chunk):
                pool.wait_ge(row_copied, chunk + 1)
                pool.dma_start(mod_scr[chunk].rearrange("c n -> (c n)").rearrange("(o n) -> o n", o=1), mod_row).then_inc(row_stored, 16)
            bias_load(0)
            for n in range(16):
                chunk, tp = n // 4, n % 4
                if n == 0:
                    pool.wait_ge(h_ready, KT)
                else:
                    pool.wait_ge(acc_step, 4 * n)
                src = wm_src[0][:, :, 2048:3072] if chunk == 0 else wm_src[1][:, :, 1024 * (chunk - 1):1024 * chunk]
                pool.dma_start(mod_w, src[:, 2 * tp:2 * tp + 2, :]).then_inc(modw_landed, 16)
                if tp == 1 and chunk:
                    row_store(chunk - 1)
                if tp == 1 and chunk < 3:
                    bias_load(chunk + 1)
            row_store(3)

        CONV_DVE = 10
        MOD_SLOTS = (2, 4, 6, 7)
        C0 = 16

        def conv_pe(pe, i, first, last):
            for p in range(8):
                pe.wait_ge(lo_ready, C0 + 8 * i + p + 1)
                if p < 4:
                    pe.wait_ge(act_freed, C0 + 4 * i - 1 + p)
                else:
                    pe.wait_ge(dve_freed, 4 * i + p - 3)
                channel_tile(pe, p % 4, p % 2)
                if p == 1:
                    mod_reduce_pe(pe, i, first)

        def conv_act(act, i, first, last):
            for p in range(8):
                act.wait_ge(unit_used, C0 + 8 * i + p + 1)
                src = pair_view(p % 2)
                j = p % 2
                if p < 2:
                    if first:
                        act.wait_ge(ya_done, 8)
                    else:
                        act.wait_ge(dve_freed, 4 * i - 3 + j)
                    act.activation(halves(cv_c[:, j, :]), src, ACT.Copy).then_inc(act_freed, 1)
                if p == 3:
                    act.wait_ge(red_ready, i + 1)
                    if not first:
                        act.wait_ge(row_stored, 16 * i)
                    act.activation(mod_row, PSf[0:1, 2048:4096], ACT.Copy).then_inc(row_copied, 1)
                if p >= 6:
                    if not first:
                        act.wait_ge(yb_done, 2 * i)
                    act.activation(halves(sz_b[:, j, :]), src, ACT.Silu).then_inc(act_freed, 1)
                split_hi(act, unit(C0 + RING, i, 8, p), p % 4)

        def conv_dve(dve, i, first, last):
            ch = Chain(dve, conv_step, CONV_DVE * i)
            for p in range(8):
                j = p % 2
                src = pair_view(p % 2)

                def tap(k):
                    return par2[:, bass.ds(2 * i + (16 + 8 * k + j), 1)]
                rows = [b[:, j, :].rearrange("p (r n) -> p r n", n=64) for b in (cv, cc)]
                if p in (2, 3):
                    dve.wait_ge(unit_used, C0 + 8 * i + p + 1)
                    dve.wait_ge(act_freed, C0 + 4 * i + j + 1)
                    dve.tensor_tensor(halves(cv[:, j, :]), src, halves(cv_c[:, j, :]), ALU.mult).then_inc(dve_freed, 1)
                    dve.wait_ge(dve_freed, 4 * i + j + 1)
                    ch.tick(dve.tensor_scalar(cc[:, j, :], cv[:, j, :], tap(1), None, ALU.mult))
                    ch.sync()
                    ch.tick(dve.scalar_tensor_tensor(out=rows[1][:, :, 1:64], in0=rows[0][:, :, 0:63], scalar=tap(0),
                                                     in1=rows[1][:, :, 1:64], op0=ALU.mult, op1=ALU.add))
                    ch.sync()
                    ch.tick(dve.scalar_tensor_tensor(out=rows[1][:, :, 0:63], in0=rows[0][:, :, 1:64], scalar=tap(2),
                                                     in1=rows[1][:, :, 0:63], op0=ALU.mult, op1=ALU.add))
                    ch.sync()
                    a, b = LAT + 63, LAT + 64
                    ch.tick(dve.scalar_tensor_tensor(out=cc[:, j, b:b + 1], in0=cv[:, j, a:a + 1], scalar=tap(0),
                                                     in1=cc[:, j, b:b + 1], op0=ALU.mult, op1=ALU.add))
                    ch.tick(dve.scalar_tensor_tensor(out=cc[:, j, a:a + 1], in0=cv[:, j, b:b + 1], scalar=tap(2),
                                                     in1=cc[:, j, a:a + 1], op0=ALU.mult, op1=ALU.add))
                if p in (4, 5):
                    if p == 4:
                        ch.sync()
                    dve.wait_ge(unit_used, C0 + 8 * i + p + 1)
                    dve.tensor_tensor(halves(cc[:, j, :]), src, halves(cc[:, j, :]), ALU.mult).then_inc(dve_freed, 1)
                if p in (6, 7):
                    dve.wait_ge(dve_freed, 4 * i + 4)
                    dve.wait_ge(act_freed, C0 + 4 * i + 3 + j)
                    dve.tensor_tensor(yT[:, bass.ds(8 + 2 * i + j, 1), :][:, 0, :], cc[:, j, :], sz_b[:, j, :],
                                      ALU.mult).then_inc(yb_done, 1)
                split_lo(dve, unit(C0 + RING, i, 8, p), p % 4)
                if not last and p in MOD_SLOTS:
                    tp = MOD_SLOTS.index(p)
                    if tp == 0:
                        dve.wait_ge(red_ready, i + 1)
                        dve.wait_ge(bias_landed, 16 * i + 32)
                    mod_slot_dve(dve, 4 * i + 4 + tp, tp, tp == 0)
            assert ch.n == CONV_DVE

        def ssd_unit_src(g, k):
            if k < 4:
                col = (DI + 256 * g, DI + 256 * g + P, 2 * DI + P * g, 2 * DI + D + P * g)[k]
                return ssd_src[:, :, bass.ds(col, P)]
            return ssd_src[:, 4 * (k - 4):4 * (k - 4) + 4].rearrange("p k (g n) -> p k g n", n=64)[:, :, bass.ds(4 * g, 4)]

        def ssd_load(sp, g, k, slot):
            dst = raw_w[:, slot, :].rearrange("p (k n) -> p k n", n=P)
            if k >= 4:
                dst = raw_w[:, slot, :].rearrange("p (k g n) -> p k g n", k=4, n=64)
            sp.dma_start(dst, ssd_unit_src(g, k)).then_inc(landed[slot], 16)

        def state_view(t, d, g):
            return t[0, 0, d].rearrange("(g j q) p n -> (q p) g j n", j=2, q=2)[:, bass.ds(g, 1), :, :]

        def lfb_load(sp, g, c, slot):
            src = l_scr.rearrange("(g r) t -> g r t", r=8)[bass.ds(g, 1), :, c * P:(c + 1) * P]
            sp.dma_start(lfb[:, slot, :, :], src.partition_broadcast(P)).then_inc(lfb_landed[slot], 16)

        def table(tab, off, n):
            return tab[:, 0:200].rearrange("p (c k) -> p c k", c=NT)[:, :, off:off + n]

        def all_tables(off, n):
            return GT[:, :, 0:200].rearrange("p g (c k) -> p c g k", c=NT)[:, :, :, off:off + n]
        EL, DTO, WDT, DEC, DLT, NLB = 0, 8, 16, 24, 32, 36

        def perm(v):
            return v.rearrange("p (d g h) -> p g d h", d=2, g=G)

        def by_group(v):
            return v.rearrange("p c (g r) -> p c g r", g=G)

        def table_sp(sp):
            sp.dma_start(dtw_raw, ssd_src[:, :, SSD_IN - 64:SSD_IN]).then_inc(dtw_landed, 16)

        def params_sp(sp):
            sp.wait_ge(acc_step, 64)
            sp.dma_start(b_in, A["ssd_dt_bias"][0].rearrange("d h -> (d h)").partition_broadcast(P)).then_inc(bc_landed, 16)
            sp.dma_start(a_in, A["ssd_a_log"][0].rearrange("d h -> (d h)").partition_broadcast(P)).then_inc(bc_landed, 16)
            sp.dma_start(d_in, A["ssd_d"][0].partition_broadcast(P)).then_inc(bc_landed, 16)

        wd = [y[:, :, :].rearrange("p a b -> p (a b)")[:, 0:512].rearrange("p (k g r) -> p k g r", k=KT, g=G) for y in (y_hi, y_lo)]

        def dt_weights_act(act):
            act.wait_ge(unit_used, IN1)
            act.wait_ge(dtw_landed, 16)
            src = dtw_raw.rearrange("p k (d g h) -> p k d g h", d=2, g=G)
            for d in range(2):
                act.activation(wd[0][:, :, :, 4 * d:4 * d + 4], src[:, :, d], ACT.Copy).then_inc(dtw_hi, 1)

        def dt_weights_dve(dve):
            dve.wait_ge(unit_used, IN1)
            for d in range(2):
                dve.wait_ge(dtw_hi, d + 1)
                dve.tensor_tensor(wd[1][:, :, :, 4 * d:4 * d + 4], dtw_raw.rearrange("p k (d g h) -> p k d g h", d=2, g=G)[:, :, d],
                                  wd[0][:, :, :, 4 * d:4 * d + 4].bitcast(F32), ALU.subtract).then_inc(dtw_lo, 1)

        def conv_params_dve(dve):
            dve.wait_ge(x_updated, 10)
            p1 = par1[:, :].rearrange("p (k t) -> p k t", k=4)
            CPv = CPG.rearrange("p g (i k) -> p i k g", i=4)
            for i in range(4):
                src = p1[:, :, i:16:2] if i < 2 else p1[:, :, 16 + 8 * (i - 2):24 + 8 * (i - 2)]
                e = dve.tensor_copy(CPv[:, i], src)
            e.then_inc(cpg_ready, 1)

        def dt_pe(pe, stage_no):
            if stage_no == 0:
                pe.wait_ge(dtw_lo, 2)
                pe.wait_ge(xt_done, 2 * NT)
                for k in range(KT):
                    for n, (w, h) in enumerate(((0, h_hi), (0, h_lo), (1, h_hi))):
                        for s in range(2):
                            mm = pe.matmul(PS[0:64, 4 + s, 0:HALF], wd[w][:, k].rearrange("p g r -> p (g r)"),
                                           h[:, k, s * HALF:(s + 1) * HALF], start=(k == 0 and n == 0), stop=(k == KT - 1 and n == 2))
                mm.then_inc(dtp_ready, 1)
            elif stage_no == 1:
                pe.wait_ge(dt_rows, 1)
                for t in range(NT):
                    mm = pe.transpose(PS[:, 6, 64 * t:64 * t + 64], lrow[0:64, t * P:(t + 1) * P], ident[0:64, 0:64])
                mm.then_inc(dtp_ready, 1)
            elif stage_no == 2:
                pe.wait_ge(tab_dve, 13)
                o = PS[:, 4, 0:320].rearrange("p (c g d h) -> p c g d h", c=NT, g=G, d=2)
                da = tDA.rearrange("p c (g d h) -> p c g d h", g=G, d=2)
                pe.matmul(o[:, :, :, 0], upper, da[:, :, :, 0], start=True, stop=True)
                pe.matmul(o[:, :, :, 1], lower, da[:, :, :, 1], start=True, stop=True)
                pe.matmul(PS[:, 5, 0:320], ones[:, :], tDA.rearrange("p c r -> p (c r)"), start=True, stop=True).then_inc(cum_ready, 1)
            else:
                pe.wait_ge(tab_act, 4)
                for t in range(NT):
                    mm = pe.transpose(PSf[0:64, 3072 + t * P:3072 + (t + 1) * P], tL[:, t, :], ident)
                mm.then_inc(lt_ready, 1)

        def dt_act(act, stage_no):
            if stage_no == 0:
                act.wait_ge(dtp_ready, 1)
                act.activation(halves(lrow[0:64, :]), PS[0:64, 4:6, 0:HALF], ACT.Copy).then_inc(dt_rows, 1)
            elif stage_no == 1:
                act.wait_ge(bc_landed, 48)
                act.activation(a_pm.rearrange("p (g d h) -> p g d h", g=G, d=2)[:, :, 0, :], perm(a_in)[:, :, 0, :], ACT.Exp)
                act.activation(a_pm.rearrange("p (g d h) -> p g d h", g=G, d=2)[:, :, 1, :], perm(a_in)[:, :, 1, :], ACT.Exp).then_inc(tab_act, 1)
                act.wait_ge(tab_dve, 4)
                act.activation(tU, tNA, ACT.Exp).then_inc(tab_act, 1)
                act.wait_ge(tab_dve, 6)
                act.activation(tLW, tW, ACT.Ln).then_inc(tab_act, 1)
            elif stage_no == 2:
                act.wait_ge(cum_ready, 1)
                act.activation(tL, PS[:, 4, 0:320].rearrange("p (c r) -> p c r", c=NT), ACT.Copy).then_inc(tab_act, 1)
                act.wait_ge(tab_dve, 14)
                act.activation(tX, tT, ACT.Exp).then_inc(tab_act, 1)
            else:
                act.wait_ge(lt_ready, 1)
                act.activation(lrow[0:64, :], PSf[0:64, 3072:3072 + TOK], ACT.Copy).then_inc(yt_done, 1)
                act.activation(all_tables(EL, 8), by_group(tL), ACT.Exp)
                act.wait_ge(tot_copied, 1)
                act.activation(all_tables(DEC, 8), by_group(tNX), ACT.Exp).then_inc(tab_act, 1)

        def dt_dve(dve, stage_no):
            ch = Chain(dve, tab_dve, (0, 0, 13, 14)[stage_no])
            if stage_no == 1:
                dve.wait_ge(bc_landed, 48)
                for d in range(2):
                    last = dve.tensor_copy(b_pm.rearrange("p (g d h) -> p g d h", g=G, d=2)[:, :, d, :], perm(b_in)[:, :, d, :])
                ch.tick(last)
                ch.sync()
                dve.wait_ge(dtp_ready, 2)
                ch.tick(dve.tensor_tensor(tX, PS[:, 6, 0:320].rearrange("p (c r) -> p c r", c=NT),
                                          b_pm.unsqueeze(1).to_broadcast([P, NT, 64]), ALU.add))
                ch.sync()
                ch.tick(dve.tensor_scalar(tNX, tX, -1.0, None, ALU.mult))
                ch.sync()
                ch.tick(dve.tensor_tensor(tNA, tX, tNX, ALU.min))
                ch.tick(dve.tensor_scalar(tC, tX, 0.0, None, ALU.max))
                dve.wait_ge(tab_act, 2)
                ch.tick(dve.tensor_scalar(tW, tU, 1.0, None, ALU.add))
                ch.sync()
                ch.tick(dve.tensor_scalar(tNA, tW, -1.0, None, ALU.add))
                ch.sync()
                ch.tick(dve.tensor_tensor(tNA, tU, tNA, ALU.subtract))
                ch.tick(dve.reciprocal(tT, tW))
                ch.sync()
                ch.tick(dve.tensor_tensor(tNA, tNA, tT, ALU.mult))
                dve.wait_ge(tab_act, 3)
                ch.sync()
                ch.tick(dve.tensor_tensor(tNA, tNA, tLW, ALU.add))
                ch.sync()
                ch.tick(dve.tensor_tensor(tDT, tNA, tC, ALU.add))
                ch.sync()
                ch.tick(dve.scalar_tensor_tensor(out=tDA, in0=tDT, scalar=-1.0, in1=a_pm.unsqueeze(1).to_broadcast([P, NT, 64]),
                                                 op0=ALU.mult, op1=ALU.mult))
            elif stage_no == 2:
                dve.wait_ge(tab_act, 4)
                ch.tick(dve.tensor_tensor(tT, PS[:, 5, 0:320].rearrange("p (c r) -> p c r", c=NT), tL, ALU.subtract))
                dve.tensor_copy(tNX, PS[:, 5, 0:320].rearrange("p (c r) -> p c r", c=NT)).then_inc(tot_copied, 1)
            elif stage_no == 3:
                dve.tensor_copy(GT[:, :, 200:204], d_in.rearrange("p (g h) -> p g h", g=G))
                dve.tensor_scalar(GT[:, :, 204:206], par2[:, 40:56].rearrange("p (g j) -> p g j", g=G), 0.5, None, ALU.mult)
                dve.tensor_copy(all_tables(DTO, 8), by_group(tDT))
                lv = tL.rearrange("p c (g d h) -> p c g d h", g=G, d=2)
                for c in range(NT):
                    dve.tensor_tensor(all_tables(DLT, 4)[:, c], lv[:, c, :, 1], lv[:, c, :, 0], ALU.subtract)
                for c in range(NT):
                    dve.tensor_scalar(all_tables(NLB, 4)[:, c], lv[:, c, :, 1], -1.0, None, ALU.mult)
                dve.wait_ge(tab_act, 5)
                dve.tensor_tensor(all_tables(WDT, 8), by_group(tDT), by_group(tX), ALU.mult).then_inc(tables_ready, 1)

        def dt_sp(sp, stage_no):
            if stage_no == 3:
                for d in range(2):
                    sp.dma_start(h0r[:, 2 * d:2 * d + 2, :], state_view(A["state_ssm"], d, 0)[:, 0]).then_inc(h0_landed, 16)
                sp.wait_ge(yt_done, 1)
                sp.dma_start(l_scr, lrow[0:64, :]).then_inc(small_stored, 16)
                sp.wait_ge(small_stored, 16)
                for c in range(2):
                    lfb_load(sp, 0, c, c)

        def groups_copy(pool, g_ssd, g_proj, ps, pp):
            last = None
            if g_ssd is not None:
                last = pool.tensor_copy(gt[:, ps, :].unsqueeze(1), GT[:, bass.ds(g_ssd, 1), :])
            if g_proj is not None:
                last = pool.tensor_copy(cp[:, pp, :].unsqueeze(1), CPG[:, bass.ds(g_proj, 1), :])
            return last

        TAP_RANGES = {0: ((0, 0, HALF - 1), (0, HALF - 1, HALF), (1, HALF, LAT - 1), (1, LAT, TOK - 1)),
                      2: ((0, 1, HALF), (1, HALF, HALF + 1), (1, HALF + 1, LAT), (1, LAT + 1, TOK))}

        BODY = """
        P00 T0 P01 tok0 T1 P02 tok1 T2 M0 lfb0 P03 tok2 T3 xdt0 exp0 P04 tok3 T4 H0 hev0 M1 lfb1 P05 xw0 tok4 hd0 exp1 CB0
        P06 S0 cbm0 CB1 xw1 hup0 P07 hd1 cbm1 S1 cen0 G0
        P10 xw2 hup1 hd2 tap0 hi0 lo0 ld0 P11 S2 xw3 hup2 tanh0 xdt1 P12 SC0 scev0 nst0 G1 fin0 P13 Y0 M2 lfb2 exp2 yt0 u0
        P14 xdt2 G2 P15 P16 ya0 sq0 rs0 grp0 P17 yn0 M3 lfb3 exp3
        Y1 P20 cen1 yt1 u1 tap1 hi1 lo1 ld1 P21 YT0 ytev0 yst0 ya1 sq1 rs1 yn1 tanh1 xdt3 P22 G3 P23 P24 Y2 fin1 yt2 u2
        P25 YT1 ytev1 yst1 M4 lfb4 exp4 P26 ya2 sq2 rs2 yn2 P27 xdt4 cen2 tap2 hi2 lo2 ld2
        P30 Y3 G4 yt3 u3 P31 tanh2 P32 YT2 ytev2 yst2 fin2 ya3 sq3 rs3 yn3 P33 P34 P35 Y4 u4 P36 YT3 ytev3 yst3
        ya4 sq4 rs4 P37 cen3 tap3 yn4 hi3 lo3 ld3
        Z00 Z01 YT4 ytev4 yst4 tanh3 fin3 ztanh0 sz0 Z10 Z11 ztanh1 sz1 Z20 Z21 ztanh2 sz2 Z30 Z31 ztanh3 sz3
        Z40 Z41 ztanh4 sz4 hi4 lo4 ld4 hi5 lo5 ld5
        """.split()
        LAST = """
        ey0 ey1 ey2 ey3 T0 tok0 T1 tok1 T2 M0 lfb0 tok2 T3 xdt0 exp0 tok3 T4 H0 hev0 M1 lfb1 xw0 tok4 hd0 exp1 CB0
        S0 cbm0 CB1 xw1 hup0 hd1 cbm1 S1 eh0 G0 eh1 el0 el1 O0 xw2 hup1 hd2 S2 O1 xw3 hup2 xdt1 SC0 scev0 nst0 G1 eh2 el2
        Y0 M2 lfb2 exp2 yt0 u0 eh3 el3 xdt2 G2 O2 ya0 sq0 rs0 yn0 M3 exp3 Y1 yt1 u1 O3 YT0 ytev0 yst0 eh4 el4 ya1 sq1 rs1 yn1
        xdt3 G3 Y2 yt2 u2 O4 YT1 ytev1 yst1 eh5 el5 M4 exp4 ya2 sq2 rs2 yn2 xdt4 Y3 G4 yt3 u3 O5 YT2 ytev2 yst2 eh6 el6
        ya3 sq3 rs3 yn3 Y4 u4 O6 YT3 ytev3 yst3 eh7 el7 ya4 sq4 rs4 yn4 O7 YT4 ytev4 yst4
        """.split()
        LAST = [(e.rstrip("0123456789"), e[len(e.rstrip("0123456789")):]) for e in LAST]
        PROLOGUE = """
        P00 P01 P02 P03 P04 P05 P06 P07 cen0 tap0 hi0 lo0 ld0 P10 P11 P12 P13 P14 P15 P16 P17 tanh0 fin0 cen1 tap1 hi1 lo1 ld1 dt0
        P20 P21 P22 P23 P24 P25 P26 P27 tanh1 fin1 dt1 cen2 tap2 hi2 lo2 ld2 P30 P31 P32 P33 P34 P35 P36 P37 tanh2 fin2 dt2
        cen3 tap3 hi3 lo3 ld3 Z00 Z01 Z10 Z11 dt3 tanh3 fin3 ztanh0 sz0 ztanh1 sz1 Z20 Z21 ztanh2 sz2 Z30 Z31 ztanh3 sz3
        Z40 Z41 ztanh4 sz4 hi4 lo4 ld4 hi5 lo5 ld5
        """.split()
        PROLOGUE = [(e.rstrip("0123456789"), e[len(e.rstrip("0123456789")):]) for e in PROLOGUE]
        BODY = [(e.rstrip("0123456789"), e[len(e.rstrip("0123456789")):]) for e in BODY]
        PROJ = ("P", "Z", "cen", "tap", "tanh", "fin", "ztanh", "sz", "hi", "lo", "ld")

        class Body:

            def __init__(self, i, par, ssd=True, proj=True):
                self.i, self.par, self.ssd, self.proj = i, par, ssd, proj
                self.g = 2 * i + par
                self.n = self.g + 1
                self.np = (par + 1) % 2
                self.static = isinstance(i, int)

            def steps(self):
                if not self.ssd:
                    for ev, num in PROLOGUE:
                        yield ev, [int(d) for d in num]
                    return
                for ev, num in BODY if self.proj else LAST:
                    if (ev in PROJ and self.proj) or (ev not in PROJ and self.ssd):
                        yield ev, [int(d) for d in num]

            def unit(self, k):
                return 12 * self.i + (IN1 + 6 * (self.par + 1) + k), (6 * (self.par + 1) + k) % RING

            def split_unit(self, k):
                c = IN1 + 6 * (self.par + 1) + k + 4
                if self.static:
                    return c + 12 * self.i
                return (12 * self.i + c, 48 * self.i + 16 * (c // RING + 1))

            def count2(self, c):
                m = 5 * self.par + c
                return 5 * self.i + m // 2, m % 2

        def ssd_pe(pe, B):
            g, n = B.g, B.n
            b0 = 5 * g
            for ev, a in B.steps():
                k = a[0]
                if ev == "O":
                    early_pe(pe, k)
                    continue
                if ev == "dt":
                    dt_pe(pe, k)
                    continue
                if ev == "P":
                    u, slot = B.unit(k)
                    pair, kt = (B.np + k) % 2, a[1]
                    if kt == 0:
                        pe.wait_ge(lo_ready, u + 1)
                        if not (B.static and 9 * n + k < 2):
                            pe.wait_ge(proj_free, 9 * n + k - 1)
                        else:
                            pe.wait_ge(*((out_evac, 10) if k == 0 else (mod_ready, 4)))
                    if B.static and 9 * n + k == 0:
                        pe.wait_ge(h_ready, KT + kt + 1)
                    ws = slice(kt * P, (kt + 1) * P)
                    for j, (w, h) in enumerate(((w_hi, h_hi), (w_hi, h_lo), (w_lo, h_hi))):
                        for s in range(2):
                            mm = pe.matmul(PS[:, 2 * pair + s, 0:HALF], w[:, slot, ws], h[:, kt, s * HALF:(s + 1) * HALF],
                                           start=(kt == 0 and j == 0), stop=(kt == KT - 1 and j == 2))
                    if kt == KT - 1:
                        mm.then_inc(unit_used, 1)
                elif ev == "Z":
                    t, half = a
                    u, slot = B.unit(4)
                    pair = (B.np + 4 + t) % 2
                    if t == 0 and half == 0:
                        pe.wait_ge(lo_ready, u + 2)
                    if half == 0:
                        pe.wait_ge(proj_free, 9 * n + 3 + t)
                    for kt in range(4 * half, 4 * half + 4):
                        for j, (h, w) in enumerate(((h_hi, w_hi), (h_hi, w_lo), (h_lo, w_hi))):
                            mm = pe.matmul(PS[:, 2 * pair, 0:256], h[:, kt, t * P:(t + 1) * P],
                                           w[:, slot + kt // 4, 256 * (kt % 4):256 * (kt % 4) + 256],
                                           start=(kt == 0 and j == 0), stop=(kt == KT - 1 and j == 2))
                    if half == 1:
                        mm.then_inc(*((z_ready, 1) if t < NT - 1 else (unit_used, 2)))
                elif ev == "T":
                    if k == 0:
                        pe.wait_ge(conv_done, 4 * g + 4)
                        pe.wait_ge(yt_done, b0 + 1)
                    if k >= 2:
                        pe.wait_ge(tok_done, b0 + k - 1)
                    for j in range(3):
                        mm = pe.transpose(PS[:, 4 + k % 2, j * P:(j + 1) * P], cvx[:, j, k * P:(k + 1) * P], ident)
                    mm.then_inc(tr_ready, 1)
                elif ev == "H":
                    pe.wait_ge(h0_landed, 32 * g + 32)
                    for j in range(4):
                        mm = pe.transpose(PS[:, 6, j * P:(j + 1) * P], h0r[:, j, :], ident)
                    mm.then_inc(h_T, 1)
                elif ev == "CB":
                    if k == 1:
                        pe.wait_ge(tok_done, b0 + 4)
                    for c in range(4) if k == 0 else (4,):
                        o = PS[:, 7, c * P:(c + 1) * P] if k == 0 else PS[:, 5, 0:P]
                        mm = pe.matmul(o, cvx[:, 2, c * P:(c + 1) * P], cvC[:, B.par, c * P:(c + 1) * P], start=True, stop=True)
                    mm.then_inc(cb_ready, 1)
                elif ev == "S":
                    bank = (4, 5, 4)[k]
                    pe.wait_ge(xw_done, 4 * g + k + 1)
                    if k == 0:
                        pe.wait_ge(tok_done, b0 + 5)
                    elif k == 1:
                        pe.wait_ge(cbm_done, 2 * g + 2)
                    else:
                        pe.wait_ge(st_done, 3 * g + 1)
                    pe.matmul(PS[:, bank, 0:256], xb[:, k, 256:384], xws[:, k, 0:256], start=True, stop=True)
                    pe.matmul(PS[:, bank, 256:512], xb[:, 3 - k, 256:384], xws[:, k, 256:512], start=True, stop=True).then_inc(st_ready, 1)
                elif ev == "SC":
                    pe.wait_ge(xw_done, 4 * g + 4)
                    pe.wait_ge(st_done, 3 * g + 2)
                    for j in range(4):
                        mm = pe.matmul(PS[:, 5, j * P:(j + 1) * P], xws[:, 3, j * P:(j + 1) * P], xb[:, 4, 256:384], start=True, stop=True)
                    mm.then_inc(sc_ready, 1)
                elif ev == "Y":
                    r = (B.par + k) % 2
                    bo, bd = (6, 7) if k % 2 == 0 else (4, 5)
                    if k == 0:
                        pe.wait_ge(st_done, 3 * g + 3)
                        pe.wait_ge(hs0_done, g + 1)
                    elif k == 1:
                        pe.wait_ge(sc_done, g + 1)
                    else:
                        pe.wait_ge(yt_done, b0 + k)
                    if k < 4:
                        cc_ = cvC[:, B.par, k * P:(k + 1) * P]
                        pe.matmul(PS[:, bo, 0:256], cc_, hs[:, k, 0:256], start=True, stop=True)
                        pe.matmul(PS[:, bo, 256:512], cc_, hs[:, 3 - k, 256:512], start=True, stop=True)
                    pe.wait_ge(g_done, b0 + k + 1)
                    for h in range(4):
                        o = PS[:, bd, 64 * h:64 * h + 64]
                        pe.matmul(o, gm[:, r, 0, h, :], xdt[:, r, 64 * h:64 * h + 64], start=True, stop=False)
                        mm = pe.matmul(o, gm[:, r, 1, h, :], xdt[:, r, 256 + 64 * h:256 + 64 * h + 64], start=False, stop=True)
                    mm.then_inc(y_ready, 1)
                elif ev == "YT":
                    r = (B.par + k) % 2
                    pe.wait_ge(yn_done, b0 + k + 1)
                    for j in range(2):
                        mm = pe.transpose(PS[:, (6, 4)[k % 2], j * P:(j + 1) * P], yn[:, r, j * P:(j + 1) * P], ident)
                    mm.then_inc(ytr_ready, 1)

        def ssd_act(act, B):
            g, n = B.g, B.n
            b0 = 5 * g
            if B.static and n == 0:
                act.wait_ge(y_stored[0], 16)
                act.wait_ge(y_stored[1], 16)
                act.wait_ge(cp0_ready, 1)
            else:
                act.wait_ge(grp_done, n)
            for ev, a in B.steps():
                k = a[0]
                if ev == "eh":
                    early_act(act, k)
                    continue
                if ev == "dt":
                    dt_act(act, k)
                    continue
                pair = (B.np + k) % 2
                src = pair_view(pair)
                cpn = cp[:, B.np, :]
                cv_ = cvx[:, k, :] if k < 3 else cvC[:, B.np, :]
                if ev == "cen":
                    u, _ = B.unit(k)
                    act.wait_ge(unit_used, u + 1)
                    if not (B.static and n == 0):
                        act.wait_ge(*((cb_ready, 2 * n) if k == 2 else (tr_ready, 5 * n)))
                    act.activation(halves(cv_), src, ACT.Identity, bias=cpn[:, 4 * k + 3:4 * k + 4], scale=cpn[:, 4 * k + 1:4 * k + 2]).then_inc(cen_done, 1)
                elif ev == "tanh":
                    act.wait_ge(proj_free, 9 * n + k + 1)
                    if not (B.static and 4 * n + k == 0):
                        act.wait_ge(conv_done, 4 * n + k)
                    act.activation(th, cv_, ACT.Tanh).then_inc(th_done, 1)
                elif ev == "ztanh":
                    if k < NT - 1:
                        act.wait_ge(z_ready, 4 * n + k + 1)
                    else:
                        act.wait_ge(unit_used, B.unit(4)[0] + 2)
                    if k >= 2:
                        act.wait_ge(proj_free, 9 * n + 4 + k - 1)
                    zs = PS[:, 2 * ((B.np + 4 + k) % 2), 0:256]
                    act.activation(zth[:, k % 2, :], zs, ACT.Tanh, scale=0.5).then_inc(zth_done, 1)
                elif ev == "hi":
                    split_hi(act, B.split_unit(k), B.unit(k)[1])
                elif ev == "tok":
                    act.wait_ge(tr_ready, b0 + k + 1)
                    act.activation(xb[:, k, :], PS[:, 4 + k % 2, 0:384], ACT.Copy).then_inc(tok_done, 1)
                elif ev == "hev":
                    act.wait_ge(h_T, g + 1)
                    act.activation(hs[:, 0, :], PS[:, 6, :], ACT.Copy).then_inc(hs0_done, 1)
                elif ev == "exp":
                    act.wait_ge(m_done, b0 + k + 1)
                    r = (B.par + k) % 2
                    for h in range(4):
                        e = act.activation(ea[:, r, h, :], ea[:, r, h, :], ACT.Exp, bias=table(gt[:, B.par, :], NLB, 4)[:, k, h:h + 1])
                    e.then_inc(exp_done, 1)
                elif ev == "scev":
                    act.wait_ge(sc_ready, g + 1)
                    act.wait_ge(small_stored, 32 * g + 16)
                    act.activation(nst, PS[:, 5, :], ACT.Copy).then_inc(sc_done, 1)
                elif ev == "sq":
                    r = (B.par + k) % 2
                    act.wait_ge(gz_done, b0 + k + 1)
                    act.activation(yn[:, r, :], aa[:, r, :], ACT.Square, scale=1.0 / 32, accum_out=ssy[:, r:r + 1]).then_inc(sqy_done, 1)
                elif ev == "yn":
                    r = (B.par + k) % 2
                    act.wait_ge(ry_done, b0 + k + 1)
                    act.activation(yn[:, r, :], aa[:, r, :], ACT.Copy, scale=ry[:, r:r + 1]).then_inc(yn_done, 1)
                elif ev == "ytev":
                    cnt, r = B.count2(k)
                    act.wait_ge(ytr_ready, b0 + k + 1)
                    act.wait_ge(y_stored[r], 16 * cnt + 16)
                    for j in range(2):
                        e = act.activation(ysb[:, r, j, :], PS[:, (6, 4)[k % 2], j * P:(j + 1) * P], ACT.Copy,
                                           scale=gt[:, B.par, 204 + j:205 + j])
                    e.then_inc(yt_done, 1)

        def ssd_dve(dve, B):
            g, n = B.g, B.n
            b0 = 5 * g
            if B.static and n == 0:
                dve.wait_ge(cp0_ready, 1)
            else:
                dve.wait_ge(grp_done, n)
            tab = gt[:, B.par, :]

            def heads(off, nh, c):
                return table(tab, off, nh)[:, c, :].unsqueeze(2).to_broadcast([P, nh, 64])
            for ev, a in B.steps():
                k = a[0]
                if ev == "el":
                    early_dve(dve, k)
                    continue
                if ev == "dt":
                    dt_dve(dve, k)
                    continue
                pair = (B.np + k) % 2
                r = (B.par + k) % 2
                if ev == "tap":
                    cpn = cp[:, B.np, :]
                    cv_ = cvx[:, k, :] if k < 3 else cvC[:, B.np, :]
                    src = pair_view(pair)
                    dve.wait_ge(cen_done, 4 * n + k + 1)
                    for side, off in ((0, 1), (2, -1)):
                        if side == 2:
                            dve.wait_ge(tap_step, 4 * n + k + 1)
                        for half, a, b in TAP_RANGES[side]:
                            ins = dve.scalar_tensor_tensor(out=cv_[:, a + off:b + off], in0=src[:, half, a - HALF * half:b - HALF * half],
                                                           scalar=cpn[:, 4 * k + side:4 * k + side + 1],
                                                           in1=cv_[:, a + off:b + off], op0=ALU.mult, op1=ALU.add)
                        ins.then_inc(proj_free if side == 2 else tap_step, 1)
                elif ev == "fin":
                    cv_ = cvx[:, k, :] if k < 3 else cvC[:, B.np, :]
                    dve.wait_ge(th_done, 4 * n + k + 1)
                    dve.scalar_tensor_tensor(out=cv_, in0=th, scalar=1.0, in1=cv_, op0=ALU.add, op1=ALU.mult).then_inc(conv_done, 1)
                elif ev == "sz":
                    zs = PS[:, 2 * ((B.np + 4 + k) % 2), 0:256]
                    dve.wait_ge(zth_done, 5 * n + k + 1)
                    if not (B.static and n == 0):
                        dve.wait_ge(gz_done, 5 * n - 5 + k + 1)
                    dve.scalar_tensor_tensor(out=sz[:, k, :], in0=zth[:, k % 2, :], scalar=1.0, in1=zs,
                                             op0=ALU.add, op1=ALU.mult).then_inc(proj_free, 1)
                elif ev == "lo":
                    split_lo(dve, B.split_unit(k), B.unit(k)[1])
                elif ev == "M":
                    cnt, slot = B.count2(k)
                    dve.wait_ge(lfb_landed[slot], 16 * cnt + 16)
                    if k >= 2:
                        dve.wait_ge(g_done, b0 + k - 1)
                    for h in range(4):
                        e = dve.scalar_tensor_tensor(out=ea[:, r, h, :], in0=lfb[:, slot, h, :], scalar=table(tab, DLT, 4)[:, k, h:h + 1],
                                                     in1=lfb[:, slot, 4 + h, :], op0=ALU.add, op1=ALU.min)
                    e.then_inc(m_done, 1)
                elif ev == "cbm":
                    dve.wait_ge(cb_ready, 2 * g + k + 1)
                    m, src = (4, PS[:, 7, :].rearrange("p (c l) -> p c l", c=4)) if k == 0 else (1, PS[:, 5, 0:P].unsqueeze(1))
                    for j, mask in enumerate((upper, lower)):
                        e = dve.tensor_tensor(cbm[:, j, 4 * k:4 * k + m, :], src, mask.unsqueeze(1).to_broadcast([P, m, P]), ALU.mult)
                    e.then_inc(cbm_done, 1)
                elif ev == "xdt":
                    dve.wait_ge(tok_done, b0 + k + 1)
                    if k >= 2:
                        dve.wait_ge(y_ready, b0 + k - 1)
                    dve.tensor_tensor(xdt[:, r, :].rearrange("p (d h q) -> p d h q", d=2, h=4),
                                      xb[:, k, 0:256].rearrange("p (h q) -> p h q", h=4).unsqueeze(1).to_broadcast([P, 2, 4, 64]),
                                      table(tab, DTO, 8)[:, k, :].rearrange("p (d h) -> p d h", d=2).unsqueeze(3).to_broadcast([P, 2, 4, 64]),
                                      ALU.mult)
                elif ev == "G":
                    dve.wait_ge(exp_done, b0 + k + 1)
                    dve.wait_ge(cbm_done, 2 * g + (1 if k < 4 else 2))
                    if k >= 2:
                        dve.wait_ge(y_ready, b0 + k - 1)
                    for j in range(2):
                        e = dve.tensor_tensor(gm[:, r, j, :, :], ea[:, r, :, :], cbm[:, j, k, :].unsqueeze(1).to_broadcast([P, 4, P]), ALU.mult)
                    e.then_inc(g_done, 1)
                elif ev == "hup":
                    dve.wait_ge(st_ready, 3 * g + k + 1)
                    dve.wait_ge(hd_done, 3 * g + k + 1)
                    dve.tensor_tensor(hs[:, k + 1, :], PS[:, (4, 5, 4)[k], :], hd, ALU.add).then_inc(st_done, 1)
                elif ev == "yt":
                    dve.wait_ge(y_ready, b0 + k + 1)
                    if k >= 1:
                        dve.wait_ge(u_done, b0 + k)
                    dve.tensor_tensor(yo.rearrange("p (h q) -> p h q", h=8), PS[:, (6, 4)[k % 2], :].rearrange("p (h q) -> p h q", h=8),
                                      heads(EL, 8, k), ALU.mult).then_inc(t_done, 1)
                elif ev == "ya":
                    dve.wait_ge(u_done, b0 + k + 1)
                    dve.wait_ge(y_ready, b0 + k + 1)
                    if k >= 2:
                        dve.wait_ge(yn_done, b0 + k - 1)
                    dve.tensor_tensor(aa[:, r, :], PS[:, (7, 5)[k % 2], 0:256], uu[:, r, :], ALU.add).then_inc(a_step, 1)
                    dve.wait_ge(a_step, b0 + k + 1)
                    dve.tensor_tensor(aa[:, r, :], aa[:, r, :], sz[:, k, :], ALU.mult).then_inc(gz_done, 1)

        def ssd_pool(pool, B):
            g, n = B.g, B.n
            b0 = 5 * g
            tab = gt[:, B.par, :]
            ch = Chain(pool, pool_step, 8 * g)

            def xh(c):
                return xb[:, c, 0:256].rearrange("p (h q) -> p h q", h=4)

            def heads(col):
                return col.unsqueeze(2).to_broadcast([P, 4, 64])

            def hv(v):
                return v.rearrange("p (h q) -> p h q", h=4)
            if not B.ssd:
                return
            pool.wait_ge(grp_done, n)
            for ev, a in B.steps():
                k = a[0]
                r = (B.par + k) % 2
                if ev == "xw":
                    pool.wait_ge(tok_done, b0 + (4 if k == 0 else 5))
                    for d in range(2):
                        c = (k, 3 - k)[d] if k < 3 else 4
                        e = pool.tensor_tensor(hv(xws[:, k, 256 * d:256 * d + 256]), xh(c), heads(table(tab, WDT + 4 * d, 4)[:, c, :]), ALU.mult)
                    e.then_inc(xw_done, 1)
                elif ev == "hd":
                    pool.wait_ge(*((hs0_done, g + 1) if k == 0 else (st_done, 3 * g + k)))
                    for d in range(2):
                        c = (k, 3 - k)[d]
                        e = pool.tensor_tensor(hv(hd[:, 256 * d:256 * d + 256]), hv(hs[:, k, 256 * d:256 * d + 256]),
                                               heads(table(tab, DEC + 4 * d, 4)[:, c, :]), ALU.mult)
                    e.then_inc(hd_done, 1)
                elif ev == "u":
                    if k < 4:
                        pool.wait_ge(t_done, 4 * g + k + 1)
                    else:
                        pool.wait_ge(gz_done, b0 + 3)
                    xd = pool.tensor_tensor(hv(uu[:, r, :]), xh(k), heads(gt[:, B.par, 200:204]), ALU.mult)
                    if k == 4:
                        xd.then_inc(u_done, 1)
                    else:
                        ch.tick(xd)
                        ch.tick(pool.tensor_tensor(yo[:, 0:256], yo[:, 0:256], yo[:, 256:512], ALU.add))
                        ch.sync()
                        pool.tensor_tensor(uu[:, r, :], uu[:, r, :], yo[:, 0:256], ALU.add).then_inc(u_done, 1)
                elif ev == "rs":
                    pool.wait_ge(sqy_done, b0 + k + 1)
                    pool.tensor_tensor(ry[:, r:r + 1], ssy[:, r:r + 1], eps_col[:, :], ALU.add).then_inc(msy_done, 1)
                    pool.wait_ge(msy_done, b0 + k + 1)
                    pool.tensor_tensor(ry[:, r:r + 1], ry[:, r:r + 1], half_neg[:, :], ALU.pow).then_inc(ry_done, 1)
                elif ev == "grp":
                    more = (not B.static) or g + 2 < G
                    if not B.static or g + 1 < G:
                        pool.wait_ge(yt_done, b0 + 1)
                        pool.wait_ge(conv_done, 4 * g + 4)
                        groups_copy(pool, g + 1, g + 2 if more else None, 1 - B.par, B.par).then_inc(grp_done, 1)

        def ssd_sp(sp, B):
            g, n = B.g, B.n
            b0 = 5 * g
            for ev, a in B.steps():
                k = a[0]
                if ev == "ey":
                    early_sp(sp, k)
                    continue
                if ev == "dt":
                    dt_sp(sp, k)
                    continue
                if ev == "ld":
                    u, slot = B.unit(k)
                    sp.wait_ge(lo_ready, u + 3)
                    if B.static and n + 1 >= G:
                        out_load(sp, 1, k)
                    else:
                        ssd_load(sp, 2 * B.i + (B.par + 2), k, (slot + 6) % RING)
                elif ev == "lfb":
                    if B.static and g == G - 1 and k >= 3:
                        continue
                    sp.wait_ge(m_done, b0 + k + 1)
                    gg, c = (g, k + 2) if k < 3 else (g + 1, k - 3)
                    lfb_load(sp, gg, c, B.count2(k)[1])
                elif ev == "nst":
                    sp.wait_ge(sc_done, g + 1)
                    for d in range(2):
                        sp.dma_start(state_view(new_state, d, g)[:, 0], nst.rearrange("p (j n) -> p j n", j=4)[:, 2 * d:2 * d + 2, :]).then_inc(small_stored, 16)
                    if not (B.static and g + 1 == G):
                        sp.wait_ge(h_T, g + 1)
                        for d in range(2):
                            sp.dma_start(h0r[:, 2 * d:2 * d + 2, :], state_view(A["state_ssm"], d, g + 1)[:, 0]).then_inc(h0_landed, 16)
                elif ev == "yst":
                    _, r = B.count2(k)
                    sp.wait_ge(yt_done, b0 + k + 2)
                    sp.dma_start(y_scr[:, bass.ds(2 * g, 2), k * P:(k + 1) * P], ysb[:, r, :, :]).then_inc(y_stored[r], 16)

        def all_groups(eng, part):
            part(eng, Body(-1, 1, ssd=False))
            with eng.Fori(0, 3) as i:
                part(eng, Body(i, 0))
                part(eng, Body(i, 1))
            part(eng, Body(3, 0))
            part(eng, Body(3, 1, proj=False))

        PAR_DMAS = 7

        def fc_col(u):
            if u < 16:
                i, k = u // 4, u % 4
                return (0, 0, D, D)[k] + P * (2 * i + k % 2)
            i, p = (u - 16) // 8, (u - 16) % 8
            return (3 * D, 4 * D, 2 * D, 5 * D)[p // 2] + P * (2 * i + p % 2)

        def out_load(sp, layer, v):
            u = (OUT0, OUT1)[layer] + v
            sp.dma_start(raw_w[:, u % 4, :].rearrange("p (k n) -> p k n", k=2),
                         wout_src[layer][:, 2 * (v % 8):2 * (v % 8) + 2, 512 * (v // 8):512 * (v // 8) + 512]).then_inc(landed[u % 4], 16)

        @block.sync
        def _(sp):
            sp.dma_start(cond[:, 0, :], A["c"].rearrange("a (p t) -> (a p) t", t=KT)).then_inc(cond_landed, 16)
            sp.dma_start(cond[:, 1, :], A["c_ctx"].rearrange("(p t) -> p t", t=KT)).then_inc(cond_landed, 16)
            sp.dma_start(cst[:, :], A["consts"]).then_inc(par_landed, 16)
            sp.dma_start(praw[0:96, 0, :], A["ssd_conv_w"].rearrange("a k (t n) -> (a k t) n", n=P)).then_inc(par_landed, 16)
            sp.dma_start(praw[96:128, 0, :], A["ssd_conv_b"].rearrange("a (t n) -> (a t) n", n=P)).then_inc(par_landed, 16)
            sp.dma_start(praw[0:16, 1, :], A["norm_g"].rearrange("a (t n) -> (a t) n", n=P)).then_inc(par_landed, 16)
            sp.dma_start(praw[16:40, 1, :], A["fc_conv_w"].rearrange("a k (t n) -> (a k t) n", n=P)).then_inc(par_landed, 16)
            sp.dma_start(praw[40:56, 1, :], A["ssd_norm_g"].rearrange("a (t n) -> (a t) n", n=P)).then_inc(par_landed, 16)
            sp.dma_start(praw[56:72, 1, :], A["b_mod"].rearrange("a (t n) -> (a t) n", n=P)[0:16, :]).then_inc(par_landed, 16)
            xs = A["x_sample"][0].rearrange("(t p) d -> p t d", p=P)
            for s in range(8):
                if s >= 4:
                    sp.wait_ge(wm_used, s - 3)
                q, half = s // 2, s % 2
                sp.dma_start(wm_ring[:, s % 4], wm_src[0][:, 2 * q:2 * q + 2, 1024 * half:1024 * half + 1024]).then_inc(wm_landed[s % 4], 16)
                if s == 3:
                    sp.dma_start(x[:, 0:4, :], xs).then_inc(x_landed, 16)
                    sp.dma_start(x[:, 4, :], A["x_prompt"][0]).then_inc(x_landed, 16)
                    for u in range(4):
                        sp.dma_start(raw_w[:, u, :], fc_src[:, :, fc_col(u):fc_col(u) + P]).then_inc(landed[u], 16)
            sp.wait_ge(mod_ready, 2)
            sp.dma_start(dft_g, A["dft_group"]).then_inc(dft_landed, 16)
            sp.dma_start(dft_l, A["dft_token"]).then_inc(dft_landed, 16)
            for i in (0, 1, 2):
                for k in range(4):
                    sp.wait_ge(lo_ready, 4 * i + k + 1)
                    sp.dma_start(raw_w[:, k, :], fc_src[:, :, fc_col(4 * i + 4 + k):fc_col(4 * i + 4 + k) + P]).then_inc(landed[k], 16)
            for k in range(4):
                sp.wait_ge(lo_ready, 12 + k + 1)
                sp.dma_start(raw_w[:, k, :], fc_src[:, :, fc_col(16 + k):fc_col(16 + k) + P]).then_inc(landed[k], 16)
            for i in range(4):
                for p in range(8):
                    u = C0 + 8 * i + p + 4
                    sp.wait_ge(lo_ready, u - 3)
                    if u < OUT0:
                        src = fc_src[:, :, fc_col(u):fc_col(u) + P]
                        sp.dma_start(raw_w[:, u % 4, :], src).then_inc(landed[u % 4], 16)
                    else:
                        out_load(sp, 0, u - OUT0)
            sp.wait_ge(row_stored, 64)
            for c in range(2):
                sp.dma_start(gate[:, c, :], mod_scr[0, c].partition_broadcast(P)).then_inc(gate_landed, 16)
            sp.dma_start(praw3[0:32, :], mod_scr[1:3].rearrange("k c (j n) -> (k c j) n", n=P)).then_inc(p3_landed, 16)
            sp.wait_ge(yb_done, 8)
            sp.dma_start(x[:, 0:4, :], xs).then_inc(x_back, 16)
            sp.dma_start(x[:, 4, :], A["x_prompt"][0]).then_inc(x_back, 16)
            for v in range(4, N_OUT):
                sp.wait_ge(lo_ready, OUT0 + v - 3)
                out_load(sp, 0, v)
            if stage:
                table_sp(sp)
                params_sp(sp)
                for k in range(4):
                    sp.wait_ge(lo_ready, IN1 + k - 3)
                    ssd_load(sp, 0, k, k)
                sp.wait_ge(x_updated, 10)
                sp.dma_start(x1_scr[:, 0:4 * D], x[:, 0:4, :].rearrange("p t d -> p (t d)")).then_inc(y_stored[0], 16)
                sp.dma_start(x1_scr[:, 4 * D:5 * D], x[:, 4, :]).then_inc(y_stored[1], 16)
                for k in range(4, 6):
                    sp.wait_ge(lo_ready, IN1 + k - 3)
                    ssd_load(sp, 0, k, k % RING)
                all_groups(sp, ssd_sp)
                sp.wait_ge(y_ready, 5 * G)
                sp.wait_ge(u_done, 5 * G)
                for r in range(2):
                    sp.wait_ge(y_stored[r], 16 + 16 * (18 - r))
                sp.dma_start(yT[:, 8:12, :], y_scr[:, 8:12, :]).then_inc(y_back[4], 16)
                sp.dma_start(yT[:, 12:14, :], y_scr[:, 12:14, :]).then_inc(y_back[5], 16)
                sp.wait_ge(yt_done, 1 + 5 * G)
                sp.wait_ge(y_stored[0], 16 + 16 * 20)
                sp.wait_ge(y_stored[1], 16 + 16 * 20)
                sp.dma_start(yT[:, 14:16, :], y_scr[:, 14:16, :]).then_inc(y_back[6], 16)
                sp.wait_ge(small_stored, 16 + 32 * G)
                sp.dma_start(x[:, 0:4, :], x1_scr[:, 0:4 * D].rearrange("p (t d) -> p t d", d=D)).then_inc(x_back, 16)
                sp.dma_start(x[:, 4, :], x1_scr[:, 4 * D:5 * D]).then_inc(x_back, 16)
                for c in range(2):
                    sp.dma_start(gate[:, c, :], mod_scr[3, c].partition_broadcast(P)).then_inc(gate_landed, 16)
                sp.dma_start(fin_g, A["final_norm_g"].partition_broadcast(P)).then_inc(fg_landed, 16)
                for v in range(6, N_OUT):
                    sp.wait_ge(lo_ready, OUT1 + v - 3)
                    out_load(sp, 1, v)
                for t in range(NT):
                    sp.wait_ge(fin_done, t + 1)
                    dst = y_sample[0].rearrange("(t p) d -> p t d", p=P)[:, t, :] if t < 4 else y_prompt[0]
                    sp.dma_start(dst, x[:, t, :]).then_inc(stored, 16)
                sp.wait_ge(stored, 16 * NT)
            if stage == 0:
                sp.wait_ge(x_updated, 10)
                sp.dma_start(y_sample[0].rearrange("(t p) d -> p t d", p=P), x[:, 0:4, :]).then_inc(stored, 16)
                sp.dma_start(y_prompt[0], x[:, 4, :]).then_inc(stored, 16)
                sp.dma_start(new_state.rearrange("a b c h p n -> (a b c h p n)").rearrange("(p f) -> p f", p=P), yT[:, 0:8, :].rearrange("p a b -> p (a b)")[:, 0:4096]).then_inc(stored, 16)
                sp.wait_ge(stored, 48)

        @block.tensor
        def _(pe):
            start_pe(pe)
            norm_pe(pe, 0, xn)
            start_pe_mod_T(pe)
            fourier_pe(pe, 0, True)
            with pe.Fori(1, 4) as i:
                fourier_pe(pe, i, False)
            conv_pe(pe, 0, True, False)
            with pe.Fori(1, 4) as i:
                conv_pe(pe, i, False, False)
            pe.wait_ge(act_freed, 32)
            pe.wait_ge(dve_freed, 16)
            pe.wait_ge(row_copied, 4)
            out_pe(pe, 0)
            if stage:
                pe.wait_ge(p3_landed, 16)
                pe.wait_ge(out_evac, 4)
                pe.transpose(PS[:, 3, 0:32], praw3[0:32, :], ident[0:32, 0:32]).then_inc(mod_T, 1)
                norm_pe(pe, 1, xn1)
                all_groups(pe, ssd_pe)
                pe.wait_ge(yt_done, 1 + 5 * G)
                out_pe(pe, 1)

        @block.scalar
        def _(act):
            act.wait_ge(cond_landed, 32)
            act.activation(cond[:, :, :], cond[:, :, :], ACT.Silu).then_inc(cond_ready, 1)
            norm_act(act, 0, xn, xT0)
            for u in range(4):
                split_hi(act, u, u)
            act.wait_ge(wm_used, 8)
            act.activation(mod_sb[0:2, 0:1024], PSf[0:2, 0:1024], ACT.Copy).then_inc(mod_copied, 1)
            h_act(act, 0, xT0)
            fourier_act(act, 0, True)
            with act.Fori(1, 4) as i:
                fourier_act(act, i, False)
            conv_act(act, 0, True, False)
            with act.Fori(1, 4) as i:
                conv_act(act, i, False, False)
            out_act(act, 0)
            if stage:
                norm_act(act, 1, xn1, xT1)
                dt_weights_act(act)
                h_act(act, 1, xT1)
                all_groups(act, ssd_act)
                out_act(act, 1)
                for t in range(NT):
                    act.wait_ge(x_updated, 15 + t + 1)
                    if t >= 2:
                        act.wait_ge(sq_done, 10 + t - 1)
                    act.activation(sq_junk[:, t % 2, :], x[:, t, :], ACT.Square, accum_out=ssq[:, 10 + t:11 + t]).then_inc(sq_done, 1)

        @block.vector
        def _(dve):
            dve.memset(ones[:, :], 1.0).then_inc(ones_ready, 1)
            dve.wait_ge(par_T, 1)
            dve.tensor_scalar(par1[:, :], PS[:, 6, 0:P], 0.5, None, ALU.mult).then_inc(par_ready, 1)
            dve.tensor_copy(par2[:, :], PS[:, 6, P:P + 72]).then_inc(par_ready, 1)
            norm_dve(dve, 0, xn)
            for u in range(4):
                split_lo(dve, u, u)
            dve.wait_ge(wm_used, 8)
            dve.tensor_copy(mod_sb[0:2, 1024:2048], PSf[0:2, 1024:2048]).then_inc(mod_copied, 1)
            dve.wait_ge(mod_T, 1)
            dve.wait_ge(par_ready, 2)
            for k in range(2):
                dve.tensor_tensor(ss_mod[:, k].rearrange("p c j -> p j c"), PS[:, 4, 16 * k:16 * k + 16].rearrange("p (j c) -> p j c", c=2),
                                  par2[:, 56 + 8 * k:64 + 8 * k].unsqueeze(2).to_broadcast([P, KT, 2]), ALU.add).then_inc(mod_ready, 1)
            dve.wait_ge(mod_ready, 2)
            dve.scalar_tensor_tensor(out=ss_mod[:, 1], in0=ss_mod[:, 1], scalar=1.0,
                                     in1=par2[:, 0:8].unsqueeze(1).to_broadcast([P, 2, KT]), op0=ALU.add, op1=ALU.mult).then_inc(mod_step, 1)
            dve.wait_ge(mod_step, 1)
            h_dve(dve, 0, xT0)
            fourier_dve(dve, 0, True)
            with dve.Fori(1, 4) as i:
                fourier_dve(dve, i, False)
            conv_dve(dve, 0, True, False)
            with dve.Fori(1, 3) as i:
                conv_dve(dve, i, False, False)
            conv_dve(dve, 3, False, True)
            out_dve(dve, 0)
            if stage:
                dve.wait_ge(mod_T, 2)
                dve.tensor_copy(ss_mod[:, 0], PS[:, 3, 0:16].rearrange("p (c j) -> p c j", c=2)).then_inc(mod_ready, 1)
                dve.scalar_tensor_tensor(out=ss_mod[:, 1], in0=PS[:, 3, 16:32].rearrange("p (c j) -> p c j", c=2), scalar=1.0,
                                         in1=par2[:, 8:16].unsqueeze(1).to_broadcast([P, 2, KT]), op0=ALU.add, op1=ALU.mult).then_inc(mod_ready, 1)
                dt_weights_dve(dve)
                conv_params_dve(dve)
                h_dve(dve, 1, xT1)
                all_groups(dve, ssd_dve)
                out_dve(dve, 1)
                dve.wait_ge(fg_landed, 16)
                for t in range(NT):
                    dve.wait_ge(rstd_done, 10 + t + 1)
                    dve.scalar_tensor_tensor(out=x[:, t, :], in0=x[:, t, :], scalar=rstd[:, 10 + t:11 + t], in1=fin_g,
                                             op0=ALU.mult, op1=ALU.mult).then_inc(fin_done, 1)

        @block.gpsimd
        def _(pool):
            pool.memset(half_neg[:, :], -0.5).then_inc(exponent_ready, 1)
            pool.memset(eps_col[:, :], EPS).then_inc(exponent_ready, 1)
            pool.wait_ge(exponent_ready, 2)
            norm_pool(pool, 0)
            mod_pool(pool)
            if stage:
                norm_pool(pool, 1)
                pool.wait_ge(cpg_ready, 1)
                groups_copy(pool, None, 0, 0, 0).then_inc(cp0_ready, 1)
                pool.wait_ge(tables_ready, 1)
                pool.wait_ge(tab_act, 6)
                groups_copy(pool, 0, None, 0, 0)
                groups_copy(pool, None, 1, 0, 1).then_inc(grp_done, 1)
                all_groups(pool, ssd_pool)
                norm_pool(pool, 2)


def constants():
    import numpy as np
    r = np.arange(P)
    tri = [np.eye(P), r[:, None] <= r[None, :], r[:, None] >= r[None, :]]
    consts = np.concatenate([np.asarray(t, np.float64) for t in tri], 1)
    k = np.arange(256)
    th = 2 * np.pi * ((k[:, None] * k[None, :]) % 256) / 256
    grp = np.concatenate([np.cos(th), np.sin(th)], 1) / 16
    grp = grp.reshape(2, P, 512).transpose(1, 0, 2)
    tok = []
    for f in (np.cos, lambda t: -np.sin(t)):
        for q in range(4):
            th = 2 * np.pi * ((r[:, None] * (4 * r[None, :] + q)) % LAT) / LAT
            tok.append(f(th) / np.sqrt(LAT))
    th = 2 * np.pi * ((r[:, None] * r[None, :]) % CTX) / CTX
    tok += [np.cos(th) / np.sqrt(CTX), -np.sin(th) / np.sqrt(CTX)]
    tok = np.stack(tok, 1)
    return {"consts": consts.astype(np.float32), "dft_group": grp.astype(np.float32), "dft_token": tok.astype(np.float32)}


_INS = ["x_prompt", "x_sample", "state_ssm", "c", "c_ctx", "w_mod", "b_mod", "norm_g", "fc_w_in", "fc_conv_w", "fc_w_out",
        "ssd_w_in", "ssd_conv_w", "ssd_conv_b", "ssd_dt_bias", "ssd_a_log", "ssd_d", "ssd_norm_g", "ssd_w_out", "final_norm_g"]
_OUTS = [(1, CTX, D), (1, LAT, D), (1, 1, 2, HEADS, 64, P)]
STAGE = 2


def kernel(**inputs):
    import numpy as _np
    import concourse.bacc as _bacc
    from concourse.bass_utils import run_bass_kernel_spmd as _run

    nc = _bacc.Bacc("TRN2", target_bir_lowering=False, num_devices=1)
    arrays, args = {}, {}
    given = {name: _np.ascontiguousarray(inputs[name]) for name in _INS}
    given.update(constants())
    for name, a in given.items():
        arrays[f"in_{name}_dram"] = a
        args[name] = nc.dram_tensor(f"in_{name}_dram", a.shape, mybir.dt.from_np(a.dtype), kind="ExternalInput").ap()
    outs = [nc.dram_tensor(f"out_{i}_dram", shape, F32, kind="ExternalOutput").ap() for i, shape in enumerate(_OUTS)]
    build_step(nc, args, outs, STAGE)
    r = _run(nc, [arrays], core_ids=[0])
    return tuple(r.results[0][f"out_{i}_dram"] for i in range(len(_OUTS)))
```

```python
from contextlib import ExitStack

import concourse.bass as bass
from concourse import mybir

F32 = mybir.dt.float32
F32R = mybir.dt.float32r
ALU = mybir.AluOpType
ACT = mybir.ActivationFunctionType

P = 128
D = 1024
KT = D // P
LAT, CTX = 512, 128
TOK = LAT + CTX
NT = TOK // P
SEGS = ((0, LAT), (LAT, TOK))
HALF = TOK // 2
FC_IN = 6 * D
UNIT = 1024
RING = 4
EPS = 1e-6
N_IN0 = 48
N_OUT = 16
OUT0 = N_IN0
IN1 = OUT0 + N_OUT
G = 8
UPG = 6
OUT1 = IN1 + G * UPG
UNITS = OUT1 + N_OUT
HEADS = 32
DI = 2048
SSD_IN = 6208


class Chain:

    def __init__(self, eng, sem, base=0):
        self.eng, self.sem, self.base, self.n = eng, sem, base, 0

    def tick(self, ins):
        self.n += 1
        ins.then_inc(self.sem, 1)

    def sync(self):
        self.eng.wait_ge(self.sem, self.base + self.n)


def build_step(nc, A, outs):
    y_prompt, y_sample, new_state = outs
    mod_scr = nc.dram_tensor("mod_scr", (4, 2, D), F32, kind="Internal").ap()
    x1_scr = nc.dram_tensor("x1_scr", (P, NT * D), F32, kind="Internal").ap()

    l_scr = nc.dram_tensor("l_scr", (64, TOK), F32, kind="Internal").ap()
    y_scr = nc.dram_tensor("y_scr", (P, 16, TOK), F32, kind="Internal").ap()

    ssd_src = A["ssd_w_in"][0].rearrange("(k p) n -> p k n", p=P)
    fc_src = A["fc_w_in"][0].rearrange("(k p) n -> p k n", p=P)
    wm_src = [A["w_mod"][l].rearrange("(p t) n -> p t n", t=KT) for l in range(2)]
    wout_src = [A[n][0].rearrange("(k p) n -> p k n", p=P) for n in ("fc_w_out", "ssd_w_out")]

    ctx = ExitStack()
    with ctx:
        def sb(name, shape, dt=F32):
            return ctx.enter_context(nc.sbuf_tensor(name, shape, dt))

        def sem(name):
            return ctx.enter_context(nc.semaphore(name))

        PS = ctx.enter_context(nc.psum_tensor("PS", [P, 8, 512], F32))
        PSf = PS[:, :, :].rearrange("p b n -> p (b n)")
        raw_w = sb("raw_w", [P, RING, UNIT])
        w_hi = sb("w_hi", [P, RING, UNIT], F32R)
        w_lo = sb("w_lo", [P, RING, UNIT], F32R)
        h_hi = sb("h_hi", [P, KT, TOK], F32R)
        h_lo = sb("h_lo", [P, KT, TOK], F32R)
        y_hi = sb("y_hi", [P, 2, TOK], F32R)
        y_lo = sb("y_lo", [P, 2, TOK], F32R)
        cst = sb("cst", [P, 3 * P])
        ident, upper, lower = cst[:, 0:P], cst[:, P:2 * P], cst[:, 2 * P:3 * P]
        ones = sb("ones", [P, P])
        cond = sb("cond", [P, 2, KT])
        par1 = sb("par1", [P, P])
        par2 = sb("par2", [P, 72])
        ss_mod = sb("ss_mod", [P, 2, 2, KT])
        ssq = sb("ssq", [P, 16])
        rstd = sb("rstd", [P, 16])
        half_neg = sb("half_neg", [P, 1])
        eps_col = sb("eps_col", [P, 1])
        NBIG = 26500
        big = sb("big", [P, NBIG])

        def carve(off, *dims):
            n = 1
            for d in dims:
                n *= d
            assert off + n <= NBIG, (off, dims)
            v = big[:, off:off + n]
            if len(dims) == 2:
                return v.rearrange("p (a b) -> p a b", a=dims[0])
            if len(dims) == 3:
                return v.rearrange("p (a b c) -> p a b c", a=dims[0], b=dims[1])
            if len(dims) == 4:
                return v.rearrange("p (a b c d) -> p a b c d", a=dims[0], b=dims[1], c=dims[2])
            return v

        x = carve(0, NT, D)
        yT = carve(5120, 16, TOK)
        mod_w = carve(15360, 2, D)
        acc = carve(17408, 2, D)
        gate = carve(19456, 2, D)
        wm = [carve(5120, 2, 1024), raw_w[:, 0:2, :], raw_w[:, 2:4, :], *(carve(5120 + 2048 * n, 2, 1024) for n in (1, 2, 3)),
              carve(23808, 2, 1024), carve(5120, 2, 1024)]
        xn = carve(5120 + 8192, 2, D)
        xT0 = carve(15360, KT, TOK)
        mod_sb = carve(21504, 2 * D)
        praw = carve(21504 + 2048, 2, P)
        praw3 = carve(23808, P)
        dft_g = carve(21504, 2, 512)
        dft_l = carve(22528, 10, P)
        sz_a = carve(23808, 2, TOK)
        ut = carve(5120 + 8 * TOK, 2, TOK)
        ub = carve(5120 + 8 * TOK + 1280, 2, 512)
        ab = carve(5120 + 8 * TOK + 2304, 5, 512)
        d02_sb = carve(0, 512)
        e01 = carve(512, 2, 256)
        cv_c = carve(0, 2, TOK)
        cv = carve(1280, 2, TOK)
        cc = carve(2560, 2, TOK)
        sz_b = carve(3840, 2, TOK)
        mod_row = carve(21504, 2 * D)[0:1]
        bias_rows = carve(20480, D)
        xn1 = carve(5120, 2, D)
        xT1 = carve(5120 + 2048, KT, TOK)
        gtmp = carve(25100, 2, 512)

        fin_g = carve(17408, D)
        sq_junk = carve(15360, 2, D)
        dtw_raw = carve(24000, KT, 64)

        at = [0]

        def take(*dims):
            n = 1
            for d in dims:
                n *= d
            v = carve(at[0], *dims)
            at[0] += n
            return v

        cvx = take(3, TOK)
        cvC = take(2, TOK)
        th = take(TOK)
        zth = take(2, 256)
        xb = take(NT, 384)
        sz = take(NT, 256)
        lfb = take(2, 8, P)
        cbm = take(2, NT, P)
        ea = take(2, 4, P)
        gm = take(2, 4, P)
        wt = take(2, 4, P)
        take(1024)
        xws = take(4, 512)
        hs = take(4, 512)
        hd = take(512)
        h0r = take(4, P)
        nst = take(512)
        yo = take(512)
        uu = take(2, 256)
        aa = take(2, 256)
        yn = take(2, 256)
        ysb = take(2, 2, P)
        GTW = 206
        GT = take(G, GTW)
        CPG = take(G, 16)
        gt = take(2, GTW)
        cp = take(2, 16)
        ssy = take(2)
        ry = take(2)
        tX, tNX, tNA, tU, tW, tLW, tC, tDT, tDA, tL = (carve(12400 + 320 * k, NT, 64) for k in range(10))
        tT = carve(12400 + 3200, NT, 64)
        lrow = carve(12400 + 3520, TOK)
        b_in, a_in, b_pm, a_pm = (carve(12400 + 4160 + 64 * k, 64) for k in range(4))
        d_in = carve(12400 + 4416, HEADS)

        landed = [sem(f"landed{i}") for i in range(RING)]
        hi_ready, lo_ready, unit_used = sem("hi_ready"), sem("lo_ready"), sem("unit_used")
        act_freed, dve_freed = sem("act_freed"), sem("dve_freed")
        cond_landed, par_landed = sem("cond_landed"), sem("par_landed")
        x_landed = [sem(f"x_landed{i}") for i in range(3)]
        wm_landed = [sem(f"wm_landed{i}") for i in range(8)]
        wm_used, mod_copied, mod_T, mod_ready = sem("wm_used"), sem("mod_copied"), sem("mod_T"), sem("mod_ready")
        cond_ready, ones_ready, par_T, par_ready = sem("cond_ready"), sem("ones_ready"), sem("par_T"), sem("par_ready")
        sq_done, ms_done, rstd_done, xn_done = sem("sq_done"), sem("ms_done"), sem("rstd_done"), sem("xn_done")
        xt_ready, xt_done, v_done, hh_done, h_ready = sem("xt_ready"), sem("xt_done"), sem("v_done"), sem("hh_done"), sem("h_ready")
        h_odd_ready = sem("h_odd_ready")
        fdone, ub_ready, gd_ready, q_ready, ab_act, ab_dve = sem("fdone"), sem("ub_ready"), sem("gd_ready"), sem("q_ready"), sem("ab_act"), sem("ab_dve")
        ld_ready, ya_done, dft_landed = sem("ld_ready"), sem("ya_done"), sem("dft_landed")
        conv_step, yb_done = sem("conv_step"), sem("yb_done")
        modw_landed, acc_step, red_ready, row_copied, row_stored, bias_landed = (
            sem("modw_landed"), sem("acc_step"), sem("red_ready"), sem("row_copied"), sem("row_stored"), sem("bias_landed"))
        bias_zeroed = sem("bias_zeroed")
        x_back, gate_landed = sem("x_back"), sem("gate_landed")
        yh_done, yl_done, y_even_used = sem("yh_done"), sem("yl_done"), sem("y_even_used")
        out_ready, out_evac, x_updated = sem("out_ready"), sem("out_evac"), sem("x_updated")
        p3_landed, stored = sem("p3_landed"), sem("stored")
        mod_step = sem("mod_step")
        exponent_ready = sem("exponent_ready")
        w_done, w_full = sem("w_done"), sem("w_full")
        cpg_ready, cp0_ready, dt_rows = sem("cpg_ready"), sem("cp0_ready"), sem("dt_rows")
        (dtw_landed, tot_copied, bc_landed, dtw_hi, dtw_lo, dtp_ready, cum_ready, lt_ready, tab_dve, tab_act, tables_ready) = (sem(n) for n in (
            "dtw_landed", "tot_copied", "bc_landed", "dtw_hi", "dtw_lo", "dtp_ready", "cum_ready", "lt_ready", "tab_dve", "tab_act", "tables_ready"))
        (proj_free, z_ready, zth_done, cen_done, tap_step, th_done, conv_done, grp_done) = (sem(n) for n in (
            "proj_free", "z_ready", "zth_done", "cen_done", "tap_step", "th_done", "conv_done", "grp_done"))
        (tr_ready, tok_done, h0_landed, h_T, hs0_done, cb_ready, cbm_done, xw_done, st_ready, st_done, hd_done) = (sem(n) for n in (
            "tr_ready", "tok_done", "h0_landed", "h_T", "hs0_done", "cb_ready", "cbm_done", "xw_done", "st_ready", "st_done", "hd_done"))
        (sc_ready, sc_done, small_stored, m_done, exp_done, g_done, y_ready, t_done, pool_step, u_done, a_step, gz_done) = (sem(n) for n in (
            "sc_ready", "sc_done", "small_stored", "m_done", "exp_done", "g_done", "y_ready", "t_done", "pool_step", "u_done", "a_step", "gz_done"))
        (sqy_done, msy_done, ry_done, yn_done, ytr_ready, yt_done, fg_landed, fin_done) = (sem(n) for n in (
            "sqy_done", "msy_done", "ry_done", "yn_done", "ytr_ready", "yt_done", "fg_landed", "fin_done"))
        y_stored = [sem(f"y_stored{i}") for i in range(2)]
        lfb_landed = [sem(f"lfb_landed{i}") for i in range(2)]

        block = ctx.enter_context(nc.Block())

        def split_hi(act, u, slot):
            act.wait_ge(landed[slot], 16 * (u // RING + 1) if isinstance(u, int) else u[1])
            un = u if isinstance(u, int) else u[0]
            if not isinstance(u, int) or u >= RING:
                act.wait_ge(unit_used, un - (RING - 1))
            act.activation(w_hi[:, slot, :], raw_w[:, slot, :], ACT.Copy).then_inc(hi_ready, 1)

        def split_lo(dve, u, slot):
            un = u if isinstance(u, int) else u[0]
            dve.wait_ge(hi_ready, un + 1)
            dve.tensor_tensor(w_lo[:, slot, :], raw_w[:, slot, :], w_hi[:, slot, :].bitcast(F32),
                              ALU.subtract).then_inc(lo_ready, 1)

        def unit(base, it, per, k):
            assert (base + k) % 1 == 0 and per % RING == 0
            if isinstance(it, int):
                return base + per * it + k
            return (per * it + (base + k), 4 * per * it + 16 * ((base + k) // RING + 1))

        def pair_view(pair):
            return PS[:, 2 * pair:2 * pair + 2, 0:HALF]

        def halves(v):
            return v.rearrange("p (s n) -> p s n", s=2)

        def h_wait(eng, layer, kt):
            eng.wait_ge(h_odd_ready if kt % 2 else h_ready, KT // 2 * layer + kt // 2 + 1)

        def channel_tile(pe, slot, pair, first=False):
            for kt in range(KT):
                if first:
                    h_wait(pe, 0, kt)
                ws = slice(kt * P, (kt + 1) * P)
                for n, (w, h) in enumerate(((w_hi, h_hi), (w_hi, h_lo), (w_lo, h_hi))):
                    for s in range(2):
                        mm = pe.matmul(PS[:, 2 * pair + s, 0:HALF], w[:, slot, ws], h[:, kt, s * HALF:(s + 1) * HALF],
                                       start=(kt == 0 and n == 0), stop=(kt == KT - 1 and n == 2))
            mm.then_inc(unit_used, 1)

        def norm_act(act, layer, xnb, xTb):
            junk = carve((20480, 17408)[layer], D)
            for t in range(NT + 2):
                if t < NT:
                    n = NT * layer + t
                    if layer == 0:
                        act.wait_ge(x_landed[t // 2], 16)
                    else:
                        act.wait_ge(x_updated, NT * 2 * (layer - 1) + NT + t + 1)
                    if t:
                        act.wait_ge(sq_done, n)
                    act.activation(junk, x[:, t, :], ACT.Square, accum_out=ssq[:, n:n + 1]).then_inc(sq_done, 1)
                if t >= 2:
                    m = NT * layer + t - 2
                    act.wait_ge(xt_ready, m + 1)
                    b = 4 + 2 * (t % 2)
                    act.activation(xTb[:, :, (t - 2) * P:(t - 1) * P],
                                   PS[:, b:b + 2, :].rearrange("p b (k n) -> p (b k) n", n=P),
                                   ACT.Copy).then_inc(xt_done, 1)

        def norm_pool(pool, layer):
            for t in range(NT):
                n = NT * layer + t
                pool.wait_ge(sq_done, n + 1)
                pool.tensor_scalar(rstd[:, n:n + 1], ssq[:, n:n + 1], 1.0 / D, EPS, ALU.mult, ALU.add).then_inc(ms_done, 1)
                pool.wait_ge(ms_done, n + 1)
                pool.tensor_tensor(rstd[:, n:n + 1], rstd[:, n:n + 1], half_neg[:, :], ALU.pow).then_inc(rstd_done, 1)

        def norm_dve(dve, layer, xnb):
            for t in range(NT):
                norm_dve_tile(dve, layer, xnb, t)

        def norm_dve_tile(dve, layer, xnb, t):
            n = NT * layer + t
            dve.wait_ge(rstd_done, n + 1)
            if t >= 2:
                dve.wait_ge(xt_ready, n - 1)
            dve.tensor_scalar(xnb[:, t % 2, :], x[:, t, :], rstd[:, n:n + 1], None, ALU.mult).then_inc(xn_done, 1)

        def norm_pe(pe, layer, xnb):
            for t in range(NT):
                norm_pe_tile(pe, layer, xnb, t)

        def norm_pe_tile(pe, layer, xnb, t):
            n = NT * layer + t
            pe.wait_ge(xn_done, n + 1)
            if t >= 2:
                pe.wait_ge(xt_done, n - 1)
            if t == 1 and layer == 1:
                pe.wait_ge(out_evac, 8)
            if t == 1 and layer == 0:
                pe.wait_ge(par_ready, 2)
            b = 4 + 2 * (t % 2)
            for k in range(KT):
                mm = pe.transpose(PS[:, b + k // 4, (k % 4) * P:(k % 4 + 1) * P], xnb[:, t % 2, k * P:(k + 1) * P], ident)
            mm.then_inc(xt_ready, 1)

        def h_dve(dve, layer, xTb):
            dve.wait_ge(xt_done, NT * (layer + 1) - 1)
            dve.wait_ge(mod_ready, 2 * (layer + 1))
            for k in range(KT):
                for c, (a, b) in enumerate(SEGS):
                    if k == 0 and c == 1:
                        dve.wait_ge(xt_done, NT * (layer + 1))
                    dve.tensor_scalar(xTb[:, k, a:b], xTb[:, k, a:b], ss_mod[:, 1, c, k:k + 1], ss_mod[:, 0, c, k:k + 1],
                                      ALU.mult, ALU.add).then_inc(v_done, 1)
                if k % 2:
                    dve.wait_ge(hh_done, KT * layer + k)
                    dve.tensor_tensor(h_lo[:, k - 1, :], xTb[:, k - 1, :], h_hi[:, k - 1, :].bitcast(F32),
                                      ALU.subtract).then_inc(h_ready, 1)

        def h_pool(pool, layer, xTb):
            for k in range(1, KT, 2):
                pool.wait_ge(hh_done, KT * layer + k + 1)
                pool.tensor_tensor(h_lo[:, k, :], xTb[:, k, :], h_hi[:, k, :].bitcast(F32), ALU.subtract).then_inc(h_odd_ready, 1)

        def h_act(act, layer, xTb):
            for k in range(KT):
                act.wait_ge(v_done, 2 * (KT * layer + k + 1))
                act.activation(h_hi[:, k, :], xTb[:, k, :], ACT.Copy).then_inc(hh_done, 1)

        RING_STEPS = (list(range(32)), list(range(8, 16)) + list(range(24, 32)))

        def y_ready_wait(eng, layer, kt):
            if layer == 0:
                if kt < 8:
                    eng.wait_ge(ya_done, kt + 1)
                else:
                    eng.wait_ge(yb_done, kt - 7)
            else:
                eng.wait_ge(y_back[4 if kt < 12 else 6 if kt < 14 else 7], 32 if kt < 12 else 16)

        def out_src(layer, q):
            return ye[q - 8] if layer == 1 and q < 12 else yT[:, q % 16, :]

        def out_ring_wait(eng, layer, q):
            r = RING_STEPS[layer].index(q)
            if r < 2:
                return
            last = RING_STEPS[layer][r - 2]
            if last % 2 == 0:
                eng.wait_ge(y_even_used, 16 * layer + last // 2 + 1)
            else:
                eng.wait_ge(unit_used, (OUT0, OUT1)[layer] + last // 2 + 1)

        def out_units(eng, split, layer, q):
            u0 = (OUT0, OUT1)[layer]
            if layer == 1 and q < 10:
                for v in (2 * (q - 8), 2 * (q - 8) + 1):
                    out_next_unit(eng, split, u0 + v)
            elif q % 2 == 1 and q > 1:
                out_next_unit(eng, split, u0 + q // 2 - 1)

        def y_split_act(act, layer, q):
            if q < 16:
                y_ready_wait(act, layer, q)
            if layer == 1 and q == 24:
                act.wait_ge(y_back[5], 16)
            out_ring_wait(act, layer, q)
            act.activation(y_hi[:, q % 2, :], out_src(layer, q), ACT.Copy).then_inc(yh_done, 1)

        def y_split_dve(dve, layer, q):
            dve.wait_ge(yh_done, 32 * layer + RING_STEPS[layer].index(q) + 1)
            dve.tensor_tensor(y_lo[:, q % 2, :], out_src(layer, q), y_hi[:, q % 2, :].bitcast(F32),
                              ALU.subtract).then_inc(yl_done, 1)

        def out_act(act, layer):
            for q in range(8 if layer else 2, 32):
                if q in RING_STEPS[layer]:
                    y_split_act(act, layer, q)
                out_units(act, split_hi, layer, q)

        def out_next_unit(eng, split, u):
            if u + RING < UNITS:
                split(eng, u + RING, u % RING)

        def residual(dve, layer, hh, t):
            u0 = (OUT0, OUT1)[layer]
            if hh == 0 and t == 0:
                dve.wait_ge(x_back, 32 * (layer + 1))
                dve.wait_ge(gate_landed, 32 * (layer + 1))
            if t < NT - 1:
                dve.wait_ge(out_ready, 8 * layer + 4 * hh + t + 1)
            else:
                dve.wait_ge(unit_used, u0 + 8 * (hh + 1))
            n = 10 * layer + 5 * hh + t
            if n >= 2:
                dve.wait_ge(x_updated, n - 1)
            dve.tensor_tensor(gtmp[:, t % 2, :], PS[:, (5 * hh + t) % 8, :], gate[:, int(t == NT - 1), 512 * hh:512 * hh + 512],
                              ALU.mult).then_inc(out_evac, 1)
            dve.wait_ge(out_evac, 10 * layer + 5 * hh + t + 1)
            xs = x[:, t, 512 * hh:512 * hh + 512]
            dve.tensor_tensor(xs, xs, gtmp[:, t % 2, :], ALU.add).then_inc(x_updated, 1)

        def out_dve(dve, layer):
            u0 = (OUT0, OUT1)[layer]
            for q in range(8 if layer else 2, 32):
                if q in RING_STEPS[layer]:
                    y_split_dve(dve, layer, q)
                if q == 16:
                    residual(dve, layer, 0, 0)
                    residual(dve, layer, 0, 1)
                if 17 <= q < 20:
                    residual(dve, layer, 0, q - 15)
                out_units(dve, split_lo, layer, q)
            for t in range(NT + 2):
                if t < NT:
                    residual(dve, layer, 1, t)
                if t >= 2 and layer == 0:
                    norm_dve_tile(dve, 1, xn1, t - 2)

        def out_tile(pe, layer, q, t):
            hh, kt, u = q // 16, q % 16, (OUT0, OUT1)[layer] + q // 2
            ys = [v[:, kt] for v in (h_hi, h_lo)] if layer == 1 and kt < 8 else [v[:, q % 2] for v in (y_hi, y_lo)]
            for n, (y, w) in enumerate(((ys[0], w_hi), (ys[0], w_lo), (ys[1], w_hi))):
                mm = pe.matmul(PS[:, (5 * hh + t) % 8, :], y[:, t * P:(t + 1) * P],
                               w[:, u % RING, (kt % 2) * 512:(kt % 2) * 512 + 512],
                               start=(kt == 0 and n == 0), stop=(kt == 15 and n == 2))
            return mm

        def out_pe(pe, layer):
            u0 = (OUT0, OUT1)[layer]
            for q in range(32):
                hh, kt = q // 16, q % 16
                if layer == 1 and q < 8:
                    out_tile(pe, 1, q, 4).then_inc(unit_used if kt % 2 else y_even_used, 1)
                    continue
                if kt % 2 == 0:
                    pe.wait_ge(lo_ready, u0 + q // 2 + 1)
                if q in RING_STEPS[layer]:
                    pe.wait_ge(yl_done, 32 * layer + RING_STEPS[layer].index(q) + 1)
                for t in range(NT):
                    if layer == 0 and q == 0 and t == 2:
                        pe.wait_ge(act_freed, 32)
                        pe.wait_ge(row_copied, 4)
                    if hh == 1 and kt == 0 and t >= 3:
                        pe.wait_ge(out_evac, 10 * layer + t - 2)
                    mm = out_tile(pe, layer, q, t)
                    if kt == 15 and t < NT - 1:
                        mm.then_inc(out_ready, 1)
                mm.then_inc(unit_used if kt % 2 else y_even_used, 1)

        def early_sp(sp, j):
            if j == 4:
                for v in (6, 7):
                    sp.wait_ge(lo_ready, OUT1 + v - 3)
                    out_load(sp, 1, v)
                for r in range(2):
                    sp.wait_ge(y_stored[r], 16 + 16 * 15)
                sp.wait_ge(cb_ready, 2 * G)
                sp.wait_ge(tr_ready, 5 * G)
                sp.wait_ge(conv_done, 4 * G)
                sp.dma_start(cvx, y_scr[:, 8:11, :]).then_inc(y_back[4], 16)
                sp.dma_start(th, y_scr[:, 11, :]).then_inc(y_back[4], 16)
                return
            if j == 0:
                sp.wait_ge(unit_used, OUT1)
                for r in range(2):
                    sp.wait_ge(y_stored[r], 16 + 16 * 10)
            sp.dma_start(h_lo[:, 2 * j:2 * j + 2, :].bitcast(F32), y_scr[:, 2 * j:2 * j + 2, :]).then_inc(y_back[j], 16)

        def early_act(act, k):
            act.wait_ge(y_back[k // 2], 16)
            act.activation(h_hi[:, k, :], h_lo[:, k, :].bitcast(F32), ACT.Copy).then_inc(eh_done, 1)

        def early_dve(dve, k):
            dve.wait_ge(eh_done, k + 1)
            dve.tensor_tensor(h_lo[:, k, :], h_lo[:, k, :].bitcast(F32), h_hi[:, k, :].bitcast(F32), ALU.subtract).then_inc(el_done, 1)

        def early_pe(pe, k):
            if k == 0:
                pe.wait_ge(proj_free, 9 * G)
            if k % 2 == 0:
                pe.wait_ge(lo_ready, OUT1 + k // 2 + 1)
            pe.wait_ge(el_done, k + 1)
            for t in range(4):
                out_tile(pe, 1, k, t)

        y_back = [sem(f"y_back{i}") for i in range(8)]
        ye = [cvx[:, 0, :], cvx[:, 1, :], cvx[:, 2, :], th]
        eh_done, el_done = sem("eh_done"), sem("el_done")

        def start_pe(pe):
            pe.wait_ge(par_landed, 16 * PAR_DMAS)
            pe.transpose(PS[:, 6, 0:P], praw[:, 0, :], ident)
            pe.transpose(PS[:, 6, P:P + 72], praw[0:72, 1, :], ident[0:72, 0:72]).then_inc(par_T, 1)
            pe.wait_ge(cond_ready, 1)
            for s in range(8):
                q, half = s // 2, s % 2
                pe.wait_ge(wm_landed[s], 16)
                for t in range(2):
                    for b in range(2):
                        mm = pe.matmul(PS[0:2, 2 * half + b, :], cond[:, :, 2 * q + t], wm[s][:, t, 512 * b:512 * b + 512],
                                       start=(q == 0 and t == 0), stop=(q == 3 and t == 1))
                mm.then_inc(wm_used, 1)
                if 1 <= s < NT + 1:
                    norm_pe_tile(pe, 0, xn, s - 1)

        def start_pe_mod_T(pe):
            pe.wait_ge(mod_copied, 2)
            pe.wait_ge(xt_done, NT)
            for j in range(16):
                mm = pe.transpose(PS[:, 4, 2 * j:2 * j + 2], mod_sb[0:2, j * P:(j + 1) * P], ident[0:2, 0:2])
            mm.then_inc(mod_T, 1)

        def fourier_pe(pe, i, first):
            for k in range(4):
                pe.wait_ge(lo_ready, 4 * i + k + 1)
                if not (first and k < 2):
                    pe.wait_ge(act_freed, 4 * i + k - 1)
                channel_tile(pe, k, k % 2, first and k == 0)
            pe.wait_ge(ub_ready, 2 * i + 2)
            if first:
                pe.wait_ge(dft_landed, 32)
            else:
                pe.wait_ge(ya_done, 2 * i)
            for b, src in enumerate((2, 3, 0, 1, None)):
                if b == 4:
                    pe.wait_ge(q_ready, i + 1)
                for kt in range(2):
                    lhs = ut[:, kt, LAT:TOK] if src is None else ub[:, kt, src * P:(src + 1) * P]
                    mm = pe.matmul(PS[:, 4 + b % 4, :], lhs, dft_g[:, kt, :], start=(kt == 0), stop=(kt == 1))
                mm.then_inc(gd_ready, 1)
            pe.wait_ge(ab_act, 3 * i + 3)
            pe.wait_ge(ab_dve, i + 1)
            for kt in range(2):
                for r in range(5):
                    o = PS[:, (5, 7)[kt], r * P:(r + 1) * P] if r < 4 else PS[:, (6, 4)[kt], 0:P]
                    cs, sn = (r, 4 + r) if r < 4 else (8, 9)
                    pe.matmul(o, ab[:, r, kt * P:(kt + 1) * P], dft_l[:, cs, :], start=True, stop=False)
                    mm = pe.matmul(o, ab[:, r, 256 + kt * P:256 + (kt + 1) * P], dft_l[:, sn, :], start=False, stop=True)
                mm.then_inc(ld_ready, 1)

        def fourier_act(act, i, first):
            for k in range(4):
                act.wait_ge(unit_used, 4 * i + k + 1)
                src = pair_view(k % 2)
                if k < 2:
                    if not first:
                        act.wait_ge(gd_ready, 5 * i)
                    act.activation(halves(ut[:, k, :]), src, ACT.Copy).then_inc(act_freed, 1)
                else:
                    if not first:
                        act.wait_ge(ya_done, 2 * i)
                    act.activation(halves(sz_a[:, k - 2, :]), src, ACT.Silu).then_inc(act_freed, 1)
                split_hi(act, unit(RING, i, 4, k), k)
            act.wait_ge(gd_ready, 5 * i + 1)
            if not first:
                act.wait_ge(ab_dve, i)
            act.activation(d02_sb, PS[:, 4, :], ACT.Copy).then_inc(q_ready, 1)
            if not first:
                act.wait_ge(ld_ready, 2 * i)
            for b, r in ((2, 0), (3, 2), (4, 4)):
                act.wait_ge(gd_ready, 5 * i + b + 1)
                act.activation(ab[:, r, :], PS[:, 4 + b % 4, :], ACT.Copy).then_inc(ab_act, 1)

        def fourier_dve(dve, i, first):
            ch = Chain(dve, fdone, 4 * i)
            for k in range(4):
                if k < 2:
                    dve.wait_ge(act_freed, 4 * i + k + 1)
                    if not first:
                        dve.wait_ge(gd_ready, 5 * i)
                        if k == 0:
                            dve.wait_ge(ub_ready, 2 * i)
                    lo2, hi2 = ut[:, k, 0:256], ut[:, k, 256:512]
                    ch.tick(dve.tensor_tensor(e01[:, k, :], lo2, hi2, ALU.add))
                    ch.tick(dve.tensor_tensor(ub[:, k, 256:512], lo2, hi2, ALU.subtract))
                    ch.sync()
                    dve.tensor_tensor(ub[:, k, 128:256], e01[:, k, 0:P], e01[:, k, P:256], ALU.subtract)
                    dve.tensor_tensor(ub[:, k, 0:P], e01[:, k, 0:P], e01[:, k, P:256], ALU.add).then_inc(ub_ready, 1)
                split_lo(dve, unit(RING, i, 4, k), k)
                if k == 2:
                    if first:
                        dve.wait_ge(bias_landed, 16)
                    mod_slot_dve(dve, i, i, first)
            dve.wait_ge(q_ready, i + 1)
            dve.wait_ge(gd_ready, 5 * i + 2)
            if not first:
                dve.wait_ge(ld_ready, 2 * i)
            C, S = slice(0, 256), slice(256, 512)
            dve.tensor_tensor(ab[:, 1, C], d02_sb[:, C], PS[:, 5, S], ALU.subtract)
            dve.tensor_tensor(ab[:, 1, S], d02_sb[:, S], PS[:, 5, C], ALU.add)
            dve.tensor_tensor(ab[:, 3, C], d02_sb[:, C], PS[:, 5, S], ALU.add)
            dve.tensor_tensor(ab[:, 3, S], d02_sb[:, S], PS[:, 5, C], ALU.subtract).then_inc(ab_dve, 1)
            for kt in range(2):
                dve.wait_ge(ld_ready, 2 * i + kt + 1)
                dve.wait_ge(act_freed, 4 * i + 4)
                yt = yT[:, bass.ds(2 * i + kt, 1), :]
                dve.tensor_tensor(yt[:, 0, 0:LAT].rearrange("p (m r) -> p r m", r=4),
                                  PS[:, (5, 7)[kt], :].rearrange("p (r m) -> p r m", r=4),
                                  sz_a[:, kt, 0:LAT].rearrange("p (m r) -> p r m", r=4), ALU.mult)
                dve.tensor_tensor(yt[:, 0, LAT:TOK], PS[:, (6, 4)[kt], 0:P], sz_a[:, kt, LAT:TOK], ALU.mult).then_inc(ya_done, 1)

        def mod_slot_dve(dve, n, tp, start):
            ch = Chain(dve, acc_step, 4 * n)
            if not start:
                ch.sync()
            dve.wait_ge(modw_landed, 16 * n + 16)
            for t in range(2):
                if t:
                    ch.sync()
                for c in range(2):
                    ch.tick(dve.scalar_tensor_tensor(out=acc[:, c, :], in0=mod_w[:, t, :],
                                                     scalar=cond[:, c, (bass.ds(2 * tp + t, 1) if not isinstance(tp, int) else slice(2 * tp + t, 2 * tp + t + 1))],
                                                     in1=bias_rows if start and t == 0 else acc[:, c, :],
                                                     op0=ALU.mult, op1=ALU.add))

        def mod_reduce_pe(pe, i, first):
            pe.wait_ge(acc_step, 16 * i + 16)
            if first:
                pe.wait_ge(ya_done, 8)
            else:
                pe.wait_ge(row_copied, i)
            for c in range(2):
                for b in range(2):
                    mm = pe.matmul(PS[0:1, 4 + 2 * c + b, :], ones[:, 0:1], acc[:, c, 512 * b:512 * b + 512], start=True, stop=True)
            mm.then_inc(red_ready, 1)

        def mod_pool(pool):
            pool.memset(bias_rows, 0.0).then_inc(bias_zeroed, 1)
            pool.wait_ge(bias_zeroed, 1)
            b_flat = A["b_mod"].rearrange("a n -> (a n)").rearrange("(o n) -> o n", o=1)

            def bias_load(chunk):
                pool.dma_start(bias_rows[0:1, :], b_flat[:, 2048 + 1024 * chunk:3072 + 1024 * chunk]).then_inc(bias_landed, 16)

            def row_store(chunk):
                pool.wait_ge(row_copied, chunk + 1)
                pool.dma_start(mod_scr[chunk].rearrange("c n -> (c n)").rearrange("(o n) -> o n", o=1), mod_row).then_inc(row_stored, 16)
            bias_load(0)
            for n in range(16):
                chunk, tp = n // 4, n % 4
                if n == 0:
                    pool.wait_ge(h_ready, KT // 2)
                    pool.wait_ge(h_odd_ready, KT // 2)
                else:
                    pool.wait_ge(acc_step, 4 * n)
                src = wm_src[0][:, :, 2048:3072] if chunk == 0 else wm_src[1][:, :, 1024 * (chunk - 1):1024 * chunk]
                pool.dma_start(mod_w, src[:, 2 * tp:2 * tp + 2, :]).then_inc(modw_landed, 16)
                if tp == 1 and chunk:
                    row_store(chunk - 1)
                if tp == 1 and chunk < 3:
                    bias_load(chunk + 1)
            row_store(3)

        CONV_DVE = 10
        MOD_SLOTS = (2, 4, 6, 7)
        C0 = 16

        def conv_pe(pe, i, first, last):
            for p in range(8):
                pe.wait_ge(lo_ready, C0 + 8 * i + p + 1)
                if p < 4:
                    pe.wait_ge(act_freed, C0 + 4 * i - 1 + p)
                else:
                    pe.wait_ge(dve_freed, 4 * i + p - 3)
                channel_tile(pe, p % 4, p % 2)
                if p == 1:
                    mod_reduce_pe(pe, i, first)

        def conv_act(act, i, first, last):
            for p in range(8):
                act.wait_ge(unit_used, C0 + 8 * i + p + 1)
                src = pair_view(p % 2)
                j = p % 2
                if p < 2:
                    if first:
                        act.wait_ge(ya_done, 8)
                    else:
                        act.wait_ge(dve_freed, 4 * i - 3 + j)
                    act.activation(halves(cv_c[:, j, :]), src, ACT.Copy).then_inc(act_freed, 1)
                if p == 3:
                    act.wait_ge(red_ready, i + 1)
                    if not first:
                        act.wait_ge(row_stored, 16 * i)
                    act.activation(mod_row, PSf[0:1, 2048:4096], ACT.Copy).then_inc(row_copied, 1)
                if p >= 6:
                    if not first:
                        act.wait_ge(yb_done, 2 * i)
                    act.activation(halves(sz_b[:, j, :]), src, ACT.Silu).then_inc(act_freed, 1)
                split_hi(act, unit(C0 + RING, i, 8, p), p % 4)

        def conv_dve(dve, i, first, last):
            ch = Chain(dve, conv_step, CONV_DVE * i)
            for p in range(8):
                j = p % 2
                src = pair_view(p % 2)

                def tap(k):
                    return par2[:, bass.ds(2 * i + (16 + 8 * k + j), 1)]
                rows = [b[:, j, :].rearrange("p (r n) -> p r n", n=64) for b in (cv, cc)]
                if p in (2, 3):
                    dve.wait_ge(unit_used, C0 + 8 * i + p + 1)
                    dve.wait_ge(act_freed, C0 + 4 * i + j + 1)
                    dve.tensor_tensor(halves(cv[:, j, :]), src, halves(cv_c[:, j, :]), ALU.mult).then_inc(dve_freed, 1)
                    dve.wait_ge(dve_freed, 4 * i + j + 1)
                    ch.tick(dve.tensor_scalar(cc[:, j, :], cv[:, j, :], tap(1), None, ALU.mult))
                    ch.sync()
                    ch.tick(dve.scalar_tensor_tensor(out=rows[1][:, :, 1:64], in0=rows[0][:, :, 0:63], scalar=tap(0),
                                                     in1=rows[1][:, :, 1:64], op0=ALU.mult, op1=ALU.add))
                    ch.sync()
                    ch.tick(dve.scalar_tensor_tensor(out=rows[1][:, :, 0:63], in0=rows[0][:, :, 1:64], scalar=tap(2),
                                                     in1=rows[1][:, :, 0:63], op0=ALU.mult, op1=ALU.add))
                    ch.sync()
                    a, b = LAT + 63, LAT + 64
                    ch.tick(dve.scalar_tensor_tensor(out=cc[:, j, b:b + 1], in0=cv[:, j, a:a + 1], scalar=tap(0),
                                                     in1=cc[:, j, b:b + 1], op0=ALU.mult, op1=ALU.add))
                    ch.tick(dve.scalar_tensor_tensor(out=cc[:, j, a:a + 1], in0=cv[:, j, b:b + 1], scalar=tap(2),
                                                     in1=cc[:, j, a:a + 1], op0=ALU.mult, op1=ALU.add))
                if p in (4, 5):
                    if p == 4:
                        ch.sync()
                    dve.wait_ge(unit_used, C0 + 8 * i + p + 1)
                    dve.tensor_tensor(halves(cc[:, j, :]), src, halves(cc[:, j, :]), ALU.mult).then_inc(dve_freed, 1)
                if p in (6, 7):
                    dve.wait_ge(dve_freed, 4 * i + 4)
                    dve.wait_ge(act_freed, C0 + 4 * i + 3 + j)
                    dve.tensor_tensor(yT[:, bass.ds(8 + 2 * i + j, 1), :][:, 0, :], cc[:, j, :], sz_b[:, j, :],
                                      ALU.mult).then_inc(yb_done, 1)
                split_lo(dve, unit(C0 + RING, i, 8, p), p % 4)
                if not last and p in MOD_SLOTS:
                    tp = MOD_SLOTS.index(p)
                    if tp == 0:
                        dve.wait_ge(red_ready, i + 1)
                        dve.wait_ge(bias_landed, 16 * i + 32)
                    mod_slot_dve(dve, 4 * i + 4 + tp, tp, tp == 0)
            assert ch.n == CONV_DVE

        def ssd_unit_src(g, k):
            if k < 4:
                col = (DI + 256 * g, DI + 256 * g + P, 2 * DI + P * g, 2 * DI + D + P * g)[k]
                return ssd_src[:, :, bass.ds(col, P)]
            return ssd_src[:, 4 * (k - 4):4 * (k - 4) + 4].rearrange("p k (g n) -> p k g n", n=64)[:, :, bass.ds(4 * g, 4)]

        def ssd_load(sp, g, k, slot):
            dst = raw_w[:, slot, :].rearrange("p (k n) -> p k n", n=P)
            if k >= 4:
                dst = raw_w[:, slot, :].rearrange("p (k g n) -> p k g n", k=4, n=64)
            sp.dma_start(dst, ssd_unit_src(g, k)).then_inc(landed[slot], 16)

        def state_view(t, d, g):
            return t[0, 0, d].rearrange("(g j q) p n -> (q p) g j n", j=2, q=2)[:, bass.ds(g, 1), :, :]

        def lfb_load(sp, g, c, slot):
            src = l_scr.rearrange("(g r) t -> g r t", r=8)[bass.ds(g, 1), :, c * P:(c + 1) * P]
            sp.dma_start(lfb[:, slot, :, :], src.partition_broadcast(P)).then_inc(lfb_landed[slot], 16)

        def table(tab, off, n):
            return tab[:, 0:200].rearrange("p (c k) -> p c k", c=NT)[:, :, off:off + n]

        def all_tables(off, n):
            return GT[:, :, 0:200].rearrange("p g (c k) -> p c g k", c=NT)[:, :, :, off:off + n]
        EL, DTO, WDT, DEC, DLT, NLB = 0, 8, 16, 24, 32, 36

        def perm(v):
            return v.rearrange("p (d g h) -> p g d h", d=2, g=G)

        def by_group(v):
            return v.rearrange("p c (g r) -> p c g r", g=G)

        def table_sp(sp):
            sp.dma_start(dtw_raw, ssd_src[:, :, SSD_IN - 64:SSD_IN]).then_inc(dtw_landed, 16)

        def params_sp(sp):
            sp.wait_ge(acc_step, 64)
            sp.dma_start(b_in, A["ssd_dt_bias"][0].rearrange("d h -> (d h)").partition_broadcast(P)).then_inc(bc_landed, 16)
            sp.dma_start(a_in, A["ssd_a_log"][0].rearrange("d h -> (d h)").partition_broadcast(P)).then_inc(bc_landed, 16)
            sp.dma_start(d_in, A["ssd_d"][0].partition_broadcast(P)).then_inc(bc_landed, 16)

        wd = [y[:, :, :].rearrange("p a b -> p (a b)")[:, 0:512].rearrange("p (k g r) -> p k g r", k=KT, g=G) for y in (y_hi, y_lo)]

        def dt_weights_act(act):
            act.wait_ge(unit_used, IN1)
            act.wait_ge(dtw_landed, 16)
            src = dtw_raw.rearrange("p k (d g h) -> p k d g h", d=2, g=G)
            for d in range(2):
                act.activation(wd[0][:, :, :, 4 * d:4 * d + 4], src[:, :, d], ACT.Copy).then_inc(dtw_hi, 1)

        def dt_weights_dve(dve):
            dve.wait_ge(unit_used, IN1)
            for d in range(2):
                dve.wait_ge(dtw_hi, d + 1)
                dve.tensor_tensor(wd[1][:, :, :, 4 * d:4 * d + 4], dtw_raw.rearrange("p k (d g h) -> p k d g h", d=2, g=G)[:, :, d],
                                  wd[0][:, :, :, 4 * d:4 * d + 4].bitcast(F32), ALU.subtract).then_inc(dtw_lo, 1)

        def conv_params_dve(dve):
            dve.wait_ge(x_updated, 10)
            p1 = par1[:, :].rearrange("p (k t) -> p k t", k=4)
            CPv = CPG.rearrange("p g (i k) -> p i k g", i=4)
            for i in range(4):
                src = p1[:, :, i:16:2] if i < 2 else p1[:, :, 16 + 8 * (i - 2):24 + 8 * (i - 2)]
                e = dve.tensor_copy(CPv[:, i], src)
            e.then_inc(cpg_ready, 1)

        def dt_pe(pe, stage_no):
            if stage_no == 0:
                pe.wait_ge(dtw_lo, 2)
                pe.wait_ge(xt_done, 2 * NT)
                for k in range(KT):
                    for n, (w, h) in enumerate(((0, h_hi), (0, h_lo), (1, h_hi))):
                        for s in range(2):
                            mm = pe.matmul(PS[0:64, 4 + s, 0:HALF], wd[w][:, k].rearrange("p g r -> p (g r)"),
                                           h[:, k, s * HALF:(s + 1) * HALF], start=(k == 0 and n == 0), stop=(k == KT - 1 and n == 2))
                mm.then_inc(dtp_ready, 1)
            elif stage_no == 1:
                pe.wait_ge(dt_rows, 1)
                for t in range(NT):
                    mm = pe.transpose(PS[:, 6, 64 * t:64 * t + 64], lrow[0:64, t * P:(t + 1) * P], ident[0:64, 0:64])
                mm.then_inc(dtp_ready, 1)
            elif stage_no == 2:
                pe.wait_ge(tab_dve, 13)
                o = PS[:, 4, 0:320].rearrange("p (c g d h) -> p c g d h", c=NT, g=G, d=2)
                da = tDA.rearrange("p c (g d h) -> p c g d h", g=G, d=2)
                pe.matmul(o[:, :, :, 0], upper, da[:, :, :, 0], start=True, stop=True)
                pe.matmul(o[:, :, :, 1], lower, da[:, :, :, 1], start=True, stop=True)
                pe.matmul(PS[:, 5, 0:320], ones[:, :], tDA.rearrange("p c r -> p (c r)"), start=True, stop=True).then_inc(cum_ready, 1)
            else:
                pe.wait_ge(tab_act, 4)
                for t in range(NT):
                    mm = pe.transpose(PSf[0:64, 3072 + t * P:3072 + (t + 1) * P], tL[:, t, :], ident)
                mm.then_inc(lt_ready, 1)

        def dt_act(act, stage_no):
            if stage_no == 0:
                act.wait_ge(dtp_ready, 1)
                act.activation(halves(lrow[0:64, :]), PS[0:64, 4:6, 0:HALF], ACT.Copy).then_inc(dt_rows, 1)
            elif stage_no == 1:
                act.wait_ge(bc_landed, 48)
                act.activation(a_pm.rearrange("p (g d h) -> p g d h", g=G, d=2)[:, :, 0, :], perm(a_in)[:, :, 0, :], ACT.Exp)
                act.activation(a_pm.rearrange("p (g d h) -> p g d h", g=G, d=2)[:, :, 1, :], perm(a_in)[:, :, 1, :], ACT.Exp).then_inc(tab_act, 1)
                act.wait_ge(tab_dve, 4)
                act.activation(tU, tNA, ACT.Exp).then_inc(tab_act, 1)
                act.wait_ge(tab_dve, 6)
                act.activation(tLW, tW, ACT.Ln).then_inc(tab_act, 1)
            elif stage_no == 2:
                act.wait_ge(cum_ready, 1)
                act.activation(tL, PS[:, 4, 0:320].rearrange("p (c r) -> p c r", c=NT), ACT.Copy).then_inc(tab_act, 1)
                act.wait_ge(tab_dve, 14)
                act.activation(tX, tT, ACT.Exp).then_inc(tab_act, 1)
            else:
                act.wait_ge(lt_ready, 1)
                act.activation(lrow[0:64, :], PSf[0:64, 3072:3072 + TOK], ACT.Copy).then_inc(yt_done, 1)
                act.activation(all_tables(EL, 8), by_group(tL), ACT.Exp)
                act.wait_ge(tot_copied, 1)
                act.activation(all_tables(DEC, 8), by_group(tNX), ACT.Exp).then_inc(tab_act, 1)

        def dt_dve(dve, stage_no):
            ch = Chain(dve, tab_dve, (0, 0, 13, 14)[stage_no])
            if stage_no == 1:
                dve.wait_ge(bc_landed, 48)
                for d in range(2):
                    last = dve.tensor_copy(b_pm.rearrange("p (g d h) -> p g d h", g=G, d=2)[:, :, d, :], perm(b_in)[:, :, d, :])
                ch.tick(last)
                ch.sync()
                dve.wait_ge(dtp_ready, 2)
                ch.tick(dve.tensor_tensor(tX, PS[:, 6, 0:320].rearrange("p (c r) -> p c r", c=NT),
                                          b_pm.unsqueeze(1).to_broadcast([P, NT, 64]), ALU.add))
                ch.sync()
                ch.tick(dve.tensor_scalar(tNX, tX, -1.0, None, ALU.mult))
                ch.sync()
                ch.tick(dve.tensor_tensor(tNA, tX, tNX, ALU.min))
                ch.tick(dve.tensor_scalar(tC, tX, 0.0, None, ALU.max))
                dve.wait_ge(tab_act, 2)
                ch.tick(dve.tensor_scalar(tW, tU, 1.0, None, ALU.add))
                ch.sync()
                ch.tick(dve.tensor_scalar(tNA, tW, -1.0, None, ALU.add))
                ch.sync()
                ch.tick(dve.tensor_tensor(tNA, tU, tNA, ALU.subtract))
                ch.tick(dve.reciprocal(tT, tW))
                ch.sync()
                ch.tick(dve.tensor_tensor(tNA, tNA, tT, ALU.mult))
                dve.wait_ge(tab_act, 3)
                ch.sync()
                ch.tick(dve.tensor_tensor(tNA, tNA, tLW, ALU.add))
                ch.sync()
                ch.tick(dve.tensor_tensor(tDT, tNA, tC, ALU.add))
                ch.sync()
                ch.tick(dve.scalar_tensor_tensor(out=tDA, in0=tDT, scalar=-1.0, in1=a_pm.unsqueeze(1).to_broadcast([P, NT, 64]),
                                                 op0=ALU.mult, op1=ALU.mult))
            elif stage_no == 2:
                dve.wait_ge(tab_act, 4)
                ch.tick(dve.tensor_tensor(tT, PS[:, 5, 0:320].rearrange("p (c r) -> p c r", c=NT), tL, ALU.subtract))
                dve.tensor_copy(tNX, PS[:, 5, 0:320].rearrange("p (c r) -> p c r", c=NT)).then_inc(tot_copied, 1)
            elif stage_no == 3:
                dve.tensor_copy(GT[:, :, 200:204], d_in.rearrange("p (g h) -> p g h", g=G))
                dve.tensor_scalar(GT[:, :, 204:206], par2[:, 40:56].rearrange("p (g j) -> p g j", g=G), 0.5, None, ALU.mult)
                dve.tensor_copy(all_tables(DTO, 8), by_group(tDT))
                lv = tL.rearrange("p c (g d h) -> p c g d h", g=G, d=2)
                for c in range(NT):
                    dve.tensor_tensor(all_tables(DLT, 4)[:, c], lv[:, c, :, 1], lv[:, c, :, 0], ALU.subtract)
                for c in range(NT):
                    dve.tensor_scalar(all_tables(NLB, 4)[:, c], lv[:, c, :, 1], -1.0, None, ALU.mult)
                dve.wait_ge(tab_act, 5)
                dve.tensor_tensor(all_tables(WDT, 8), by_group(tDT), by_group(tX), ALU.mult).then_inc(tables_ready, 1)

        def dt_sp(sp, stage_no):
            if stage_no == 3:
                for d in range(2):
                    sp.dma_start(h0r[:, 2 * d:2 * d + 2, :], state_view(A["state_ssm"], d, 0)[:, 0]).then_inc(h0_landed, 16)
                sp.wait_ge(yt_done, 1)
                sp.dma_start(l_scr, lrow[0:64, :]).then_inc(small_stored, 16)
                sp.wait_ge(small_stored, 16)
                for c in range(2):
                    lfb_load(sp, 0, c, c)

        def groups_copy(pool, g_ssd, g_proj, ps, pp):
            last = None
            if g_ssd is not None:
                last = pool.tensor_copy(gt[:, ps, :].unsqueeze(1), GT[:, bass.ds(g_ssd, 1), :])
            if g_proj is not None:
                last = pool.tensor_copy(cp[:, pp, :].unsqueeze(1), CPG[:, bass.ds(g_proj, 1), :])
            return last

        TAP_RANGES = {0: ((0, 0, HALF - 1), (0, HALF - 1, HALF), (1, HALF, LAT - 1), (1, LAT, TOK - 1)),
                      2: ((0, 1, HALF), (1, HALF, HALF + 1), (1, HALF + 1, LAT), (1, LAT + 1, TOK))}

        BODY = {
            "PE": """
                P00 CB0 P01 T0 P02 T1 T2 P03 T3 T4 P04 P05 P06 CB1 H0 S0 P07 P10 P11 P12 P13 P14 P15 P16 P17 S1 P20 S2 SC0 P21 P22
                P23 P24 Y0 Y1 P25 P26 P27 P30 P31 P32 P33 P34 P35 YT0 P36 P37 Y2 Z00 Z01 YT1 Z10 Y3 Z11 Z20 Z21 YT2 Z30 Y4 Z31 Z40
                YT3 Z41 YT4
                """.split(),
            "ACT": """
                tok0 tok1 tok2 exp0 tok3 tok4 exp1 hev0 hi0 cen0 exp2 tanh0 exp3 hi1 cen1 scev0 tanh1 exp4 hi2 cen2 sq0 yn0 ytev0
                tanh2 cen3 sq1 hi3 yn1 tanh3 ztanh0 ytev1 sq2 ztanh1 yn2 ztanh2 ytev2 sq3 yn3 sq4 ztanh3 yn4 ytev3 ztanh4 hi4 ytev4
                hi5
                """.split(),
            "DVE": """
                M0 cbm0 M1 G0 cbm1 G1 M2 hup0 tap0 M3 fin0 lo0 hup1 lo1 tap1 hup2 fin1 G2 yt0 M4 G3 ya0 lo2 yt1 tap2 ya1 fin2 tap3
                yt2 G4 sz0 lo3 ya2 yt3 fin3 sz1 sz2 ya3 ya4 sz3 sz4 lo4 lo5
                """.split(),
            "Pool": """
                W0 xw0 W1 grp0 hd0 W2 xw1 W3 hd1 xw2 xw3 hd2 W4 u0 rs0 u1 rs1 u2 rs2 u3 u4 rs3 rs4
                """.split(),
            "SP": """
                lfb0 lfb1 lfb2 lfb3 ld0 ld1 nst0 lfb4 ld2 yst0 yst1 ld3 yst2 yst3 yst4 ld4 ld5
                """.split(),
        }
        LAST = {
            "PE": """
                T0 T1 T2 T3 T4 H0 CB0 CB1 S0 S1 S2 O0 SC0 Y0 O1 O2 Y1 YT0 O3 Y2 O4 YT1 O5 Y3 YT2 O6 Y4 O7 YT3 YT4
                """.split(),
            "ACT": """
                tok0 tok1 tok2 tok3 tok4 hev0 exp0 exp1 eh0 eh1 eh2 eh3 scev0 eh4 eh5 exp2 sq0 eh6 eh7 yn0 ytev0 exp3 sq1 yn1 ytev1
                exp4 sq2 yn2 ytev2 sq3 sq4 yn3 yn4 ytev3 ytev4
                """.split(),
            "DVE": """
                M0 cbm0 hup0 cbm1 M1 hup1 el0 el1 hup2 G0 el2 M2 yt0 el3 G1 ya0 G2 M3 yt1 el4 el5 G3 ya1 yt2 el6 el7 M4 ya2 G4 yt3
                ya3 ya4
                """.split(),
            "Pool": """
                xw0 hd0 xw1 hd1 xw2 hd2 xw3 W0 W1 W2 u0 W3 rs0 W4 u1 rs1 u2 rs2 u3 u4 rs3 rs4
                """.split(),
            "SP": """
                ey0 ey1 ey2 ey3 ey4 lfb0 lfb1 nst0 lfb2 yst0 yst1 yst2 yst3 yst4
                """.split(),
        }
        PROLOGUE = """
        P00 P01 P02 P03 P04 P05 P06 P07 cen0 tap0 hi0 lo0 ld0 P10 P11 P12 P13 P14 P15 P16 P17 tanh0 fin0 pdt0 dt0 cen1 tap1 hi1 lo1 ld1
        P20 P21 P22 pdt1 P23 P24 P25 P26 P27 tanh1 fin1 dt1 cen2 tap2 hi2 lo2 ld2 P30 P31 P32 P33 P34 pdt2 P35 P36 P37 pdt3
        dt2 tanh2 fin2 cen3 tap3 hi3 lo3 ld3 dt3 Z00 Z01 Z10 Z11 tanh3 fin3 ztanh0 sz0 ztanh1 sz1 Z20 Z21 ztanh2 sz2 Z30 Z31 ztanh3 sz3
        Z40 Z41 ztanh4 sz4 hi4 lo4 ld4 hi5 lo5 ld5
        """.split()

        class Body:

            def __init__(self, i, par, ssd=True, proj=True):
                self.i, self.par, self.ssd, self.proj = i, par, ssd, proj
                self.g = 2 * i + par
                self.n = self.g + 1
                self.np = (par + 1) % 2
                self.static = isinstance(i, int)

            def steps(self, engine):
                for step in PROLOGUE if not self.ssd else BODY[engine] if self.proj else LAST[engine]:
                    name = step.rstrip("0123456789")
                    yield name, [int(d) for d in step[len(name):]]

            def unit(self, k):
                return 12 * self.i + (IN1 + 6 * (self.par + 1) + k), (6 * (self.par + 1) + k) % RING

            def split_unit(self, k):
                c = IN1 + 6 * (self.par + 1) + k + 4
                if self.static:
                    return c + 12 * self.i
                return (12 * self.i + c, 48 * self.i + 16 * (c // RING + 1))

            def count2(self, c):
                m = 5 * self.par + c
                return 5 * self.i + m // 2, m % 2

        def ssd_pe(pe, B):
            g, n = B.g, B.n
            b0 = 5 * g
            for ev, a in B.steps("PE"):
                k = a[0]
                if ev == "O":
                    early_pe(pe, k)
                    continue
                if ev == "pdt":
                    dt_pe(pe, k)
                    continue
                if ev == "P":
                    u, slot = B.unit(k)
                    pair, kt = (B.np + k) % 2, a[1]
                    if kt == 0:
                        pe.wait_ge(lo_ready, u + 1)
                        if not (B.static and 9 * n + k < 2):
                            pe.wait_ge(proj_free, 9 * n + k - 1)
                        else:
                            pe.wait_ge(*((out_evac, 10) if k == 0 else (mod_ready, 4)))
                    if B.static and 9 * n + k == 0:
                        h_wait(pe, 1, kt)
                    ws = slice(kt * P, (kt + 1) * P)
                    for j, (w, h) in enumerate(((w_hi, h_hi), (w_hi, h_lo), (w_lo, h_hi))):
                        for s in range(2):
                            mm = pe.matmul(PS[:, 2 * pair + s, 0:HALF], w[:, slot, ws], h[:, kt, s * HALF:(s + 1) * HALF],
                                           start=(kt == 0 and j == 0), stop=(kt == KT - 1 and j == 2))
                    if kt == KT - 1:
                        mm.then_inc(unit_used, 1)
                elif ev == "Z":
                    t, half = a
                    u, slot = B.unit(4)
                    pair = (B.np + 4 + t) % 2
                    if t == 0 and half == 0:
                        pe.wait_ge(lo_ready, u + 2)
                    if half == 0:
                        pe.wait_ge(proj_free, 9 * n + 3 + t)
                    for kt in range(4 * half, 4 * half + 4):
                        for j, (h, w) in enumerate(((h_hi, w_hi), (h_hi, w_lo), (h_lo, w_hi))):
                            mm = pe.matmul(PS[:, 2 * pair, 0:256], h[:, kt, t * P:(t + 1) * P],
                                           w[:, slot + kt // 4, 256 * (kt % 4):256 * (kt % 4) + 256],
                                           start=(kt == 0 and j == 0), stop=(kt == KT - 1 and j == 2))
                    if half == 1:
                        mm.then_inc(*((z_ready, 1) if t < NT - 1 else (unit_used, 2)))
                elif ev == "T":
                    if k == 0:
                        pe.wait_ge(conv_done, 4 * g + 4)
                        pe.wait_ge(yt_done, b0 + 1)
                    if k >= 2:
                        pe.wait_ge(tok_done, b0 + k - 1)
                    for j in range(3):
                        mm = pe.transpose(PS[:, 4 + k % 2, j * P:(j + 1) * P], cvx[:, j, k * P:(k + 1) * P], ident)
                    mm.then_inc(tr_ready, 1)
                elif ev == "H":
                    pe.wait_ge(h0_landed, 32 * g + 32)
                    for j in range(4):
                        mm = pe.transpose(PS[:, 6, j * P:(j + 1) * P], h0r[:, j, :], ident)
                    mm.then_inc(h_T, 1)
                elif ev == "CB":
                    if k == 1:
                        pe.wait_ge(tok_done, b0 + 4)
                    for c in range(4) if k == 0 else (4,):
                        o = PS[:, 7, c * P:(c + 1) * P] if k == 0 else PS[:, 5, 0:P]
                        mm = pe.matmul(o, cvx[:, 2, c * P:(c + 1) * P], cvC[:, B.par, c * P:(c + 1) * P], start=True, stop=True)
                    mm.then_inc(cb_ready, 1)
                elif ev == "S":
                    bank = (4, 5, 4)[k]
                    pe.wait_ge(xw_done, 4 * g + k + 1)
                    if k == 0:
                        pe.wait_ge(tok_done, b0 + 5)
                    elif k == 1:
                        pe.wait_ge(cbm_done, 2 * g + 2)
                    else:
                        pe.wait_ge(st_done, 3 * g + 1)
                    pe.matmul(PS[:, bank, 0:256], xb[:, k, 256:384], xws[:, k, 0:256], start=True, stop=True)
                    pe.matmul(PS[:, bank, 256:512], xb[:, 3 - k, 256:384], xws[:, k, 256:512], start=True, stop=True).then_inc(st_ready, 1)
                elif ev == "SC":
                    pe.wait_ge(xw_done, 4 * g + 4)
                    pe.wait_ge(st_done, 3 * g + 2)
                    for j in range(4):
                        mm = pe.matmul(PS[:, 5, j * P:(j + 1) * P], xws[:, 3, j * P:(j + 1) * P], xb[:, 4, 256:384], start=True, stop=True)
                    mm.then_inc(sc_ready, 1)
                elif ev == "Y":
                    r = (B.par + k) % 2
                    bo, bd = (6, 7) if k % 2 == 0 else (4, 5)
                    if k == 0:
                        pe.wait_ge(st_done, 3 * g + 3)
                        pe.wait_ge(hs0_done, g + 1)
                    elif k == 1:
                        pe.wait_ge(sc_done, g + 1)
                    else:
                        pe.wait_ge(yt_done, b0 + k)
                    if k < 4:
                        cc_ = cvC[:, B.par, k * P:(k + 1) * P]
                        pe.matmul(PS[:, bo, 0:256], cc_, hs[:, k, 0:256], start=True, stop=True)
                        pe.matmul(PS[:, bo, 256:512], cc_, hs[:, 3 - k, 256:512], start=True, stop=True)
                    pe.wait_ge(g_done, b0 + k + 1)
                    for h in range(4):
                        mm = pe.matmul(PS[:, bd, 64 * h:64 * h + 64], gm[:, r, h, :], xb[:, k, 64 * h:64 * h + 64], start=True, stop=True)
                    mm.then_inc(y_ready, 1)
                elif ev == "YT":
                    r = (B.par + k) % 2
                    pe.wait_ge(yn_done, b0 + k + 1)
                    for j in range(2):
                        mm = pe.transpose(PS[:, (6, 4)[k % 2], j * P:(j + 1) * P], yn[:, r, j * P:(j + 1) * P], ident)
                    mm.then_inc(ytr_ready, 1)

        def ssd_act(act, B):
            g, n = B.g, B.n
            b0 = 5 * g
            if B.static and n == 0:
                act.wait_ge(y_stored[0], 16)
                act.wait_ge(y_stored[1], 16)
                act.wait_ge(cp0_ready, 1)
            else:
                act.wait_ge(grp_done, n)
            for ev, a in B.steps("ACT"):
                k = a[0]
                if ev == "eh":
                    early_act(act, k)
                    continue
                if ev == "dt":
                    dt_act(act, k)
                    continue
                pair = (B.np + k) % 2
                src = pair_view(pair)
                cpn = cp[:, B.np, :]
                cv_ = cvx[:, k, :] if k < 3 else cvC[:, B.np, :]
                if ev == "cen":
                    u, _ = B.unit(k)
                    act.wait_ge(unit_used, u + 1)
                    if not (B.static and n == 0):
                        act.wait_ge(*((cb_ready, 2 * n) if k == 2 else (tr_ready, 5 * n)))
                    act.activation(halves(cv_), src, ACT.Identity, bias=cpn[:, 4 * k + 3:4 * k + 4], scale=cpn[:, 4 * k + 1:4 * k + 2]).then_inc(cen_done, 1)
                elif ev == "tanh":
                    act.wait_ge(proj_free, 9 * n + k + 1)
                    if not (B.static and 4 * n + k == 0):
                        act.wait_ge(conv_done, 4 * n + k)
                    act.activation(th, cv_, ACT.Tanh).then_inc(th_done, 1)
                elif ev == "ztanh":
                    if k < NT - 1:
                        act.wait_ge(z_ready, 4 * n + k + 1)
                    else:
                        act.wait_ge(unit_used, B.unit(4)[0] + 2)
                    if k >= 2:
                        act.wait_ge(proj_free, 9 * n + 4 + k - 1)
                    zs = PS[:, 2 * ((B.np + 4 + k) % 2), 0:256]
                    act.activation(zth[:, k % 2, :], zs, ACT.Tanh, scale=0.5).then_inc(zth_done, 1)
                elif ev == "hi":
                    split_hi(act, B.split_unit(k), B.unit(k)[1])
                elif ev == "tok":
                    act.wait_ge(tr_ready, b0 + k + 1)
                    act.activation(xb[:, k, :], PS[:, 4 + k % 2, 0:384], ACT.Copy).then_inc(tok_done, 1)
                elif ev == "hev":
                    act.wait_ge(h_T, g + 1)
                    act.activation(hs[:, 0, :], PS[:, 6, :], ACT.Copy).then_inc(hs0_done, 1)
                elif ev == "exp":
                    act.wait_ge(m_done, b0 + k + 1)
                    r = (B.par + k) % 2
                    for h in range(4):
                        e = act.activation(ea[:, r, h, :], ea[:, r, h, :], ACT.Exp, bias=table(gt[:, B.par, :], NLB, 4)[:, k, h:h + 1])
                    e.then_inc(exp_done, 1)
                elif ev == "scev":
                    act.wait_ge(sc_ready, g + 1)
                    act.wait_ge(small_stored, 32 * g + 16)
                    act.activation(nst, PS[:, 5, :], ACT.Copy).then_inc(sc_done, 1)
                elif ev == "sq":
                    r = (B.par + k) % 2
                    act.wait_ge(gz_done, b0 + k + 1)
                    act.activation(yn[:, r, :], aa[:, r, :], ACT.Square, scale=1.0 / 32, accum_out=ssy[:, r:r + 1]).then_inc(sqy_done, 1)
                elif ev == "yn":
                    r = (B.par + k) % 2
                    act.wait_ge(ry_done, b0 + k + 1)
                    act.activation(yn[:, r, :], aa[:, r, :], ACT.Copy, scale=ry[:, r:r + 1]).then_inc(yn_done, 1)
                elif ev == "ytev":
                    cnt, r = B.count2(k)
                    act.wait_ge(ytr_ready, b0 + k + 1)
                    act.wait_ge(y_stored[r], 16 * cnt + 16)
                    for j in range(2):
                        e = act.activation(ysb[:, r, j, :], PS[:, (6, 4)[k % 2], j * P:(j + 1) * P], ACT.Copy,
                                           scale=gt[:, B.par, 204 + j:205 + j])
                    e.then_inc(yt_done, 1)

        def ssd_dve(dve, B):
            g, n = B.g, B.n
            b0 = 5 * g
            if B.static and n == 0:
                dve.wait_ge(cp0_ready, 1)
            else:
                dve.wait_ge(grp_done, n)
            tab = gt[:, B.par, :]

            def heads(off, nh, c):
                return table(tab, off, nh)[:, c, :].unsqueeze(2).to_broadcast([P, nh, 64])
            for ev, a in B.steps("DVE"):
                k = a[0]
                if ev == "el":
                    early_dve(dve, k)
                    continue
                if ev == "dt":
                    dt_dve(dve, k)
                    continue
                pair = (B.np + k) % 2
                r = (B.par + k) % 2
                if ev == "tap":
                    cpn = cp[:, B.np, :]
                    cv_ = cvx[:, k, :] if k < 3 else cvC[:, B.np, :]
                    src = pair_view(pair)
                    dve.wait_ge(cen_done, 4 * n + k + 1)
                    for side, off in ((0, 1), (2, -1)):
                        if side == 2:
                            dve.wait_ge(tap_step, 4 * n + k + 1)
                        for half, a, b in TAP_RANGES[side]:
                            ins = dve.scalar_tensor_tensor(out=cv_[:, a + off:b + off], in0=src[:, half, a - HALF * half:b - HALF * half],
                                                           scalar=cpn[:, 4 * k + side:4 * k + side + 1],
                                                           in1=cv_[:, a + off:b + off], op0=ALU.mult, op1=ALU.add)
                        ins.then_inc(proj_free if side == 2 else tap_step, 1)
                elif ev == "fin":
                    cv_ = cvx[:, k, :] if k < 3 else cvC[:, B.np, :]
                    dve.wait_ge(th_done, 4 * n + k + 1)
                    dve.scalar_tensor_tensor(out=cv_, in0=th, scalar=1.0, in1=cv_, op0=ALU.add, op1=ALU.mult).then_inc(conv_done, 1)
                elif ev == "sz":
                    zs = PS[:, 2 * ((B.np + 4 + k) % 2), 0:256]
                    dve.wait_ge(zth_done, 5 * n + k + 1)
                    if not (B.static and n == 0):
                        dve.wait_ge(gz_done, 5 * n - 5 + k + 1)
                    dve.scalar_tensor_tensor(out=sz[:, k, :], in0=zth[:, k % 2, :], scalar=1.0, in1=zs,
                                             op0=ALU.add, op1=ALU.mult).then_inc(proj_free, 1)
                elif ev == "lo":
                    split_lo(dve, B.split_unit(k), B.unit(k)[1])
                elif ev == "M":
                    cnt, slot = B.count2(k)
                    dve.wait_ge(lfb_landed[slot], 16 * cnt + 16)
                    if k >= 2:
                        dve.wait_ge(g_done, b0 + k - 1)
                    for h in range(4):
                        e = dve.scalar_tensor_tensor(out=ea[:, r, h, :], in0=lfb[:, slot, h, :], scalar=table(tab, DLT, 4)[:, k, h:h + 1],
                                                     in1=lfb[:, slot, 4 + h, :], op0=ALU.add, op1=ALU.min)
                    e.then_inc(m_done, 1)
                elif ev == "cbm":
                    dve.wait_ge(cb_ready, 2 * g + k + 1)
                    m, src = (4, PS[:, 7, :].rearrange("p (c l) -> p c l", c=4)) if k == 0 else (1, PS[:, 5, 0:P].unsqueeze(1))
                    for j, mask in enumerate((upper, lower)):
                        e = dve.tensor_tensor(cbm[:, j, 4 * k:4 * k + m, :], src, mask.unsqueeze(1).to_broadcast([P, m, P]), ALU.mult)
                    e.then_inc(cbm_done, 1)
                elif ev == "G":
                    dve.wait_ge(w_done, b0 + k + 1)
                    for h in range(4):
                        e = dve.scalar_tensor_tensor(out=wt[:, r, h, :], in0=cbm[:, 0, k, :], scalar=table(tab, DTO, 4)[:, k, h:h + 1],
                                                     in1=wt[:, r, h, :], op0=ALU.mult, op1=ALU.add)
                    e.then_inc(w_full, 1)
                    dve.wait_ge(w_full, b0 + k + 1)
                    dve.wait_ge(exp_done, b0 + k + 1)
                    if k >= 2:
                        dve.wait_ge(y_ready, b0 + k - 1)
                    dve.tensor_tensor(gm[:, r, :, :], ea[:, r, :, :], wt[:, r, :, :], ALU.mult).then_inc(g_done, 1)
                elif ev == "hup":
                    dve.wait_ge(st_ready, 3 * g + k + 1)
                    dve.wait_ge(hd_done, 3 * g + k + 1)
                    dve.tensor_tensor(hs[:, k + 1, :], PS[:, (4, 5, 4)[k], :], hd, ALU.add).then_inc(st_done, 1)
                elif ev == "yt":
                    dve.wait_ge(y_ready, b0 + k + 1)
                    if k >= 1:
                        dve.wait_ge(u_done, b0 + k)
                    dve.tensor_tensor(yo.rearrange("p (h q) -> p h q", h=8), PS[:, (6, 4)[k % 2], :].rearrange("p (h q) -> p h q", h=8),
                                      heads(EL, 8, k), ALU.mult).then_inc(t_done, 1)
                elif ev == "ya":
                    dve.wait_ge(u_done, b0 + k + 1)
                    dve.wait_ge(y_ready, b0 + k + 1)
                    if k >= 2:
                        dve.wait_ge(yn_done, b0 + k - 1)
                    dve.tensor_tensor(aa[:, r, :], PS[:, (7, 5)[k % 2], 0:256], uu[:, r, :], ALU.add).then_inc(a_step, 1)
                    dve.wait_ge(a_step, b0 + k + 1)
                    dve.tensor_tensor(aa[:, r, :], aa[:, r, :], sz[:, k, :], ALU.mult).then_inc(gz_done, 1)

        def ssd_pool(pool, B):
            g, n = B.g, B.n
            b0 = 5 * g
            tab = gt[:, B.par, :]
            ch = Chain(pool, pool_step, 8 * g)

            def xh(c):
                return xb[:, c, 0:256].rearrange("p (h q) -> p h q", h=4)

            def heads(col):
                return col.unsqueeze(2).to_broadcast([P, 4, 64])

            def hv(v):
                return v.rearrange("p (h q) -> p h q", h=4)
            if not B.ssd:
                return
            pool.wait_ge(grp_done, n)
            for ev, a in B.steps("Pool"):
                k = a[0]
                r = (B.par + k) % 2
                if ev == "xw":
                    pool.wait_ge(tok_done, b0 + (4 if k == 0 else 5))
                    for d in range(2):
                        c = (k, 3 - k)[d] if k < 3 else 4
                        e = pool.tensor_tensor(hv(xws[:, k, 256 * d:256 * d + 256]), xh(c), heads(table(tab, WDT + 4 * d, 4)[:, c, :]), ALU.mult)
                    e.then_inc(xw_done, 1)
                elif ev == "W":
                    pool.wait_ge(cbm_done, 2 * g + (1 if k < 4 else 2))
                    if k >= 2:
                        pool.wait_ge(g_done, b0 + k - 1)
                    pool.tensor_tensor(wt[:, r, :, :], cbm[:, 1, k, :].unsqueeze(1).to_broadcast([P, 4, P]),
                                       table(tab, DTO + 4, 4)[:, k, :].unsqueeze(2).to_broadcast([P, 4, P]), ALU.mult).then_inc(w_done, 1)
                elif ev == "hd":
                    pool.wait_ge(*((hs0_done, g + 1) if k == 0 else (st_done, 3 * g + k)))
                    for d in range(2):
                        c = (k, 3 - k)[d]
                        e = pool.tensor_tensor(hv(hd[:, 256 * d:256 * d + 256]), hv(hs[:, k, 256 * d:256 * d + 256]),
                                               heads(table(tab, DEC + 4 * d, 4)[:, c, :]), ALU.mult)
                    e.then_inc(hd_done, 1)
                elif ev == "u":
                    if k < 4:
                        pool.wait_ge(t_done, 4 * g + k + 1)
                    if k >= 2:
                        pool.wait_ge(gz_done, b0 + k - 1)
                    xd = pool.tensor_tensor(hv(uu[:, r, :]), xh(k), heads(gt[:, B.par, 200:204]), ALU.mult)
                    if k == 4:
                        xd.then_inc(u_done, 1)
                    else:
                        ch.tick(xd)
                        ch.tick(pool.tensor_tensor(yo[:, 0:256], yo[:, 0:256], yo[:, 256:512], ALU.add))
                        ch.sync()
                        pool.tensor_tensor(uu[:, r, :], uu[:, r, :], yo[:, 0:256], ALU.add).then_inc(u_done, 1)
                elif ev == "rs":
                    pool.wait_ge(sqy_done, b0 + k + 1)
                    pool.tensor_tensor(ry[:, r:r + 1], ssy[:, r:r + 1], eps_col[:, :], ALU.add).then_inc(msy_done, 1)
                    pool.wait_ge(msy_done, b0 + k + 1)
                    pool.tensor_tensor(ry[:, r:r + 1], ry[:, r:r + 1], half_neg[:, :], ALU.pow).then_inc(ry_done, 1)
                elif ev == "grp":
                    more = (not B.static) or g + 2 < G
                    if not B.static or g + 1 < G:
                        pool.wait_ge(yt_done, b0 + 1)
                        pool.wait_ge(conv_done, 4 * g + 4)
                        groups_copy(pool, g + 1, g + 2 if more else None, 1 - B.par, B.par).then_inc(grp_done, 1)

        def ssd_sp(sp, B):
            g, n = B.g, B.n
            b0 = 5 * g
            for ev, a in B.steps("SP"):
                k = a[0]
                if ev == "ey":
                    early_sp(sp, k)
                    continue
                if ev == "dt":
                    dt_sp(sp, k)
                    continue
                if ev == "ld":
                    u, slot = B.unit(k)
                    sp.wait_ge(lo_ready, u + 3)
                    if B.static and n + 1 >= G:
                        out_load(sp, 1, k)
                    else:
                        ssd_load(sp, 2 * B.i + (B.par + 2), k, (slot + 6) % RING)
                elif ev == "lfb":
                    if B.static and g == G - 1 and k >= 3:
                        continue
                    sp.wait_ge(m_done, b0 + k + 1)
                    gg, c = (g, k + 2) if k < 3 else (g + 1, k - 3)
                    lfb_load(sp, gg, c, B.count2(k)[1])
                elif ev == "nst":
                    sp.wait_ge(sc_done, g + 1)
                    for d in range(2):
                        sp.dma_start(state_view(new_state, d, g)[:, 0], nst.rearrange("p (j n) -> p j n", j=4)[:, 2 * d:2 * d + 2, :]).then_inc(small_stored, 16)
                    if not (B.static and g + 1 == G):
                        sp.wait_ge(h_T, g + 1)
                        for d in range(2):
                            sp.dma_start(h0r[:, 2 * d:2 * d + 2, :], state_view(A["state_ssm"], d, g + 1)[:, 0]).then_inc(h0_landed, 16)
                elif ev == "yst":
                    _, r = B.count2(k)
                    sp.wait_ge(yt_done, b0 + k + 2)
                    sp.dma_start(y_scr[:, bass.ds(2 * g, 2), k * P:(k + 1) * P], ysb[:, r, :, :]).then_inc(y_stored[r], 16)

        def all_groups(eng, part):
            part(eng, Body(-1, 1, ssd=False))
            with eng.Fori(0, 3) as i:
                part(eng, Body(i, 0))
                part(eng, Body(i, 1))
            part(eng, Body(3, 0))
            part(eng, Body(3, 1, proj=False))

        PAR_DMAS = 7

        def fc_col(u):
            if u < 16:
                i, k = u // 4, u % 4
                return (0, 0, D, D)[k] + P * (2 * i + k % 2)
            i, p = (u - 16) // 8, (u - 16) % 8
            return (3 * D, 4 * D, 2 * D, 5 * D)[p // 2] + P * (2 * i + p % 2)

        def out_load(sp, layer, v):
            u = (OUT0, OUT1)[layer] + v
            sp.dma_start(raw_w[:, u % 4, :].rearrange("p (k n) -> p k n", k=2),
                         wout_src[layer][:, 2 * (v % 8):2 * (v % 8) + 2, 512 * (v // 8):512 * (v // 8) + 512]).then_inc(landed[u % 4], 16)

        @block.sync
        def _(sp):
            sp.dma_start(cond[:, 0, :], A["c"].rearrange("a (p t) -> (a p) t", t=KT)).then_inc(cond_landed, 16)
            sp.dma_start(cond[:, 1, :], A["c_ctx"].rearrange("(p t) -> p t", t=KT)).then_inc(cond_landed, 16)
            sp.dma_start(cst[:, :], A["consts"]).then_inc(par_landed, 16)
            sp.dma_start(praw[0:96, 0, :], A["ssd_conv_w"].rearrange("a k (t n) -> (a k t) n", n=P)).then_inc(par_landed, 16)
            sp.dma_start(praw[96:128, 0, :], A["ssd_conv_b"].rearrange("a (t n) -> (a t) n", n=P)).then_inc(par_landed, 16)
            sp.dma_start(praw[0:16, 1, :], A["norm_g"].rearrange("a (t n) -> (a t) n", n=P)).then_inc(par_landed, 16)
            sp.dma_start(praw[16:40, 1, :], A["fc_conv_w"].rearrange("a k (t n) -> (a k t) n", n=P)).then_inc(par_landed, 16)
            sp.dma_start(praw[40:56, 1, :], A["ssd_norm_g"].rearrange("a (t n) -> (a t) n", n=P)).then_inc(par_landed, 16)
            sp.dma_start(praw[56:72, 1, :], A["b_mod"].rearrange("a (t n) -> (a t) n", n=P)[0:16, :]).then_inc(par_landed, 16)
            xs = A["x_sample"][0].rearrange("(t p) d -> p t d", p=P)
            for s in range(8):
                if s == 7:
                    sp.wait_ge(wm_used, 1)
                q, half = s // 2, s % 2
                sp.dma_start(wm[s], wm_src[0][:, 2 * q:2 * q + 2, 1024 * half:1024 * half + 1024]).then_inc(wm_landed[s], 16)
                if s < 2:
                    sp.dma_start(x[:, 2 * s:2 * s + 2, :], xs[:, 2 * s:2 * s + 2, :]).then_inc(x_landed[s], 16)
                if s == 2:
                    sp.dma_start(x[:, 4, :], A["x_prompt"][0]).then_inc(x_landed[2], 16)
            for u in range(4):
                if u % 2 == 0:
                    sp.wait_ge(wm_used, 2 + u // 2)
                sp.dma_start(raw_w[:, u, :], fc_src[:, :, fc_col(u):fc_col(u) + P]).then_inc(landed[u], 16)
            sp.wait_ge(mod_ready, 2)
            sp.dma_start(dft_g, A["dft_group"]).then_inc(dft_landed, 16)
            sp.dma_start(dft_l, A["dft_token"]).then_inc(dft_landed, 16)
            for i in (0, 1, 2):
                for k in range(4):
                    sp.wait_ge(lo_ready, 4 * i + k + 1)
                    sp.dma_start(raw_w[:, k, :], fc_src[:, :, fc_col(4 * i + 4 + k):fc_col(4 * i + 4 + k) + P]).then_inc(landed[k], 16)
            for k in range(4):
                sp.wait_ge(lo_ready, 12 + k + 1)
                sp.dma_start(raw_w[:, k, :], fc_src[:, :, fc_col(16 + k):fc_col(16 + k) + P]).then_inc(landed[k], 16)
            for i in range(4):
                for p in range(8):
                    u = C0 + 8 * i + p + 4
                    sp.wait_ge(lo_ready, u - 3)
                    if u < OUT0:
                        src = fc_src[:, :, fc_col(u):fc_col(u) + P]
                        sp.dma_start(raw_w[:, u % 4, :], src).then_inc(landed[u % 4], 16)
                    else:
                        out_load(sp, 0, u - OUT0)
            for v in range(4, 8):
                sp.wait_ge(lo_ready, OUT0 + v - 3)
                out_load(sp, 0, v)
            sp.wait_ge(row_stored, 64)
            for c in range(2):
                sp.dma_start(gate[:, c, :], mod_scr[0, c].partition_broadcast(P)).then_inc(gate_landed, 16)
            sp.dma_start(praw3[0:32, :], mod_scr[1:3].rearrange("k c (j n) -> (k c j) n", n=P)).then_inc(p3_landed, 16)
            sp.wait_ge(yb_done, 8)
            sp.dma_start(x[:, 0:4, :], xs).then_inc(x_back, 16)
            sp.dma_start(x[:, 4, :], A["x_prompt"][0]).then_inc(x_back, 16)
            for v in range(8, N_OUT):
                sp.wait_ge(lo_ready, OUT0 + v - 3)
                out_load(sp, 0, v)
            table_sp(sp)
            params_sp(sp)
            for k in range(4):
                sp.wait_ge(lo_ready, IN1 + k - 3)
                ssd_load(sp, 0, k, k)
            sp.wait_ge(x_updated, 10)
            sp.dma_start(x1_scr[:, 0:4 * D], x[:, 0:4, :].rearrange("p t d -> p (t d)")).then_inc(y_stored[0], 16)
            sp.dma_start(x1_scr[:, 4 * D:5 * D], x[:, 4, :]).then_inc(y_stored[1], 16)
            for k in range(4, 6):
                sp.wait_ge(lo_ready, IN1 + k - 3)
                ssd_load(sp, 0, k, k % RING)
            all_groups(sp, ssd_sp)
            sp.wait_ge(y_ready, 5 * G)
            sp.wait_ge(u_done, 5 * G)
            for r in range(2):
                sp.wait_ge(y_stored[r], 16 + 16 * (18 - r))
            sp.dma_start(yT[:, 12:14, :], y_scr[:, 12:14, :]).then_inc(y_back[6], 16)
            sp.wait_ge(yt_done, 1 + 5 * G)
            sp.wait_ge(y_stored[0], 16 + 16 * 20)
            sp.wait_ge(y_stored[1], 16 + 16 * 20)
            sp.dma_start(yT[:, 14:16, :], y_scr[:, 14:16, :]).then_inc(y_back[7], 16)
            for v in range(8, N_OUT):
                sp.wait_ge(lo_ready, OUT1 + v - 3)
                out_load(sp, 1, v)
                if v == 9:
                    sp.wait_ge(yl_done, 32 + 4)
                    sp.wait_ge(small_stored, 16 + 32 * G)
                    sp.dma_start(x[:, 0:4, :], x1_scr[:, 0:4 * D].rearrange("p (t d) -> p t d", d=D)).then_inc(x_back, 16)
                    sp.dma_start(x[:, 4, :], x1_scr[:, 4 * D:5 * D]).then_inc(x_back, 16)
                if v == 10:
                    for c in range(2):
                        sp.dma_start(gate[:, c, :], mod_scr[3, c].partition_broadcast(P)).then_inc(gate_landed, 16)
                    sp.dma_start(yT[:, 8:12, :], y_scr[:, 8:12, :]).then_inc(y_back[5], 16)
                if v == 12:
                    sp.dma_start(fin_g, A["final_norm_g"].partition_broadcast(P)).then_inc(fg_landed, 16)
            for t in range(NT):
                sp.wait_ge(fin_done, t + 1)
                dst = y_sample[0].rearrange("(t p) d -> p t d", p=P)[:, t, :] if t < 4 else y_prompt[0]
                sp.dma_start(dst, x[:, t, :]).then_inc(stored, 16)
            sp.wait_ge(stored, 16 * NT)

        @block.tensor
        def _(pe):
            start_pe(pe)
            start_pe_mod_T(pe)
            fourier_pe(pe, 0, True)
            with pe.Fori(1, 4) as i:
                fourier_pe(pe, i, False)
            conv_pe(pe, 0, True, False)
            with pe.Fori(1, 4) as i:
                conv_pe(pe, i, False, False)
            pe.wait_ge(act_freed, 31)
            pe.wait_ge(dve_freed, 16)
            out_pe(pe, 0)
            pe.wait_ge(p3_landed, 16)
            pe.wait_ge(out_evac, 4)
            pe.transpose(PS[:, 3, 0:32], praw3[0:32, :], ident[0:32, 0:32]).then_inc(mod_T, 1)
            norm_pe(pe, 1, xn1)
            all_groups(pe, ssd_pe)
            pe.wait_ge(yt_done, 1 + 5 * G)
            out_pe(pe, 1)

        @block.scalar
        def _(act):
            act.wait_ge(cond_landed, 32)
            act.activation(cond[:, :, :], cond[:, :, :], ACT.Silu).then_inc(cond_ready, 1)
            norm_act(act, 0, xn, xT0)
            for u in range(2):
                split_hi(act, u, u)
            act.wait_ge(wm_used, 8)
            act.activation(mod_sb[0:2, 0:1024], PSf[0:2, 0:1024], ACT.Copy).then_inc(mod_copied, 1)
            h_act(act, 0, xT0)
            for u in range(2, 4):
                split_hi(act, u, u)
            fourier_act(act, 0, True)
            with act.Fori(1, 4) as i:
                fourier_act(act, i, False)
            conv_act(act, 0, True, False)
            for q in range(2):
                y_split_act(act, 0, q)
            with act.Fori(1, 4) as i:
                conv_act(act, i, False, False)
            out_act(act, 0)
            norm_act(act, 1, xn1, xT1)
            h_act(act, 1, xT1)
            out_next_unit(act, split_hi, OUT0 + 15)
            dt_weights_act(act)
            all_groups(act, ssd_act)
            out_act(act, 1)
            for t in range(NT):
                act.wait_ge(x_updated, 15 + t + 1)
                if t >= 2:
                    act.wait_ge(sq_done, 10 + t - 1)
                act.activation(sq_junk[:, t % 2, :], x[:, t, :], ACT.Square, accum_out=ssq[:, 10 + t:11 + t]).then_inc(sq_done, 1)

        @block.vector
        def _(dve):
            dve.memset(ones[:, :], 1.0).then_inc(ones_ready, 1)
            dve.wait_ge(par_T, 1)
            dve.tensor_scalar(par1[:, :], PS[:, 6, 0:P], 0.5, None, ALU.mult).then_inc(par_ready, 1)
            dve.tensor_copy(par2[:, :], PS[:, 6, P:P + 72]).then_inc(par_ready, 1)
            norm_dve(dve, 0, xn)
            for u in range(2):
                split_lo(dve, u, u)
            dve.wait_ge(wm_used, 8)
            dve.tensor_copy(mod_sb[0:2, 1024:2048], PSf[0:2, 1024:2048]).then_inc(mod_copied, 1)
            dve.wait_ge(mod_T, 1)
            dve.wait_ge(par_ready, 2)
            for k in range(2):
                dve.tensor_tensor(ss_mod[:, k].rearrange("p c j -> p j c"), PS[:, 4, 16 * k:16 * k + 16].rearrange("p (j c) -> p j c", c=2),
                                  par2[:, 56 + 8 * k:64 + 8 * k].unsqueeze(2).to_broadcast([P, KT, 2]), ALU.add).then_inc(mod_ready, 1)
            dve.wait_ge(mod_ready, 2)
            dve.scalar_tensor_tensor(out=ss_mod[:, 1], in0=ss_mod[:, 1], scalar=1.0,
                                     in1=par2[:, 0:8].unsqueeze(1).to_broadcast([P, 2, KT]), op0=ALU.add, op1=ALU.mult).then_inc(mod_step, 1)
            dve.wait_ge(mod_step, 1)
            h_dve(dve, 0, xT0)
            for u in range(2, 4):
                split_lo(dve, u, u)
            fourier_dve(dve, 0, True)
            with dve.Fori(1, 4) as i:
                fourier_dve(dve, i, False)
            conv_dve(dve, 0, True, False)
            for q in range(2):
                y_split_dve(dve, 0, q)
            with dve.Fori(1, 3) as i:
                conv_dve(dve, i, False, False)
            conv_dve(dve, 3, False, True)
            out_dve(dve, 0)
            dve.wait_ge(mod_T, 2)
            dve.tensor_copy(ss_mod[:, 0], PS[:, 3, 0:16].rearrange("p (c j) -> p c j", c=2)).then_inc(mod_ready, 1)
            dve.scalar_tensor_tensor(out=ss_mod[:, 1], in0=PS[:, 3, 16:32].rearrange("p (c j) -> p c j", c=2), scalar=1.0,
                                     in1=par2[:, 8:16].unsqueeze(1).to_broadcast([P, 2, KT]), op0=ALU.add, op1=ALU.mult).then_inc(mod_ready, 1)
            conv_params_dve(dve)
            h_dve(dve, 1, xT1)
            out_next_unit(dve, split_lo, OUT0 + 15)
            dt_weights_dve(dve)
            all_groups(dve, ssd_dve)
            out_dve(dve, 1)
            dve.wait_ge(fg_landed, 16)
            for t in range(NT):
                dve.wait_ge(rstd_done, 10 + t + 1)
                dve.scalar_tensor_tensor(out=x[:, t, :], in0=x[:, t, :], scalar=rstd[:, 10 + t:11 + t], in1=fin_g,
                                         op0=ALU.mult, op1=ALU.mult).then_inc(fin_done, 1)

        @block.gpsimd
        def _(pool):
            pool.memset(half_neg[:, :], -0.5).then_inc(exponent_ready, 1)
            pool.memset(eps_col[:, :], EPS).then_inc(exponent_ready, 1)
            pool.wait_ge(exponent_ready, 2)
            norm_pool(pool, 0)
            h_pool(pool, 0, xT0)
            mod_pool(pool)
            norm_pool(pool, 1)
            h_pool(pool, 1, xT1)
            pool.wait_ge(cpg_ready, 1)
            groups_copy(pool, None, 0, 0, 0).then_inc(cp0_ready, 1)
            pool.wait_ge(tables_ready, 1)
            pool.wait_ge(tab_act, 6)
            groups_copy(pool, 0, None, 0, 0)
            groups_copy(pool, None, 1, 0, 1).then_inc(grp_done, 1)
            all_groups(pool, ssd_pool)
            norm_pool(pool, 2)


def constants():
    import numpy as np
    r = np.arange(P)
    tri = [np.eye(P), r[:, None] <= r[None, :], r[:, None] >= r[None, :]]
    consts = np.concatenate([np.asarray(t, np.float64) for t in tri], 1)
    k = np.arange(256)
    th = 2 * np.pi * ((k[:, None] * k[None, :]) % 256) / 256
    grp = np.concatenate([np.cos(th), np.sin(th)], 1) / 16
    grp = grp.reshape(2, P, 512).transpose(1, 0, 2)
    tok = []
    for f in (np.cos, lambda t: -np.sin(t)):
        for q in range(4):
            th = 2 * np.pi * ((r[:, None] * (4 * r[None, :] + q)) % LAT) / LAT
            tok.append(f(th) / np.sqrt(LAT))
    th = 2 * np.pi * ((r[:, None] * r[None, :]) % CTX) / CTX
    tok += [np.cos(th) / np.sqrt(CTX), -np.sin(th) / np.sqrt(CTX)]
    tok = np.stack(tok, 1)
    return {"consts": consts.astype(np.float32), "dft_group": grp.astype(np.float32), "dft_token": tok.astype(np.float32)}


_INS = ["x_prompt", "x_sample", "state_ssm", "c", "c_ctx", "w_mod", "b_mod", "norm_g", "fc_w_in", "fc_conv_w", "fc_w_out",
        "ssd_w_in", "ssd_conv_w", "ssd_conv_b", "ssd_dt_bias", "ssd_a_log", "ssd_d", "ssd_norm_g", "ssd_w_out", "final_norm_g"]
_OUTS = [(1, CTX, D), (1, LAT, D), (1, 1, 2, HEADS, 64, P)]


def kernel(**inputs):
    import numpy as _np
    import concourse.bacc as _bacc
    from concourse.bass_utils import run_bass_kernel_spmd as _run

    nc = _bacc.Bacc("TRN2", target_bir_lowering=False, num_devices=1)
    arrays, args = {}, {}
    given = {name: _np.ascontiguousarray(inputs[name]) for name in _INS}
    given.update(constants())
    for name, a in given.items():
        arrays[f"in_{name}_dram"] = a
        args[name] = nc.dram_tensor(f"in_{name}_dram", a.shape, mybir.dt.from_np(a.dtype), kind="ExternalInput").ap()
    outs = [nc.dram_tensor(f"out_{i}_dram", shape, F32, kind="ExternalOutput").ap() for i, shape in enumerate(_OUTS)]
    build_step(nc, args, outs)
    r = _run(nc, [arrays], core_ids=[0])
    return tuple(r.results[0][f"out_{i}_dram"] for i in range(len(_OUTS)))
```
